# Optimizing a Trainium2 kernel written in Bass

```python
import math
import jax, jax.numpy as jnp
from jax import lax
import numpy as np

D_MODEL = 1024
BATCH = 1
SEQ = 512
DEPTH = 2

D_FF = 2816
EPS = 1e-6
A_HEADS = 8
A_KV_HEADS = 2
A_HEAD_DIM = 64
WINDOW = 128
B_HEADS = 4
B_KEY_DIM = 128
B_VAL_DIM = 128
B_CHUNK = 32
S5_GROUP = 16
S5_GROUPS = D_MODEL // S5_GROUP
S5_STATE = 64
S5_DT_MIN = 1e-3
S5_DT_MAX = 1e-1

A_Q_W = A_HEADS * A_HEAD_DIM
A_KV_W = A_KV_HEADS * A_HEAD_DIM
B_W = B_HEADS * B_KEY_DIM
MIX_SPLITS = (A_Q_W, A_Q_W + A_KV_W, A_Q_W + 2 * A_KV_W, A_Q_W + 2 * A_KV_W + B_W, A_Q_W + 2 * A_KV_W + 2 * B_W, A_Q_W + 2 * A_KV_W + 3 * B_W)
MIX_IN = A_Q_W + 2 * A_KV_W + 4 * B_W
MIX_OUT = A_Q_W + B_HEADS * B_VAL_DIM
N_EVEN = (DEPTH + 1) // 2
N_ODD = DEPTH // 2

kernel_name = 'hybrid_swa_hgrn2_s5_macaron'

def _rmsnorm(x, g):
    x32 = x.astype(jnp.float32)
    y = x32 * lax.rsqrt(jnp.mean(x32 * x32, axis=-1, keepdims=True) + EPS)
    return (y * g.astype(jnp.float32)).astype(x.dtype)

def _swiglu(h, w_in, w_out):
    gate, up = jnp.split(h @ w_in, 2, axis=-1)
    return (jax.nn.silu(gate) * up) @ w_out

def _alibi_slopes():
    s = 2.0 ** (-8.0 * np.arange(1, A_HEADS + 1) / A_HEADS)
    return jnp.asarray(s, dtype=jnp.float32).reshape(A_KV_HEADS, A_HEADS // A_KV_HEADS)

def _sliding_window_gqa(q, k, v, sinks):
    b, l, _ = q.shape
    nb = l // WINDOW
    grp = A_HEADS // A_KV_HEADS
    qb = q.reshape(b, nb, WINDOW, A_KV_HEADS, grp, A_HEAD_DIM)
    kb = k.reshape(b, nb, WINDOW, A_KV_HEADS, A_HEAD_DIM)
    vb = v.reshape(b, nb, WINDOW, A_KV_HEADS, A_HEAD_DIM)
    pad = ((0, 0), (1, 0), (0, 0), (0, 0), (0, 0))
    kw = jnp.concatenate([jnp.pad(kb[:, :-1], pad), kb], axis=2)
    vw = jnp.concatenate([jnp.pad(vb[:, :-1], pad), vb], axis=2)
    s = jnp.einsum('bnqhgd,bnkhd->bnhgqk', qb, kw, preferred_element_type=jnp.float32) * (A_HEAD_DIM ** -0.5)
    qpos = jnp.arange(WINDOW) + WINDOW
    kpos = jnp.arange(2 * WINDOW)
    dist_i = qpos[:, None] - kpos[None, :]
    in_band = (dist_i >= 0) & (dist_i < WINDOW)
    has_prev = (jnp.arange(nb)[:, None, None] > 0) | (kpos[None, None, :] >= WINDOW)
    mask = in_band[None] & has_prev
    dist = dist_i.astype(jnp.float32)
    s = s - _alibi_slopes()[:, :, None, None] * dist
    s = jnp.where(mask[None, :, None, None], s, -jnp.inf)
    sink = sinks.astype(jnp.float32).reshape(A_KV_HEADS, grp)[None, None, :, :, None, None]
    m = jnp.maximum(jnp.max(s, axis=-1, keepdims=True), sink)
    p = jnp.exp(s - m)
    denom = jnp.sum(p, axis=-1, keepdims=True) + jnp.exp(sink - m)
    o = jnp.einsum('bnhgqk,bnkhd->bnhgqd', p / denom, vw.astype(jnp.float32))
    o = o.transpose(0, 1, 4, 2, 3, 5).reshape(b, l, A_Q_W)
    return o.astype(q.dtype)

def _hgrn2(q, f_logit, i_val, g, lb):
    b, l, _ = q.shape
    nc = l // B_CHUNK

    def heads(t):
        return t.astype(jnp.float32).reshape(b, nc, B_CHUNK, B_HEADS, -1).transpose(0, 3, 1, 2, 4)

    lbh = lb.astype(jnp.float32).reshape(B_HEADS, 1, 1, B_KEY_DIM)
    f = lbh + (1.0 - lbh) * jax.nn.sigmoid(heads(f_logit))
    k = 1.0 - f
    qh = jax.nn.silu(heads(q))
    vh = heads(i_val)
    cum = jnp.cumsum(jnp.log(f), axis=3)
    q_dec = qh * jnp.exp(cum)
    k_inv = k * jnp.exp(-cum)
    k_end = k * jnp.exp(cum[:, :, :, -1:] - cum)
    causal = jnp.tril(jnp.ones((B_CHUNK, B_CHUNK), dtype=bool))
    scores = jnp.where(causal, jnp.einsum('bhnqd,bhnkd->bhnqk', q_dec, k_inv), 0.0)
    o = jnp.einsum('bhnqk,bhnkv->bhnqv', scores, vh)
    chunk_decay = jnp.exp(cum[:, :, :, -1])
    chunk_kv = jnp.einsum('bhnkd,bhnkv->bhndv', k_end, vh)

    def step(state, inp):
        dec, kv = inp
        return dec[..., None] * state + kv, state

    s0 = jnp.zeros((b, B_HEADS, B_KEY_DIM, B_VAL_DIM), jnp.float32)
    _, s_start = lax.scan(step, s0, (jnp.moveaxis(chunk_decay, 2, 0), jnp.moveaxis(chunk_kv, 2, 0)))
    o = o + jnp.einsum('bhnqd,nbhdv->bhnqv', q_dec, s_start)
    o = o.transpose(0, 2, 3, 1, 4).reshape(b, l, B_HEADS, B_VAL_DIM)
    o = o * lax.rsqrt(jnp.mean(o * o, axis=-1, keepdims=True) + EPS)
    gate = jax.nn.silu(g.astype(jnp.float32)).reshape(b, l, B_HEADS, B_VAL_DIM)
    return (o * gate).reshape(b, l, B_HEADS * B_VAL_DIM).astype(q.dtype)

def _complex_linear_combine(e1, e2):
    ar1, ai1, br1, bi1 = e1
    ar2, ai2, br2, bi2 = e2
    ar = ar2 * ar1 - ai2 * ai1
    ai = ar2 * ai1 + ai2 * ar1
    br = ar2 * br1 - ai2 * bi1 + br2
    bi = ar2 * bi1 + ai2 * br1 + bi2
    return (ar, ai, br, bi)

def _s5(u, a_re, a_im, log_step, b_re, b_im, c_re, c_im, d_skip):
    b, l, _ = u.shape
    u32 = u.astype(jnp.float32)
    lam_r = a_re.astype(jnp.float32)
    lam_i = a_im.astype(jnp.float32)
    step = jnp.exp(log_step.astype(jnp.float32))[:, None]
    mag = jnp.exp(step * lam_r)
    ab_r = mag * jnp.cos(step * lam_i)
    ab_i = mag * jnp.sin(step * lam_i)
    den = lam_r * lam_r + lam_i * lam_i
    coef_r = ((ab_r - 1.0) * lam_r + ab_i * lam_i) / den
    coef_i = (ab_i * lam_r - (ab_r - 1.0) * lam_i) / den
    br = b_re.astype(jnp.float32)
    bi = b_im.astype(jnp.float32)
    bb_r = coef_r[..., None] * br - coef_i[..., None] * bi
    bb_i = coef_r[..., None] * bi + coef_i[..., None] * br
    ug = u32.reshape(b, l, S5_GROUPS, S5_GROUP)
    bu_r = jnp.einsum('blgc,gpc->blgp', ug, bb_r)
    bu_i = jnp.einsum('blgc,gpc->blgp', ug, bb_i)
    a_shape = (1, l, S5_GROUPS, S5_STATE)
    ar = jnp.broadcast_to(ab_r[None, None], a_shape)
    ai = jnp.broadcast_to(ab_i[None, None], a_shape)
    _, _, xr, xi = lax.associative_scan(_complex_linear_combine, (ar, ai, bu_r, bu_i), axis=1)
    y = jnp.einsum('blgp,gcp->blgc', xr, c_re.astype(jnp.float32)) - jnp.einsum('blgp,gcp->blgc', xi, c_im.astype(jnp.float32))
    return y.reshape(b, l, D_MODEL) + d_skip.astype(jnp.float32) * u32

def setup_inputs(seed: int = 0) -> dict:
    key = jax.random.key(seed)
    ks = jax.random.split(key, 18)
    f32 = jnp.float32

    def nrm(k, shape, scale):
        return jax.random.normal(k, shape, f32) * scale

    n = jnp.arange(S5_STATE, dtype=f32)
    return {
        'x': nrm(ks[0], (BATCH, SEQ, D_MODEL), 1.0),
        'norm_g': 1.0 + nrm(ks[1], (DEPTH, 3, D_MODEL), 0.02),
        'ffn_w_in': nrm(ks[2], (DEPTH, 2, D_MODEL, 2 * D_FF), D_MODEL ** -0.5),
        'ffn_w_out': nrm(ks[3], (DEPTH, 2, D_FF, D_MODEL), D_FF ** -0.5),
        'mix_w_in': nrm(ks[4], (N_EVEN, D_MODEL, MIX_IN), D_MODEL ** -0.5),
        'attn_sinks': nrm(ks[5], (N_EVEN, A_HEADS), 0.5),
        'hgrn_lb': nrm(ks[6], (N_EVEN, B_HEADS * B_KEY_DIM), 0.1),
        'mix_w_out': nrm(ks[7], (N_EVEN, MIX_OUT, D_MODEL), MIX_OUT ** -0.5),
        's5_a_re': -0.5 + nrm(ks[8], (N_ODD, S5_GROUPS, S5_STATE), 0.01),
        's5_a_im': math.pi * n + nrm(ks[9], (N_ODD, S5_GROUPS, S5_STATE), 0.01),
        's5_log_step': jax.random.uniform(ks[10], (N_ODD, S5_GROUPS), f32, math.log(S5_DT_MIN), math.log(S5_DT_MAX)),
        's5_b_re': nrm(ks[11], (N_ODD, S5_GROUPS, S5_STATE, S5_GROUP), (2 * S5_GROUP) ** -0.5),
        's5_b_im': nrm(ks[12], (N_ODD, S5_GROUPS, S5_STATE, S5_GROUP), (2 * S5_GROUP) ** -0.5),
        's5_c_re': nrm(ks[13], (N_ODD, S5_GROUPS, S5_GROUP, S5_STATE), S5_STATE ** -0.5),
        's5_c_im': nrm(ks[14], (N_ODD, S5_GROUPS, S5_GROUP, S5_STATE), S5_STATE ** -0.5),
        's5_d': nrm(ks[15], (N_ODD, D_MODEL), 1.0),
        's5_w_glu': nrm(ks[16], (N_ODD, D_MODEL, 2 * D_MODEL), D_MODEL ** -0.5),
        'final_g': 1.0 + nrm(ks[17], (D_MODEL,), 0.02),
    }

def reference(x, norm_g, ffn_w_in, ffn_w_out, mix_w_in, attn_sinks, hgrn_lb, mix_w_out, s5_a_re, s5_a_im, s5_log_step, s5_b_re, s5_b_im, s5_c_re, s5_c_im, s5_d, s5_w_glu, final_g):
    lb_p = jax.nn.softmax(hgrn_lb.astype(jnp.float32), axis=0)
    lb_all = jnp.cumsum(lb_p, axis=0) - lb_p[0]
    for layer in range(DEPTH):
        x = x + 0.5 * _swiglu(_rmsnorm(x, norm_g[layer, 0]), ffn_w_in[layer, 0], ffn_w_out[layer, 0])
        h = _rmsnorm(x, norm_g[layer, 1])
        if layer % 2 == 0:
            e = layer // 2
            q_a, k_a, v_a, q_b, f_b, i_b, g_b = jnp.split(h @ mix_w_in[e], MIX_SPLITS, axis=-1)
            attn = _sliding_window_gqa(q_a, k_a, v_a, attn_sinks[e])
            rec = _hgrn2(q_b, f_b, i_b, g_b, lb_all[e])
            mix = jnp.concatenate([attn, rec], axis=-1) @ mix_w_out[e]
        else:
            o = layer // 2
            y = _s5(h, s5_a_re[o], s5_a_im[o], s5_log_step[o], s5_b_re[o], s5_b_im[o], s5_c_re[o], s5_c_im[o], s5_d[o])
            y = jax.nn.gelu(y).astype(x.dtype)
            val, gate = jnp.split(y @ s5_w_glu[o], 2, axis=-1)
            mix = val * jax.nn.sigmoid(gate)
        x = x + mix.astype(x.dtype)
        x = x + 0.5 * _swiglu(_rmsnorm(x, norm_g[layer, 2]), ffn_w_in[layer, 1], ffn_w_out[layer, 1])
    return _rmsnorm(x, final_g)


_drawn_inputs = setup_inputs


def setup_inputs(seed=0):
    import zlib

    import numpy as np

    out = dict(_drawn_inputs(seed))
    spreads = {}
    factors = {'attn_sinks': 7.79,
     's5_a_re': 8.0,
     's5_b_re': 3.256,
     's5_b_im': 3.243,
     's5_c_re': 3.238,
     's5_c_im': 3.3,
     'final_g': 2.87}
    for name, (base, spread) in spreads.items():
        noise = np.random.default_rng([zlib.crc32(name.encode()), seed]).standard_normal(out[name].shape)
        drawn = base * np.exp(spread * noise) if base else spread * noise
        out[name] = __import__('jax').numpy.asarray(drawn.astype(out[name].dtype))
    for name, factor in factors.items():
        out[name] = (out[name] * factor).astype(out[name].dtype)
    return out
```

```python
from contextlib import ExitStack

import numpy as np

import concourse.bass as bass
from concourse import mybir

F32 = mybir.dt.float32
F32R = mybir.dt.float32r
I32 = mybir.dt.int32
ACT = mybir.ActivationFunctionType
ALU = mybir.AluOpType
AX = mybir.AxisListType

P = 128
EPS = 1e-6
RING = 4
LEAD = 2
CH = 32
MASKED = 1e30
POOL_CONSTS = 9
POOL_COUNT = POOL_CONSTS + 2
POOL_ALL = POOL_COUNT + 2
U_DMAS = 8
MK_STORES = 19
TWO_PI = 6.283185307179586
TWO_PI_PARTS = (6.28125, 0.001934051513671875, 1.2556659146e-06)
ROUND = 12582912.0
PI_BELOW = 3.1415925


def trunk(nc, x_t, norm_g, ffn_w_in, ffn_w_out, mix_w_in, attn_sinks, hgrn_lb, mix_w_out, s5_a_re, s5_a_im,
          s5_log_step, s5_b_re, s5_b_im, s5_bt_re, s5_bt_im, s5_c_re, s5_c_im, s5_d, s5_w_glu, final_g, out_t):
    D, T = x_t.shape
    F = ffn_w_out.shape[2]
    KD = D // P
    NT = T // P
    HALVES = 2
    KF = F // P // HALVES
    SLAB_IN, SLAB_OUT = KD * P, KF * P
    SLAB = max(SLAB_IN, SLAB_OUT)
    HEADS = attn_sinks.shape[1]
    AD = 64
    AT = HEADS * AD // P
    BH = hgrn_lb.shape[1]
    KV_W = 2 * AD
    COL_K, COL_V = HEADS * AD, HEADS * AD + KV_W
    COL_BQ = HEADS * AD + 2 * KV_W
    COL_BF, COL_BI, COL_BG = COL_BQ + BH * P, COL_BQ + 2 * BH * P, COL_BQ + 3 * BH * P
    NCH = T // CH
    CPT = P // CH
    NORMS = [0, 2, 3, 5]
    NORM_MIX, NORM_S5, NORM_FIN = 1, 4, 6
    SPLIT_NORMS = [0, 1, 2, 3, 5]

    PAIRS = s5_a_re.shape[1]
    NS = P // 2
    GC = s5_bt_re.shape[0]
    G = 2 * PAIRS
    L = P // GC
    NC = T // L
    PPB = 512 // NC

    KIB = 1024
    o_x = 16640
    o_xg = o_x + KD * T * 4
    o_h = o_xg + 2 * KD * T * 4
    o_ring = o_h + 2 * KF * T * 4
    o_norm = o_ring + 3 * RING * SLAB * 4
    o_const = o_norm + 4 * T * 4
    o_tmp = o_const + 7808
    o_free = o_tmp + 4 * T * 4
    o_end = 229368

    with ExitStack() as ctx:
        def at(name, shape, offset, dt=F32):
            n = 4
            for d in shape[1:]:
                n *= d
            assert offset + n <= o_end, (name, offset + n)
            return nc.alloc_sbuf_tensor_at(name, shape, dt, offset=offset), offset + -(-n // 32) * 32

        def sem(name):
            return ctx.enter_context(nc.semaphore(name))

        x, _ = at("x", [P, KD, T], o_x)
        xg_hi, o = at("xg_hi", [P, KD, T], o_xg, F32R)
        xg_lo, _ = at("xg_lo", [P, KD, T], o, F32R)
        h_hi, o = at("h_hi", [P, KF, T], o_h, F32R)
        h_lo, _ = at("h_lo", [P, KF, T], o, F32R)
        raw, o = at("raw", [P, RING, SLAB], o_ring)
        w_hi, o = at("w_hi", [P, RING, SLAB], o, F32R)
        w_lo, _ = at("w_lo", [P, RING, SLAB], o, F32R)
        gate_r, o = at("gate_r", [P, T], o_tmp)
        silu_g, o = at("silu_g", [P, T], o)
        up_s, o = at("up_s", [P, T], o)
        hid, _ = at("hid", [P, T], o)
        sq, o = at("sq", [P, T], o_norm)
        ssq, o = at("ssq", [P, T], o)
        rms, o = at("rms", [P, T], o)
        rinv, _ = at("rinv", [P, T], o)
        ones, o = at("ones", [P, P], o_const)
        ident, o = at("ident", [P, P], o)
        causal, o = at("causal", [P, P], o)
        dist, o = at("dist", [P, 2 * P], o)
        dist_i, _ = at("dist_i", [P, 2 * P], o_tmp, I32)
        g_all, o = at("g_all", [P, 7, KD], o)
        sink, o = at("sink", [P, HEADS], o)
        sink_neg, o = at("sink_neg", [P, HEADS], o)
        lb_in, o = at("lb_in", [P, BH], o)
        lb, o = at("lb", [P, BH], o)
        lb_c, o = at("lb_c", [P, BH], o)
        r_col, o = at("r_col", [P, NT], o)
        max_neg, o = at("max_neg", [P, 2, 2], o)
        sink_d, o = at("sink_d", [P, 2, 2], o)
        sink_e, o = at("sink_e", [P, 2, 2], o)
        rowsum, o = at("rowsum", [P, 2, 2], o)
        den, o = at("den", [P, 2, 2], o)
        rden, o = at("rden", [P, 2, 2], o)
        decay, o = at("decay", [P, BH, NCH], o)
        pow_r, o = at("pow_r", [P, L + 1, PAIRS], o)
        pow_i, o = at("pow_i", [P, L + 1, PAIRS], o)
        leap_r, o = at("leap_r", [P, 2, PAIRS], o)
        leap_i, o = at("leap_i", [P, 2, PAIRS], o)
        coef, o = at("coef", [P, 2, PAIRS], o)
        d_col, o = at("d_col", [P, KD], o)
        diag, o = at("diag", [P, GC], o)
        r_sel, o = at("r_sel", [1, (2 * L - 1) * GC], o)
        r_row, o = at("r_row", [P, NC], o)
        assert o <= o_tmp, o - o_const
        b_k, o = at("b_k", [P, BH, T], o_h)
        b_cum, o = at("b_cum", [P, BH, T], o)
        b_q, o = at("b_q", [P, BH, T], o)
        b_e, o = at("b_e", [P, BH, T], o)
        b_g, o = at("b_g", [P, BH, T], o)
        states, _ = at("states", [P, NCH, P], o_h + BH * T * 4)
        a_q, _ = at("a_q", [P, AT, T], o_h + 3 * BH * T * 4)
        b_kinv, o = at("b_kinv", [P, BH, T], o_free)
        b_o, _ = at("b_o", [P, BH, T], o_free)
        b_v, o = at("b_v", [P, NT, BH * P], o)
        a_k, _ = at("a_k", [P, T], o_norm)
        a_v, o = at("a_v", [P, NT, KV_W], o)
        k_end, o = at("k_end", [P, 2, NT, P], o)
        scores, o = at("scores", [P, 2, NT, P], o)
        prob, _ = at("prob", [P, 2, 2, 2 * P], o_tmp)
        prob_t, _ = at("prob_t", [P, 2, 2, 2, P], o_tmp + 2 * T * 4)
        b_tmp, _ = at("b_tmp", [P, 2, T], o_tmp)
        att_h, _ = at("att_h", [P, AT, T], o_h, F32R)
        rec_h, _ = at("rec_h", [P, BH, T], o_h + BH * T * 4, F32R)
        rec_l, _ = at("rec_l", [P, BH, T], o_h + 2 * BH * T * 4, F32R)
        att_l, _ = at("att_l", [P, AT, T], o_free + BH * T * 4, F32R)
        squares, _ = at("squares", [P, BH, T], o_tmp)
        rec, _ = at("rec", [P, 2, T], o_tmp + 2 * T * 4)

        o = o_h
        names = ["lam_r", "lam_i", "log_dt", "den_l", "num_a", "num_b", "abr1"]
        tiny = {}
        for name in names:
            tiny[name], o = at("s5_" + name, [P, PAIRS], o)
        for name in ["angle", "turns", "angle_c", "fold", "mag"]:
            tiny[name], o = at("s5_" + name, [P, L + 1, PAIRS], o)
        k_count, o = at("k_count", [P, L + 1], o)
        for name in ["w_r", "w_i", "w_t"]:
            tiny[name], o = at("s5_" + name, [P, L, PAIRS], o)
        w_rows, _ = at("w_rows", [P, 4, P], o)
        GQ = G // 4
        o = o_free
        mk = {}
        for name in ["wr", "wi", "br", "bi", "t1", "t2"]:
            mk[name], o = at("mk_" + name, [P, GQ * NS], o)
        PQ = PAIRS // 4
        o = o_free
        mk_c, o = at("mk_c", [P, 2, PQ, (L + 1) * GC], o)
        for name in ["cr", "ci", "ncr"]:
            mk[name], o = at("mk_" + name, [P, PAIRS, GC], o)
        for name in ["u1", "u2"]:
            mk[name], o = at("mk_" + name, [P, PQ, (L + 1) * GC], o)
        mk_bb, _ = at("mk_bb", [P, PAIRS, 2, 2 * GC], o_free + 12 * KIB)
        mk["sr"], o = at("mk_sr", [P, PAIRS, GC], o_free)
        mk["si"], o = at("mk_si", [P, PAIRS, GC], o)
        mk["s1"], o = at("mk_s1", [P, PAIRS, GC], o)
        mk["s2"], o = at("mk_s2", [P, PAIRS, GC], o)
        mk_zero, _ = at("mk_zero", [P, KD, (L - 1) * GC], o_free + 20 * KIB)
        s5_c, o = at("s5_c", [P, 2, PAIRS, (L + 1) * GC], o_h)
        s5_bb, o = at("s5_bb", [P, PAIRS, 2, 2 * GC], o)
        assert o <= o_ring
        s5_bm, _ = at("s5_bm", [P, 2, G, NS], o_tmp)
        s5_t, _ = at("s5_t", [P, G, P], o_tmp)
        s5_xg, _ = at("s5_xg", [P, KD, T], o_xg)
        s5_y2, _ = at("s5_y2", [P, G, NC], o_xg)
        s5_y, _ = at("s5_y", [P, KD, T], o_xg + KD * T * 4)
        y_hi, o = at("y_hi", [P, KD, T], o_tmp, F32R)
        y_lo, _ = at("y_lo", [P, KD, T], o, F32R)
        sig, o = at("sig", [P, 2, T], o_h)
        glu, _ = at("glu", [P, 2, T], o)
        s5_u, o = at("s5_u", [P, G, NC], o_ring + RING * SLAB * 4)
        s5_k, o = at("s5_k", [P, KD, L * GC], o)
        assert o <= o_ring + 2 * RING * SLAB * 4
        s5_x, o = at("s5_x", [P, 2, PAIRS, NC], o_ring + 2 * RING * SLAB * 4)
        scan_a, o = at("scan_a", [P, 2, 2, PAIRS], o)
        scan_b, o = at("scan_b", [P, 2, 2, PAIRS], o)
        assert o <= o_norm

        def dram(name, *shape):
            return nc.dram_tensor(name, shape, F32).ap()

        dram_w = dram("dram_w", 2, L, G, NS)
        dram_bm = dram("dram_bm", P, 2, G, NS)
        dram_c = dram("dram_c", P, 2, PAIRS, (L + 1) * GC)
        dram_bb = dram("dram_bb", P, PAIRS * 2 * 2 * GC)
        dram_k = dram("dram_k", D, (2 * L - 1) * GC)
        dram_u = dram("dram_u", D, T)
        dram_y = dram("dram_y", D, T)

        bank = [ctx.enter_context(nc.psum_tensor(f"bank{i}", [P, 512], F32)) for i in range(8)]
        gate_ps, up_ps, out_ps, norm_ps = bank[0:2], bank[2:4], bank[4:6], bank[6]

        const_loaded = sem("const_loaded")
        small_loaded = sem("small_loaded")
        x_loaded = sem("x_loaded")
        ones_set = sem("ones_set")
        pool_const = sem("pool_const")
        slab_loaded = [sem(f"slab_loaded{i}") for i in range(RING)]
        slab_hi = sem("slab_hi")
        slab_lo = sem("slab_lo")
        slab_used = sem("slab_used")
        gate_scaled = sem("gate_scaled")
        silu_ready = sem("silu_ready")
        banks_free = sem("banks_free")
        hid_ready = sem("hid_ready")
        hid_hi = sem("hid_hi")
        hid_lo = sem("hid_lo")
        x_half = sem("x_half")
        x_ready = sem("x_ready")
        xg_hi_ready = sem("xg_hi_ready")
        xg_lo_ready = sem("xg_lo_ready")
        sq_ready = sem("sq_ready")
        ssq_ready = sem("ssq_ready")
        norm_sum = sem("norm_sum")
        mean_ready = sem("mean_ready")
        rms_ready = sem("rms_ready")
        rinv_ready = sem("rinv_ready")
        stored = sem("stored")
        fin_ready = sem("fin_ready")
        dve_step = sem("dve_step")
        act_step = sem("act_step")
        lb_exp = sem("lb_exp")
        col_ready = sem("col_ready")
        col_taken = sem("col_taken")
        proj_scaled = sem("proj_scaled")
        proj_free = sem("proj_free")
        nat_taken = sem("nat_taken")
        sig_ready = sem("sig_ready")
        sig_used = sem("sig_used")
        f_one = sem("f_one")
        f_ready = sem("f_ready")
        logf_ready = sem("logf_ready")
        cum_ready = sem("cum_ready")
        exp_ready = sem("exp_ready")
        exp_used = sem("exp_used")
        b_ready = sem("b_ready")
        sc_ready = sem("sc_ready")
        sc_masked = sem("sc_masked")
        kt_ready = sem("kt_ready")
        kt_taken = sem("kt_taken")
        kv_ready = sem("kv_ready")
        state_ready = sem("state_ready")
        inter_done = sem("inter_done")
        o_taken = sem("o_taken")
        o_sq = sem("o_sq")
        o_sum = sem("o_sum")
        o_mean = sem("o_mean")
        o_rms = sem("o_rms")
        o_rinv = sem("o_rinv")
        o_bcast = sem("o_bcast")
        rec_ready = sem("rec_ready")
        mix_hi = sem("mix_hi")
        mix_lo = sem("mix_lo")
        s_ready = sem("s_ready")
        s_taken = sem("s_taken")
        m_ready = sem("m_ready")
        p_exp = sem("p_exp")
        p_ready = sem("p_ready")
        pt_ready = sem("pt_ready")
        pt_taken = sem("pt_taken")
        pv_done = sem("pv_done")
        att_hi = sem("att_hi")
        att_lo = sem("att_lo")

        s5_loaded = sem("s5_loaded")
        s5_dt = sem("s5_dt")
        s5_angles = sem("s5_angles")
        s5_trig = sem("s5_trig")
        s5_w_ready = sem("s5_w_ready")
        s5_w_turned = sem("s5_w_turned")
        s5_w_rows = sem("s5_w_rows")
        s5_w_stored = sem("s5_w_stored")
        mk_loaded = sem("mk_loaded")
        mk_stored = sem("mk_stored")
        pool_step = sem("pool_step")
        mats_loaded = sem("mats_loaded")
        k_summed = sem("k_summed")
        k_ready = sem("k_ready")
        k_diag = sem("k_diag")
        k_stored = sem("k_stored")
        bm_loaded = sem("bm_loaded")
        t_loaded = sem("t_loaded")
        u_tile = sem("u_tile")
        u_stored = sem("u_stored")
        u_loaded = sem("u_loaded")
        row_ready = sem("row_ready")
        row_taken = sem("row_taken")
        u_ready = sem("u_ready")
        st_ready = sem("st_ready")
        st_taken_a = sem("st_taken_a")
        st_taken_d = sem("st_taken_d")
        scanned = sem("scanned")
        y_ready = sem("y_ready")
        y_taken_a = sem("y_taken_a")
        y_taken_d = sem("y_taken_d")
        y_stored = sem("y_stored")
        y_loaded = [sem(f"y_loaded{q}") for q in range(PAIRS // PPB)]
        gelu_ready = sem("gelu_ready")
        y_hi_ready = sem("y_hi_ready")
        y_lo_ready = sem("y_lo_ready")
        glu_sig = sem("glu_sig")
        glu_mul = sem("glu_mul")

        phases = []
        sizes = []

        def phase(kind, f=0, half=0, count=0, size=0):
            phases.append((kind, f, half, len(sizes)))
            sizes.extend([size] * count)

        def swiglu(f):
            for half in range(HALVES):
                phase("in", f, half, 2 * KF, SLAB_IN)
                phase("out", f, half, KD, SLAB_OUT)

        MIX_COLS = [COL_BF + i * P for i in range(BH)] + [COL_BQ + i * P for i in range(BH)] \
            + [COL_BG + i * P for i in range(BH)] + [COL_BI + i * P for i in range(BH)]
        swiglu(0)
        phase("mixer0", count=len(MIX_COLS) + AT + 2, size=SLAB_IN)
        phase("mixer0_out", count=KD, size=KD * P)
        swiglu(1)
        swiglu(2)
        phase("mixer1", count=2 * KD, size=SLAB_IN)
        swiglu(3)
        total = len(sizes)

        w_in = [ffn_w_in[f // 2, f % 2].rearrange("(k p) c -> p k c", p=P) for f in range(4)]
        w_out = [ffn_w_out[f // 2, f % 2].rearrange("(k p) c -> p k c", p=P) for f in range(4)]
        w_glu = s5_w_glu.rearrange("(k p) c -> p k c", p=P)
        w_mix = mix_w_in.rearrange("(k p) c -> p k c", p=P)
        w_mix_out = mix_w_out.rearrange("(k p) c -> p k c", p=P)

        late = [s0 + i for kind, _, _, s0 in phases if kind == "mixer1" for i in range(LEAD)]

        def slot(s):
            return s % RING

        def arrived(s, per=1):
            return 16 * (s // RING + 1)

        def split(s):
            return RING + s + 1

        def used(s):
            return RING + s + 1

        def xg_count(n, k):
            return SPLIT_NORMS.index(n) * KD + k + 1

        UNITS = [(n, tp, g) for n in range(NT) for tp in range(AT // 2) for g in range(2)]
        SLOPES = [2.0 ** (-8.0 * (h + 1) / HEADS) for h in range(HEADS)]

        def taken(v):
            return sum(2 if n else 1 for n, _, _ in UNITS[:v + 1])

        block = ctx.enter_context(nc.Block())

        @block.sync
        def _(sp):
            def load(s, src, n, turn=0):
                sp.wait_ge(slab_lo, s + 1 + turn)
                sp.dma_start(raw[:, slot(s), 0:n * P].rearrange("p (k c) -> p k c", c=P), src)\
                  .then_inc(slab_loaded[slot(s)], 16)

            for k in range(KD):
                sp.dma_start(x[:, k, :], x_t[k * P:(k + 1) * P, :]).then_inc(x_loaded, 16)
            for kind, f, half, s0 in phases:
                if kind == "in":
                    def tile(t, i=0):
                        for part in range(2):
                            c = part * F + (half * KF + t) * P
                            load(s0 + 2 * t + part, w_in[f][:, :, bass.ds(c + i * 2 * P, P)], KD, i * RING)

                    with sp.Fori(0, KF // 2) as i:
                        tile(0, i)
                        tile(1, i)
                    tile(KF - 1)
                elif kind == "out":
                    with sp.Fori(0, KD // RING) as i:
                        for d in range(RING):
                            load(s0 + d, w_out[f][:, half * KF:(half + 1) * KF, bass.ds(d * P + i * RING * P, P)],
                                 KF, i * RING)
                elif kind == "mixer0":
                    for n, c in enumerate(MIX_COLS):
                        load(s0 + n, w_mix[:, :, c:c + P], KD)
                    s = s0 + len(MIX_COLS)
                    for t in range(AT):
                        sp.wait_ge(slab_lo, s + t + 1)
                        for g in range(2):
                            c = (t + g * AT) * AD
                            sp.dma_start(raw[:, slot(s + t), 0:SLAB_IN].rearrange("p (k c) -> p k c", c=P)
                                         [:, :, g * AD:(g + 1) * AD], w_mix[:, :, c:c + AD])\
                              .then_inc(slab_loaded[slot(s + t)], 8 * 2 if g else 16)
                    load(s + AT, w_mix[:, :, COL_K:COL_K + P], KD)
                    load(s + AT + 1, w_mix[:, :, COL_V:COL_V + P], KD)
                elif kind == "mixer0_out":
                    for d in range(KD):
                        s = s0 + d
                        sp.wait_ge(slab_lo, s + 1)
                        dst = raw[:, slot(s), 0:SLAB_IN].rearrange("p (k c) -> p k c", c=P)
                        for g in range(2):
                            sp.dma_start(dst[g * AD:(g + 1) * AD, 0:AT, :],
                                         mix_w_out[g * AT * AD:(g + 1) * AT * AD, d * P:(d + 1) * P]
                                         .rearrange("(t r) c -> r t c", r=AD)).then_inc(slab_loaded[slot(s)], 16)
                        sp.dma_start(dst[:, AT:KD, :], w_mix_out[:, AT:KD, d * P:(d + 1) * P])\
                          .then_inc(slab_loaded[slot(s)], 16)
                elif kind == "mixer1":
                    for d in range(KD):
                        for part in range(2):
                            c = part * D + d * P
                            load(s0 + 2 * d + part, w_glu[:, :, c:c + P], KD)
            for k in range(KD):
                sp.wait_ge(fin_ready, k + 1)
                sp.dma_start(out_t[k * P:(k + 1) * P, :], x[:, k, :]).then_inc(stored, 16)
            sp.wait_ge(stored, 16 * KD)

        parts = [1] * total
        for kind, f, half, s0 in phases:
            if kind == "mixer0":
                for t in range(AT):
                    parts[s0 + len(MIX_COLS) + t] = 2
            if kind == "mixer0_out":
                for d in range(KD):
                    parts[s0 + d] = 3

        def in_ring(s):
            return 16 * sum(parts[slot(s):s + 1:RING])

        def y2_view(q, g):
            n = PPB * 2
            return s5_y2[:, q * n:(q + 1) * n, :].rearrange("p (a g) c -> p g a c", g=2)[:, g, :, :]

        @block.scalar
        def _(act):
            steps = [0]

            def split_hi(s, n, i=0):
                act.wait_ge(slab_loaded[slot(s)], in_ring(s) + i * 16)
                act.wait_ge(slab_used, s + 1 + i * RING)
                act.activation(w_hi[:, slot(s), 0:n], raw[:, slot(s), 0:n], ACT.Copy).then_inc(slab_hi, 1)

            def split_ahead(s, count):
                for q in range(s + LEAD, min(s + LEAD + count, total)):
                    if q not in late:
                        split_hi(q, sizes[q])

            def norm_tile(n, k):
                if n:
                    act.wait_ge(x_ready, (n - 1) * KD + k + 1)
                if n == NORM_S5:
                    act.activation(s5_xg[:, k, :].rearrange("p (j c) -> p j c", j=L),
                                   x[:, k, :].rearrange("p (c j) -> p j c", j=L), ACT.Copy,
                                   scale=g_all[:, n, k:k + 1]).then_inc(u_tile, 1)
                if n in SPLIT_NORMS:
                    act.activation(xg_hi[:, k, :], x[:, k, :], ACT.Copy, scale=g_all[:, n, k:k + 1])\
                       .then_inc(xg_hi_ready, 1)
                if n * KD + k:
                    act.wait_ge(ssq_ready, n * KD + k)
                act.activation(sq[:], x[:, k, :], ACT.Square).then_inc(sq_ready, 1)

            def norm_root(n):
                act.wait_ge(mean_ready, n + 1)
                act.activation(rms[:], rms[:], ACT.Sqrt).then_inc(rms_ready, 1)

            def hidden(t, hi, i=0):
                act.wait_ge(gate_scaled, t + 1 + i)
                act.activation(silu_g[:], gate_r[:], ACT.Silu).then_inc(silu_ready, 1)
                act.wait_ge(hid_ready, t + 1 + i)
                act.activation(hi, hid[:], ACT.Copy).then_inc(hid_hi, 1)

            def mixer0(s0):
                for n in range(3 * BH):
                    split_ahead(s0 + n, 1)
                    act.wait_ge(proj_scaled, n + 1)
                    src = (b_e, b_q, b_g)[n // BH][:, n % BH, :]
                    dst = b_k[:, n % BH, :] if n < BH else b_tmp[:, n % 2, :]
                    if n >= BH + 2:
                        act.wait_ge(sig_used, n - BH - 1)
                    act.activation(dst, src, ACT.Sigmoid).then_inc(sig_ready, 1)
                act.wait_ge(f_ready, 1)
                act.activation(b_cum[:], b_k[:], ACT.Ln).then_inc(logf_ready, 1)
                s = s0 + 3 * BH
                act.wait_ge(mk_stored, 16 * MK_STORES)
                for pair in range(BH // 2):
                    split_ahead(s + 2 * pair, 2)
                    act.wait_ge(slab_used, used(s + 2 * pair + 1))
                    for m in range(NT):
                        src = bank[2 * pair + m // 2][:, (m % 2) * 2 * P:(m % 2 + 1) * 2 * P]
                        act.activation(b_v[:, m, 2 * pair * P:2 * (pair + 1) * P], src, ACT.Copy,
                                       scale=r_col[:, m:m + 1]).then_inc(nat_taken, 1)
                    if pair == 0:
                        act.wait_ge(cum_ready, 1)
                        act.wait_ge(f_ready, 2)
                        act.activation(b_e[:], b_cum[:], ACT.Exp).then_inc(exp_ready, 1)
                        act.wait_ge(exp_used, 1)
                        act.activation(b_e[:], b_cum[:], ACT.Exp, scale=-1.0).then_inc(exp_ready, 1)
                    else:
                        act.wait_ge(cum_ready, 2)
                        act.activation(b_cum[:], b_cum[:], ACT.Exp).then_inc(exp_ready, 1)
                s = s0 + 4 * BH
                for n in range(AT + 2):
                    split_ahead(s + n, 1)
                act.wait_ge(slab_used, used(s + AT + 1))
                act.activation(a_v[:, 0, :], bank[1][:, 0:P], ACT.Copy, scale=r_col[:, 0:1]).then_inc(nat_taken, 1)
                for m in range(1, NT):
                    act.activation(a_v[:, m, :], bank[1][:, m * P:(m + 1) * P], ACT.Copy,
                                   scale=r_col[:, m:m + 1]).then_inc(nat_taken, 1)
                for h in range(BH):
                    act.wait_ge(kt_ready, h + 1)
                    if h >= 2:
                        act.wait_ge(kv_ready, h - 1)
                    act.activation(k_end[:, h % 2, :, :], bank[1][:].rearrange("p (m d) -> p m d", d=P), ACT.Copy)\
                       .then_inc(kt_taken, 1)
                    if h >= 1:
                        o_out(h - 1)
                o_out(BH - 1)
                act.wait_ge(o_mean, 1)
                act.activation(rms[:], rms[:], ACT.Sqrt).then_inc(o_rms, 1)
                for h in range(BH):
                    act.wait_ge(rec_ready, h + 1)
                    act.activation(rec_h[:, h, :], rec[:, h % 2, :], ACT.Copy).then_inc(mix_hi, 1)
                for u in range(len(UNITS) + 2):
                    if u < len(UNITS):
                        n, tp, g = UNITS[u]
                        k0 = 0 if n else P
                        act.wait_ge(m_ready, u + 1)
                        for j in range(2):
                            act.activation(prob[:, u % 2, j, k0:], prob[:, u % 2, j, k0:], ACT.Exp,
                                           bias=max_neg[:, u % 2, j:j + 1], accum_out=rowsum[:, u % 2, j:j + 1])\
                               .then_inc(p_exp, 1)
                        act.activation(sink_e[:, u % 2, :], sink_d[:, u % 2, :], ACT.Exp).then_inc(p_exp, 1)
                    if 1 <= u <= len(UNITS):
                        v = u - 1
                        n = UNITS[v][0]
                        act.wait_ge(pt_ready, v + 1)
                        if v >= 2:
                            act.wait_ge(pv_done, v - 1)
                        for kt in range(0 if n else 1, 2):
                            act.activation(prob_t[:, v % 2, :, kt, :],
                                           bank[2 + v % 2][:].rearrange("p (j k q) -> p j k q", j=2, k=2)[:, :, kt, :],
                                           ACT.Copy).then_inc(pt_taken, 1)
                    if u >= 2 and (u - 2) % 4 == 3:
                        n = (u - 2) // 4
                        act.wait_ge(pv_done, 4 * (n + 1))
                        act.activation(att_h[:, :, n * P:(n + 1) * P],
                                       bank[4 + n % 2][:].rearrange("p (t q) -> p t q", q=P), ACT.Copy).then_inc(att_hi, 1)

            def mixer1(s0):
                for b in range(2):
                    act.wait_ge(k_summed, b + 1)
                    act.activation(s5_k[:, b * KD // 2:(b + 1) * KD // 2, :],
                                   bank[b][:].rearrange("p (t c) -> p t c", c=P), ACT.Copy).then_inc(k_ready, 1)
                for b in range(PAIRS // PPB):
                    act.wait_ge(st_ready, b + 1)
                    act.activation(s5_x[:, 1, b * PPB:(b + 1) * PPB, 1:NC],
                                   bank[4 + b][:].rearrange("p (a c) -> p a c", c=NC)[:, :, 0:NC - 1], ACT.Copy)\
                       .then_inc(st_taken_a, 1)
                for q in range(PAIRS // PPB):
                    act.wait_ge(y_ready, 2 * q + 1)
                    act.activation(y2_view(q, 0), bank[2 * q][:].rearrange("p (a c) -> p a c", c=NC), ACT.Copy)\
                       .then_inc(y_taken_a, 1)
                for k in range(KD):
                    act.wait_ge(y_loaded[k // 2], 16)
                    if k >= 2:
                        act.wait_ge(y_lo_ready, k - 1)
                    gelu = (sq, ssq)[k % 2]
                    act.activation(gelu[:], s5_y[:, k, :], ACT.Gelu_apprx_tanh).then_inc(gelu_ready, 1)
                    act.wait_ge(gelu_ready, k + 1)
                    act.activation(y_hi[:, k, :], gelu[:], ACT.Copy).then_inc(y_hi_ready, 1)
                    if k == 0:
                        for s in late:
                            split_hi(s, sizes[s])
                for d in range(KD):
                    split_ahead(s0 + 2 * d, 2)
                    act.wait_ge(slab_used, used(s0 + 2 * d + 1))
                    if d >= 2:
                        act.wait_ge(glu_mul, d - 1)
                    act.activation(sig[:, d % 2, :], up_ps[d % 2][:], ACT.Sigmoid).then_inc(glu_sig, 1)
                    if d:
                        norm_tile(NORM_S5 + 1, d - 1)
                norm_tile(NORM_S5 + 1, KD - 1)
                norm_root(NORM_S5 + 1)

            def o_out(h):
                act.wait_ge(inter_done, h + 1)
                act.activation(b_o[:, h, :], bank[2 + h % 2][:], ACT.Copy).then_inc(o_taken, 1)
                act.activation(squares[:, h, :], bank[2 + h % 2][:], ACT.Square).then_inc(o_sq, 1)

            act.dma_start(g_all[:, 0:6, :], norm_g).then_inc(const_loaded, 16)
            act.dma_start(g_all[:, 6, :], final_g).then_inc(const_loaded, 16)
            act.dma_start(tiny["lam_r"][:], s5_a_re).then_inc(s5_loaded, 16)
            act.dma_start(tiny["lam_i"][:], s5_a_im).then_inc(s5_loaded, 16)
            for g in range(2):
                act.dma_start(tiny["log_dt"][g * NS:(g + 1) * NS, :], s5_log_step[g].partition_broadcast(NS))\
                   .then_inc(s5_loaded, 16)
            act.dma_start(d_col[:], s5_d).then_inc(s5_loaded, 16)
            act.dma_start(sink[:], attn_sinks[0].partition_broadcast(P)).then_inc(small_loaded, 16)
            act.dma_start(lb_in[:], hgrn_lb).then_inc(small_loaded, 16)
            act.wait_ge(s5_loaded, 16 * 5)
            act.activation(tiny["log_dt"][:], tiny["log_dt"][:], ACT.Exp).then_inc(s5_dt, 1)
            act.wait_ge(s5_angles, 1)
            act.activation(tiny["mag"][:], tiny["mag"][:], ACT.Exp).then_inc(s5_trig, 1)
            act.activation(tiny["angle"][:], tiny["angle"][:], ACT.Sin).then_inc(s5_trig, 1)
            act.activation(tiny["angle_c"][:], tiny["angle_c"][:], ACT.Sin).then_inc(s5_trig, 1)
            act.wait_ge(s5_w_turned, 1)
            act.activation(w_rows[:], bank[7][:].rearrange("p (a c) -> p a c", c=P), ACT.Copy).then_inc(s5_w_rows, 1)
            act.wait_ge(const_loaded, 32)
            act.wait_ge(x_loaded, 16 * KD)
            for k in range(KD):
                norm_tile(0, k)
            norm_root(0)
            split_ahead(-LEAD, LEAD)
            act.wait_ge(mk_stored, 16)
            for kind, f, half, s0 in phases:
                if kind == "in":
                    t0 = (HALVES * f + half) * KF
                    with act.Fori(0, KF // 2) as i:
                        for t in range(2):
                            for part in range(2):
                                split_hi(s0 + 2 * t + part + LEAD, SLAB_IN, i)
                            hidden(t0 + t, h_hi[:, bass.ds(i * 2 + t, 1), :].squeeze(1), i * 2)
                    split_ahead(s0 + 2 * (KF - 1), 2)
                    hidden(t0 + KF - 1, h_hi[:, KF - 1, :])
                elif kind == "out":
                    for d in range(KD):
                        split_ahead(s0 + d, 1)
                        if half == HALVES - 1:
                            norm_tile(NORMS[f] + 1, d)
                    if half == HALVES - 1:
                        norm_root(NORMS[f] + 1)
                elif kind == "mixer1":
                    mixer1(s0)
                elif kind == "mixer0":
                    act.wait_ge(lb_exp, 1)
                    act.activation(lb[:], lb_c[:], ACT.Exp).then_inc(act_step, 1)
                    mixer0(s0)
                elif kind == "mixer0_out":
                    for d in range(KD):
                        split_ahead(s0 + d, 1)
                        norm_tile(NORM_MIX + 1, d)
                    norm_root(NORM_MIX + 1)

        @block.vector
        def _(dve):
            count = [0]

            def step(ins):
                count[0] += 1
                ins.then_inc(dve_step, 1)
                dve.wait_ge(dve_step, count[0])

            def split_lo(s, n, i=0):
                dve.wait_ge(slab_hi, s + 1 + i * RING)
                dve.tensor_tensor(w_lo[:, slot(s), 0:n], raw[:, slot(s), 0:n],
                                  w_hi[:, slot(s), 0:n].bitcast(F32), ALU.subtract).then_inc(slab_lo, 1)

            def split_ahead(s, count):
                for q in range(s + LEAD, min(s + LEAD + count, total)):
                    if q not in late:
                        split_lo(q, sizes[q])

            def norm_tile(n, k):
                if n in SPLIT_NORMS:
                    dve.wait_ge(xg_hi_ready, xg_count(n, k))
                    dve.scalar_tensor_tensor(out=xg_lo[:, k, :], in0=x[:, k, :], scalar=g_all[:, n, k:k + 1],
                                             in1=xg_hi[:, k, :].bitcast(F32), op0=ALU.mult,
                                             op1=ALU.subtract).then_inc(xg_lo_ready, 1)
                dve.wait_ge(sq_ready, n * KD + k + 1)
                if k == 0:
                    if n:
                        dve.wait_ge(norm_sum, n)
                    dve.tensor_copy(ssq[:], sq[:]).then_inc(ssq_ready, 1)
                else:
                    dve.wait_ge(ssq_ready, n * KD + k)
                    dve.tensor_tensor(ssq[:], ssq[:], sq[:], ALU.add).then_inc(ssq_ready, 1)

            def norm_root(n):
                dve.wait_ge(norm_sum, n + 1)
                dve.tensor_scalar(rms[:], norm_ps[:], 1.0 / D, EPS, ALU.mult, ALU.add).then_inc(mean_ready, 1)
                dve.wait_ge(rms_ready, n + 1)
                dve.reciprocal(rinv[:], rms[:]).then_inc(rinv_ready, 1)
                dve.wait_ge(rinv_ready, n + 1)

            def hidden(t, s, b, hi, lo, i=0, turn=0):
                dve.wait_ge(slab_used, used(s) + turn)
                dve.tensor_tensor(gate_r[:], gate_ps[b][:], rinv[:], ALU.mult).then_inc(gate_scaled, 1)
                dve.wait_ge(slab_used, used(s + 1) + turn)
                dve.wait_ge(silu_ready, t + 1 + i)
                dve.tensor_tensor(up_s[:], up_ps[b][:], silu_g[:], ALU.mult).then_inc(banks_free, 1)
                dve.wait_ge(banks_free, 2 + t + 1 + i)
                dve.tensor_tensor(hid[:], up_s[:], rinv[:], ALU.mult).then_inc(hid_ready, 1)
                dve.wait_ge(hid_hi, t + 1 + i)
                dve.tensor_tensor(lo, hid[:], hi.bitcast(F32), ALU.subtract).then_inc(hid_lo, 1)

            def s5_parameters():
                t = tiny
                dt, lr, li = t["log_dt"][:], t["lam_r"][:], t["lam_i"][:]
                dve.wait_ge(pool_const, POOL_COUNT)
                dve.wait_ge(s5_dt, 1)
                kk = k_count[:].unsqueeze(2).broadcast_to([P, L + 1, PAIRS])

                def times_k(a):
                    return a.unsqueeze(1).broadcast_to([P, L + 1, PAIRS])

                step(dve.tensor_tensor(t["num_a"][:], lr, dt, ALU.mult))
                step(dve.tensor_tensor(t["num_b"][:], li, dt, ALU.mult))
                step(dve.tensor_tensor(t["mag"][:], kk, times_k(t["num_a"][:]), ALU.mult))
                step(dve.tensor_tensor(t["angle"][:], kk, times_k(t["num_b"][:]), ALU.mult))
                step(dve.tensor_scalar(t["turns"][:], t["angle"][:], 1.0 / TWO_PI, ROUND, ALU.mult, ALU.add))
                step(dve.tensor_scalar(t["turns"][:], t["turns"][:], -ROUND, None, ALU.add))
                for part in TWO_PI_PARTS:
                    step(dve.scalar_tensor_tensor(out=t["angle"][:], in0=t["turns"][:], scalar=-part,
                                                  in1=t["angle"][:], op0=ALU.mult, op1=ALU.add))
                step(dve.tensor_scalar(t["angle_c"][:], t["angle"][:], TWO_PI / 4, None, ALU.add))
                step(dve.tensor_scalar(t["fold"][:], t["angle_c"][:], TWO_PI / 2, -TWO_PI, ALU.is_gt, ALU.mult))
                step(dve.tensor_tensor(t["angle_c"][:], t["angle_c"][:], t["fold"][:], ALU.add))
                step(dve.tensor_scalar(t["angle_c"][:], t["angle_c"][:], PI_BELOW, -PI_BELOW, ALU.min, ALU.max))
                dve.tensor_scalar(t["angle"][:], t["angle"][:], PI_BELOW, -PI_BELOW, ALU.min, ALU.max)\
                   .then_inc(s5_angles, 1)
                step(dve.tensor_tensor(t["den_l"][:], lr, lr, ALU.mult))
                step(dve.tensor_tensor(t["abr1"][:], li, li, ALU.mult))
                step(dve.tensor_tensor(t["den_l"][:], t["den_l"][:], t["abr1"][:], ALU.add))
                step(dve.reciprocal(t["den_l"][:], t["den_l"][:]))
                dve.wait_ge(s5_trig, 3)
                step(dve.tensor_tensor(pow_r[:], t["mag"][:], t["angle_c"][:], ALU.mult))
                step(dve.tensor_tensor(pow_i[:], t["mag"][:], t["angle"][:], ALU.mult))
                ar, ai = pow_r[:, 1, :], pow_i[:, 1, :]
                step(dve.tensor_scalar(t["abr1"][:], ar, -1.0, None, ALU.add))
                step(dve.tensor_tensor(t["num_a"][:], t["abr1"][:], lr, ALU.mult))
                step(dve.tensor_tensor(t["num_b"][:], ai, li, ALU.mult))
                step(dve.tensor_tensor(t["num_a"][:], t["num_a"][:], t["num_b"][:], ALU.add))
                step(dve.tensor_tensor(coef[:, 0, :], t["num_a"][:], t["den_l"][:], ALU.mult))
                step(dve.tensor_tensor(t["num_a"][:], ai, lr, ALU.mult))
                step(dve.tensor_tensor(t["num_b"][:], t["abr1"][:], li, ALU.mult))
                step(dve.tensor_tensor(t["num_a"][:], t["num_a"][:], t["num_b"][:], ALU.subtract))
                step(dve.tensor_tensor(coef[:, 1, :], t["num_a"][:], t["den_l"][:], ALU.mult))
                for j in range(L):
                    k = L - 1 - j
                    cr, ci, pr, pi = coef[:, 0, :], coef[:, 1, :], pow_r[:, k, :], pow_i[:, k, :]
                    wr, wi, wt = t["w_r"][:, j, :], t["w_i"][:, j, :], t["w_t"][:, j, :]
                    step(dve.tensor_tensor(wr, cr, pr, ALU.mult))
                    step(dve.tensor_tensor(wt, ci, pi, ALU.mult))
                    step(dve.tensor_tensor(wr, wr, wt, ALU.subtract))
                    step(dve.tensor_tensor(wi, cr, pi, ALU.mult))
                    step(dve.tensor_tensor(wt, ci, pr, ALU.mult))
                    step(dve.tensor_tensor(wi, wi, wt, ALU.add))
                step(dve.tensor_copy(leap_r[:], pow_r[:, L, :].unsqueeze(1).broadcast_to([P, 2, PAIRS])))
                step(dve.tensor_scalar(leap_i[:, 0, :], pow_i[:, L, :], -1.0, None, ALU.mult))
                step(dve.tensor_copy(leap_i[:, 1, :], pow_i[:, L, :]))
                dve.tensor_reduce(diag[:], ident[:].rearrange("p (b c) -> p c b", c=GC), AX.X, ALU.add)\
                   .then_inc(s5_w_ready, 1)

            def mixer1(s0):
                dve.wait_ge(k_ready, 2)
                for t in range(KD):
                    ins = dve.scalar_tensor_tensor(out=s5_k[:, t, 0:GC], in0=diag[:], scalar=d_col[:, t:t + 1],
                                                   in1=s5_k[:, t, 0:GC], op0=ALU.mult, op1=ALU.add)
                    ins.then_inc(k_diag, 1)
                dve.wait_ge(row_ready, 1)
                dve.tensor_copy(r_row[:], bank[7][:, 0:NC]).then_inc(row_taken, 1)
                dve.wait_ge(row_taken, 1)
                dve.wait_ge(u_loaded, 16 * U_DMAS)
                for q in range(4):
                    n = G // 4
                    u = s5_u[:, q * n:(q + 1) * n, :]
                    dve.tensor_tensor(u, u, r_row[:].unsqueeze(1).broadcast_to([P, n, NC]), ALU.mult)\
                       .then_inc(u_ready, 1)
                dve.memset(s5_x[:, :, :, 0], 0.0).then_inc(u_ready, 1)
                for b in range(PAIRS // PPB):
                    dve.wait_ge(st_ready, b + 1)
                    dve.tensor_copy(s5_x[:, 0, b * PPB:(b + 1) * PPB, 1:NC],
                                    bank[b][:].rearrange("p (a c) -> p a c", c=NC)[:, :, 0:NC - 1])\
                       .then_inc(st_taken_d, 1)
                dve.wait_ge(st_taken_d, PAIRS // PPB)
                dve.wait_ge(st_taken_a, PAIRS // PPB)
                for c in range(1, NC - 1):
                    b = c % 2
                    now, nxt = s5_x[:, :, :, c], s5_x[:, :, :, c + 1]
                    dve.tensor_tensor(scan_a[:, b], leap_r[:], now, ALU.mult).then_inc(dve_step, 1)
                    dve.tensor_tensor(scan_b[:, b, 0], leap_i[:, 0], s5_x[:, 1, :, c], ALU.mult).then_inc(dve_step, 1)
                    count[0] += 2
                    step(dve.tensor_tensor(scan_b[:, b, 1], leap_i[:, 1], s5_x[:, 0, :, c], ALU.mult))
                    step(dve.tensor_tensor(nxt, nxt, scan_a[:, b], ALU.add))
                    ins = dve.tensor_tensor(nxt, nxt, scan_b[:, b], ALU.add)
                    if c < NC - 2:
                        step(ins)
                    else:
                        ins.then_inc(scanned, 1)
                for q in range(PAIRS // PPB):
                    dve.wait_ge(y_ready, 2 * q + 2)
                    dve.tensor_copy(y2_view(q, 1), bank[2 * q + 1][:].rearrange("p (a c) -> p a c", c=NC))\
                       .then_inc(y_taken_d, 1)
                for k in range(KD):
                    gelu = (sq, ssq)[k % 2]
                    dve.wait_ge(y_hi_ready, k + 1)
                    dve.tensor_tensor(y_lo[:, k, :], gelu[:], y_hi[:, k, :].bitcast(F32), ALU.subtract)\
                       .then_inc(y_lo_ready, 1)
                    if k == 0:
                        for s in late:
                            split_lo(s, sizes[s])
                for d in range(KD):
                    split_ahead(s0 + 2 * d, 2)
                    dve.wait_ge(glu_sig, d + 1)
                    dve.tensor_tensor(glu[:, d % 2, :], gate_ps[d % 2][:], sig[:, d % 2, :], ALU.mult).then_inc(glu_mul, 1)
                    dve.wait_ge(glu_mul, d + 1)
                    xv = x[:, d, :].rearrange("p (c j) -> p j c", j=L)
                    dve.tensor_tensor(xv, xv, glu[:, d % 2, :].rearrange("p (j c) -> p j c", j=L), ALU.add).then_inc(x_ready, 1)
                    norm_tile(NORM_S5 + 1, d)
                norm_root(NORM_S5 + 1)

            def mixer0(s0):
                dve.wait_ge(col_ready, 1)
                dve.tensor_copy(r_col[:], bank[7][:, 0:NT]).then_inc(col_taken, 1)
                for n in range(3 * BH):
                    split_ahead(s0 + n, 1)
                    dve.wait_ge(slab_used, used(s0 + n))
                    dst = (b_e, b_q, b_g)[n // BH]
                    dve.tensor_tensor(dst[:, n % BH, :], bank[n % 4][:], rinv[:], ALU.mult).then_inc(proj_scaled, 1)
                    dve.wait_ge(sig_ready, n + 1)
                    if n < BH:
                        f = b_k[:, n, :]
                        dve.tensor_scalar(f, f, lb_c[:, n:n + 1], lb[:, n:n + 1], ALU.mult, ALU.add)\
                           .then_inc(f_one, 1)
                        if n == BH - 1:
                            dve.wait_ge(f_one, BH)
                            dve.wait_ge(mk_stored, 16 * MK_STORES)
                            dve.memset(scores[:], 0.0).then_inc(f_ready, 1)
                    else:
                        dve.tensor_tensor(dst[:, n % BH, :], dst[:, n % BH, :], b_tmp[:, n % 2, :], ALU.mult)\
                           .then_inc(sig_used, 1)
                dve.wait_ge(logf_ready, 1)
                step(dve.tensor_scalar(b_k[:], b_k[:], -1.0, 1.0, ALU.mult, ALU.add))
                cum = b_cum[:].rearrange("p h (c j) -> p (h c) j", j=CH)
                for j in range(1, CH):
                    ins = dve.tensor_tensor(cum[:, :, j], cum[:, :, j], cum[:, :, j - 1], ALU.add)
                    if j < CH - 1:
                        step(ins)
                    else:
                        ins.then_inc(cum_ready, 1)
                s = s0 + 3 * BH
                split_ahead(s, 2)
                dve.wait_ge(cum_ready, 1)
                dve.tensor_copy(decay[:].rearrange("p h c -> p (h c)"), cum[:, :, CH - 1]).then_inc(f_ready, 1)
                dve.wait_ge(exp_ready, 1)
                step(dve.tensor_tensor(b_q[:], b_q[:], b_e[:], ALU.mult))
                dve.tensor_copy(decay[:], b_e[:].rearrange("p h (c j) -> p h c j", j=CH)[:, :, :, CH - 1])\
                   .then_inc(exp_used, 1)
                dve.wait_ge(exp_ready, 2)
                step(dve.tensor_tensor(b_kinv[:], b_k[:], b_e[:], ALU.mult))
                for h in range(BH):
                    c3 = b_cum[:, h, :].rearrange("p (c j) -> p c j", j=CH)
                    dve.wait_ge(dve_step, count[0])
                    ins = dve.tensor_tensor(c3, c3[:, :, CH - 1:CH].broadcast_to([P, NCH, CH]), c3, ALU.subtract)
                    if h < BH - 1:
                        step(ins)
                    else:
                        ins.then_inc(cum_ready, 1)
                split_ahead(s + 2, 2)
                dve.wait_ge(exp_ready, 3)
                dve.tensor_tensor(b_k[:], b_k[:], b_cum[:], ALU.mult).then_inc(b_ready, 1)
                s = s0 + 4 * BH
                for t in range(AT):
                    split_ahead(s + t, 1)
                    dve.wait_ge(slab_used, used(s + t))
                    dve.scalar_tensor_tensor(out=a_q[:, t, :], in0=bank[t % 4][:], scalar=AD ** -0.5, in1=rinv[:],
                                             op0=ALU.mult, op1=ALU.mult).then_inc(proj_scaled, 1)
                split_ahead(s + AT, 1)
                dve.wait_ge(slab_used, used(s + AT))
                dve.tensor_tensor(a_k[:], bank[0][:], rinv[:], ALU.mult).then_inc(proj_scaled, 1)
                split_ahead(s + AT + 1, 1)
                mask = causal[:].bitcast(I32).unsqueeze(1).broadcast_to([P, NT, P])
                for h in range(BH):
                    dve.wait_ge(sc_ready, h + 1)
                    dve.copy_predicated(scores[:, h % 2, :, :], mask,
                                        bank[0][:].rearrange("p (m q) -> p m q", q=P)).then_inc(sc_masked, 1)
                    dve.wait_ge(kv_ready, h + 1)
                    if h:
                        dve.wait_ge(inter_done, h)
                    kv = [bank[4 + i][:].rearrange("p (m v) -> p m v", v=P) for i in range(CPT)]
                    dve.tensor_copy(states[:, 1, :], kv[0][:, 0, :]).then_inc(state_ready, 1)
                    for c in range(1, NCH - 1):
                        dve.wait_ge(state_ready, h * (NCH - 1) + c)
                        dve.scalar_tensor_tensor(out=states[:, c + 1, :], in0=states[:, c, :],
                                                 scalar=decay[:, h, c:c + 1], in1=kv[c % CPT][:, c // CPT, :],
                                                 op0=ALU.mult, op1=ALU.add).then_inc(state_ready, 1)
                dve.wait_ge(o_sum, BH)
                dve.tensor_scalar(rms[:], bank[1][:], 1.0 / P, EPS, ALU.mult, ALU.add).then_inc(o_mean, 1)
                dve.wait_ge(o_rms, 1)
                dve.reciprocal(ssq[:], rms[:]).then_inc(o_rinv, 1)
                for h in range(BH):
                    dve.wait_ge(o_taken, h + 1)
                    step(dve.tensor_tensor(b_g[:, h, :], b_g[:, h, :], b_o[:, h, :], ALU.mult))
                    dve.wait_ge(o_bcast, h + 1)
                    dve.tensor_tensor(rec[:, h % 2, :], bank[4 + h][:], b_g[:, h, :], ALU.mult).then_inc(rec_ready, 1)
                    dve.wait_ge(mix_hi, h + 1)
                    dve.tensor_tensor(rec_l[:, h, :], rec[:, h % 2, :], rec_h[:, h, :].bitcast(F32),
                                      ALU.subtract).then_inc(mix_lo, 1)
                for u in range(len(UNITS) + 3):
                    if u < len(UNITS):
                        n, tp, g = UNITS[u]
                        k0 = 0 if n else P
                        b = u % 2
                        h0 = AT * g + 2 * tp
                        dve.wait_ge(s_ready, u + 1)
                        if u >= 2:
                            dve.wait_ge(pt_ready, u - 1)
                        for j in range(2):
                            ins = dve.scalar_tensor_tensor(
                                out=prob[:, b, j, k0:], in0=dist[:, k0:], scalar=-SLOPES[h0 + j],
                                in1=bank[g][:, j * 2 * P + k0:(j + 1) * 2 * P], op0=ALU.mult, op1=ALU.add)
                            if j:
                                ins.then_inc(s_taken, 1)
                            else:
                                ins.then_inc(dve_step, 1)
                                count[0] += 1
                        dve.wait_ge(s_taken, u + 1)
                        dve.wait_ge(dve_step, count[0])
                        step(dve.tensor_reduce(max_neg[:, b, :], prob[:, b, :, k0:], AX.X, ALU.max, negate=True))
                        step(dve.tensor_tensor(max_neg[:, b, :], max_neg[:, b, :], sink_neg[:, h0:h0 + 2], ALU.min))
                        dve.tensor_tensor(sink_d[:, b, :], sink[:, h0:h0 + 2], max_neg[:, b, :], ALU.add)\
                           .then_inc(m_ready, 1)
                    if 1 <= u <= len(UNITS):
                        v = u - 1
                        b = v % 2
                        k0 = 0 if UNITS[v][0] else P
                        dve.wait_ge(p_exp, 3 * (v + 1))
                        step(dve.tensor_tensor(den[:, b, :], rowsum[:, b, :], sink_e[:, b, :], ALU.add))
                        step(dve.reciprocal(rden[:, b, :], den[:, b, :]))
                        for j in range(2):
                            dve.tensor_scalar(prob[:, b, j, k0:], prob[:, b, j, k0:], rden[:, b, j:j + 1], None,
                                              ALU.mult).then_inc(p_ready, 1)
                    if u >= 3 and (u - 3) % 4 == 3:
                        n = (u - 3) // 4
                        dve.wait_ge(att_hi, n + 1)
                        dve.tensor_tensor(att_l[:, :, n * P:(n + 1) * P],
                                          bank[4 + n % 2][:].rearrange("p (t q) -> p t q", q=P),
                                          att_h[:, :, n * P:(n + 1) * P].bitcast(F32), ALU.subtract)\
                           .then_inc(att_lo, 1)

            dve.memset(ones[:], 1.0).then_inc(ones_set, 1)
            s5_parameters()
            dve.wait_ge(small_loaded, 32)
            step(dve.tensor_tensor(lb_c[:], lb_in[:], lb_in[:], ALU.subtract))
            dve.tensor_scalar(sink_neg[:], sink[:], -1.0, None, ALU.mult).then_inc(lb_exp, 1)
            dve.wait_ge(const_loaded, 32)
            dve.wait_ge(x_loaded, 16 * KD)
            for k in range(KD):
                norm_tile(0, k)
            norm_root(0)
            split_ahead(-LEAD, LEAD)
            for kind, f, half, s0 in phases:
                if kind == "in":
                    t0 = (HALVES * f + half) * KF
                    with dve.Fori(0, KF // 2) as i:
                        for t in range(2):
                            for part in range(2):
                                split_lo(s0 + 2 * t + part + LEAD, SLAB_IN, i)
                            hidden(t0 + t, s0 + 2 * t, t, h_hi[:, bass.ds(i * 2 + t, 1), :].squeeze(1),
                                   h_lo[:, bass.ds(i * 2 + t, 1), :].squeeze(1), i * 2, i * RING)
                    split_ahead(s0 + 2 * (KF - 1), 2)
                    hidden(t0 + KF - 1, s0 + 2 * (KF - 1), 0, h_hi[:, KF - 1, :], h_lo[:, KF - 1, :])
                elif kind == "out":
                    for d in range(KD):
                        split_ahead(s0 + d, 1)
                        dve.wait_ge(slab_used, used(s0 + d))
                        add = dve.scalar_tensor_tensor(out=x[:, d, :], in0=out_ps[d % 2][:], scalar=0.5,
                                                       in1=x[:, d, :], op0=ALU.mult, op1=ALU.add)
                        if half == HALVES - 1:
                            add.then_inc(x_ready, 1)
                            norm_tile(NORMS[f] + 1, d)
                        else:
                            add.then_inc(x_half, 1)
                    if half == HALVES - 1:
                        norm_root(NORMS[f] + 1)
                elif kind == "mixer1":
                    mixer1(s0)
                elif kind == "mixer0":
                    dve.wait_ge(act_step, 1)
                    step(dve.reciprocal(lb_c[:], lb[:]))
                    step(dve.tensor_tensor(lb_in[:], lb[:], lb_c[:], ALU.mult))
                    step(dve.tensor_tensor(lb[:], lb_in[:], lb_in[:], ALU.subtract))
                    step(dve.tensor_scalar(lb_c[:], lb[:], -1.0, 1.0, ALU.mult, ALU.add))
                    mixer0(s0)
                elif kind == "mixer0_out":
                    for d in range(KD):
                        split_ahead(s0 + d, 1)
                        dve.wait_ge(slab_used, used(s0 + d))
                        dve.tensor_tensor(x[:, d, :], out_ps[d % 2][:], x[:, d, :], ALU.add).then_inc(x_ready, 1)
                        norm_tile(NORM_MIX + 1, d)
                    norm_root(NORM_MIX + 1)
            for k in range(KD):
                dve.scalar_tensor_tensor(out=x[:, k, :], in0=x[:, k, :], scalar=g_all[:, NORM_FIN, k:k + 1],
                                         in1=rinv[:], op0=ALU.mult, op1=ALU.mult).then_inc(fin_ready, 1)

        @block.tensor
        def _(pe):
            def product(out, s, k, hi, lo, start, stop):
                wh = w_hi[:, slot(s), k * P:(k + 1) * P]
                wl = w_lo[:, slot(s), k * P:(k + 1) * P]
                pe.matmul(out, wh, hi, start=start, stop=False)
                pe.matmul(out, wh, lo, start=False, stop=False)
                return pe.matmul(out, wl, hi, start=False, stop=stop)

            def norm(n):
                pe.wait_ge(ssq_ready, (n + 1) * KD)
                if n:
                    pe.wait_ge(mean_ready, n)
                pe.matmul(norm_ps[:], ones[:], ssq[:], start=True, stop=True).then_inc(norm_sum, 1)

            def natural(s, count, out):
                for m in range(NT):
                    for k in range(KD):
                        xh = xg_hi[:, k, m * P:(m + 1) * P]
                        xl = xg_lo[:, k, m * P:(m + 1) * P]
                        wh = w_hi[:, slot(s):slot(s) + count, k * P:(k + 1) * P]
                        wl = w_lo[:, slot(s):slot(s) + count, k * P:(k + 1) * P]
                        pe.matmul(out(m), xh, wh, start=k == 0, stop=False)
                        pe.matmul(out(m), xh, wl, start=False, stop=False)
                        mm = pe.matmul(out(m), xl, wh, start=False, stop=k == KD - 1)
                return mm

            def mixer0(s0):
                for n in range(3 * BH):
                    s = s0 + n
                    if n >= 4:
                        pe.wait_ge(proj_scaled, n - 3)
                    pe.wait_ge(slab_lo, split(s))
                    for k in range(KD):
                        if n == 0:
                            pe.wait_ge(xg_lo_ready, xg_count(NORM_MIX, k))
                        mm = product(bank[n % 4][:], s, k, xg_hi[:, k, :], xg_lo[:, k, :], k == 0, k == KD - 1)
                    mm.then_inc(slab_used, 1)
                    if n == 0:
                        pe.wait_ge(rinv_ready, NORM_MIX + 1)
                        for m in range(NT):
                            mm = pe.matmul(bank[7][:, m:m + 1], rinv[0:1, m * P:(m + 1) * P], ones[0:1, 0:1],
                                           start=True, stop=True)
                        mm.then_inc(col_ready, 1)
                s = s0 + 3 * BH
                for pair in range(BH // 2):
                    pe.wait_ge(proj_scaled, 3 * BH)
                    pe.wait_ge(slab_lo, split(s + 2 * pair + 1))
                    assert slot(s + 2 * pair) % 2 == 0

                    def out(m):
                        return bank[2 * pair + m // 2][:, (m % 2) * 2 * P:(m % 2 + 1) * 2 * P]\
                            .rearrange("p (a c) -> p a c", a=2)
                    natural(s + 2 * pair, 2, out).then_inc(slab_used, 2)
                s = s0 + 4 * BH
                for n in range(AT + 1):
                    pe.wait_ge(nat_taken, min(2 * NT, NT * (n // 2 + 1)) if n < AT else 2 * NT)
                    if n == AT:
                        pe.wait_ge(proj_scaled, 3 * BH + 1)
                    pe.wait_ge(slab_lo, split(s + n))
                    for k in range(KD):
                        mm = product(bank[n % 4][:], s + n, k, xg_hi[:, k, :], xg_lo[:, k, :], k == 0, k == KD - 1)
                    mm.then_inc(slab_used, 1)
                pe.wait_ge(proj_scaled, 3 * BH + 2)
                pe.wait_ge(slab_lo, split(s + AT + 1))
                natural(s + AT + 1, 1, lambda m: bank[1][:, m * P:(m + 1) * P]).then_inc(slab_used, 1)

                def head_scores(h):
                    if h:
                        pe.wait_ge(sc_masked, h)
                    for m in range(NT):
                        t = slice(m * P, (m + 1) * P)
                        mm = pe.matmul(bank[0][:, t], b_kinv[:, h, t], b_q[:, h, t], start=True, stop=True)
                    mm.then_inc(sc_ready, 1)
                    if h:
                        pe.wait_ge(kt_taken, h)
                    for m in range(NT):
                        t = slice(m * P, (m + 1) * P)
                        mm = pe.transpose(bank[1][:, t], b_k[:, h, t], ident[:])
                    mm.then_inc(kt_ready, 1)

                def head_chunks(h):
                    v = b_v[:, :, h * P:(h + 1) * P]
                    pe.wait_ge(kt_taken, h + 1)
                    if h:
                        pe.wait_ge(state_ready, h * (NCH - 1))
                    for m in range(NT):
                        for i in range(CPT):
                            rows = slice(i * CH, (i + 1) * CH)
                            mm = pe.matmul(bank[4 + i][:, m * P:(m + 1) * P], k_end[rows, h % 2, m, :], v[rows, m, :],
                                           start=True, stop=True)
                    mm.then_inc(kv_ready, 1)
                    pe.wait_ge(sc_masked, h + 1)
                    if h >= 2:
                        pe.wait_ge(o_sq, h - 1)
                    ob = bank[2 + h % 2]
                    for m in range(NT):
                        pe.matmul(ob[:, m * P:(m + 1) * P], v[:, m, :], scores[:, h % 2, m, :], start=m == 0,
                                  stop=False, skip_group_check=True)
                    for c in range(1, NCH):
                        pe.wait_ge(state_ready, h * (NCH - 1) + c)
                        mm = pe.matmul(ob[:, c * CH:(c + 1) * CH], states[:, c, :], b_q[:, h, c * CH:(c + 1) * CH],
                                       start=False, stop=c == NCH - 1, skip_group_check=True)
                    mm.then_inc(inter_done, 1)

                def head_square(h):
                    pe.wait_ge(o_sq, h + 1)
                    if h == 0:
                        pe.wait_ge(kt_taken, BH)
                    pe.matmul(bank[1][h * CH:(h + 1) * CH, :], ones[:, 0:CH], squares[:, h, :], start=True, stop=True)\
                      .then_inc(o_sum, 1)

                pe.wait_ge(b_ready, 1)
                pe.wait_ge(nat_taken, 3 * NT)
                pe.wait_ge(proj_scaled, 3 * BH + AT + 1)
                head_scores(0)
                for h in range(BH):
                    head_chunks(h)
                    if h + 1 < BH:
                        head_scores(h + 1)
                    else:
                        for g in range(BH):
                            head_square(g)
                pe.wait_ge(o_rinv, 1)
                for h in range(BH):
                    pe.matmul(bank[4 + h][:], ones[h * CH:h * CH + 1, :], ssq[h * CH:h * CH + 1, :], start=True, stop=True)\
                      .then_inc(o_bcast, 1)

                for u in range(len(UNITS) + 2):
                    if u < len(UNITS):
                        n, tp, g = UNITS[u]
                        rows = slice(g * AD, (g + 1) * AD)
                        k0 = 0 if n else P
                        if u == 0:
                            pe.wait_ge(sc_masked, BH)
                            pe.wait_ge(o_mean, 1)
                        if u >= 2:
                            pe.wait_ge(s_taken, u - 1)
                        for j in range(2):
                            mm = pe.matmul(bank[g][:, j * 2 * P + k0:(j + 1) * 2 * P],
                                           a_q[rows, 2 * tp + j, n * P:(n + 1) * P],
                                           a_k[rows, (n - 1) * P + k0:(n + 1) * P], start=True, stop=True)
                        mm.then_inc(s_ready, 1)
                    if 1 <= u <= len(UNITS):
                        v = u - 1
                        n, tp, g = UNITS[v]
                        pe.wait_ge(p_ready, 2 * (v + 1))
                        if v >= 2:
                            pe.wait_ge(pt_taken, taken(v - 2))
                        else:
                            pe.wait_ge(o_sq, BH - 1 + v)
                        for j in range(2):
                            for kt in range(0 if n else 1, 2):
                                mm = pe.transpose(bank[2 + v % 2][:, (2 * j + kt) * P:(2 * j + kt + 1) * P],
                                                  prob[:, v % 2, j, kt * P:(kt + 1) * P], ident[:])
                        mm.then_inc(pt_ready, 1)
                    if u >= 2:
                        v = u - 2
                        n, tp, g = UNITS[v]
                        pe.wait_ge(pt_taken, taken(v))
                        if v % 4 == 0:
                            if n >= 2:
                                pe.wait_ge(att_lo, n - 1)
                            else:
                                pe.wait_ge(rec_ready, n + 1)
                        kts = range(0 if n else 1, 2)
                        for j in range(2):
                            for kt in kts:
                                mm = pe.matmul(bank[4 + n % 2][g * AD:(g + 1) * AD, (2 * tp + j) * P:(2 * tp + j + 1) * P],
                                               a_v[:, n - 1 + kt, g * AD:(g + 1) * AD], prob_t[:, v % 2, j, kt, :],
                                               start=kt == kts[0], stop=kt == 1)
                        mm.then_inc(pv_done, 1)

            def mixer1(s0):
                pe.wait_ge(mats_loaded, 16 * 2)
                for t in range(KD):
                    for i in range(PAIRS // KD):
                        pair = t * (PAIRS // KD) + i
                        for part in range(2):
                            mm = pe.matmul(bank[t // 4][i * 2 * GC:(i + 1) * 2 * GC, (t % 4) * P:(t % 4 + 1) * P],
                                           s5_bb[:, pair, part, :], s5_c[:, part, pair, 0:L * GC],
                                           start=part == 0, stop=part == 1)
                    if t % 4 == 3:
                        mm.then_inc(k_summed, 1)
                pe.wait_ge(rinv_ready, NORM_S5 + 1)
                r3 = rinv[0:1, :].rearrange("p (c j) -> p j c", j=L)
                pe.wait_ge(pool_const, POOL_ALL)
                for j in range(L):
                    mm = pe.matmul(bank[7][:, 0:NC], r_sel[:, (L - 1 - j) * GC:(2 * L - 1 - j) * GC], r3[:, j, :], start=j == 0, stop=j == L - 1)
                mm.then_inc(row_ready, 1)
                pe.wait_ge(bm_loaded, 16)
                pe.wait_ge(k_ready, 2)
                pe.wait_ge(row_taken, 1)
                for b in range(PAIRS // PPB):
                    pe.wait_ge(u_ready, b + 1)
                    for part in range(2):
                        for a in range(PPB):
                            for g in range(2):
                                group = 2 * (b * PPB + a) + g
                                mm = pe.matmul(bank[4 * part + b][g * NS:(g + 1) * NS, a * NC:(a + 1) * NC],
                                               s5_bm[:, part, group, :], s5_u[:, group, :], start=True, stop=True)
                    mm.then_inc(st_ready, 1)
                pe.wait_ge(t_loaded, 16 * L)
                pe.wait_ge(st_taken_a, PAIRS // PPB)
                pe.wait_ge(st_taken_d, PAIRS // PPB)
                for q in range(PAIRS // PPB):
                    for a in range(PPB):
                        for g in range(2):
                            group = 2 * (q * PPB + a) + g
                            pe.matmul(bank[2 * q + g][:, a * NC:(a + 1) * NC], s5_t[:, group, :], s5_u[:, group, :],
                                      start=a == 0, stop=False, skip_group_check=True)
                pe.wait_ge(scanned, 1)
                for q in range(PAIRS // PPB):
                    for g in range(2):
                        rows = slice(g * NS, (g + 1) * NS)
                        for a in range(PPB):
                            pair = q * PPB + a
                            for part in range(2):
                                mm = pe.matmul(bank[2 * q + g][:, a * NC:(a + 1) * NC],
                                               s5_c[rows, part, pair, GC:], s5_x[rows, part, pair, :],
                                               start=False, stop=a == PPB - 1 and part == 1, skip_group_check=True)
                        mm.then_inc(y_ready, 1)
                for d in range(KD):
                    if d >= 2:
                        pe.wait_ge(glu_mul, d - 1)
                    for part, out in enumerate((gate_ps[d % 2], up_ps[d % 2])):
                        s = s0 + 2 * d + part
                        if d < 2:
                            pe.wait_ge(y_taken_a, PAIRS // PPB)
                            pe.wait_ge(y_taken_d, PAIRS // PPB)
                        pe.wait_ge(slab_lo, split(s))
                        for k in range(KD):
                            if d == 0 and part == 0:
                                pe.wait_ge(y_lo_ready, k + 1)
                            mm = product(out[:], s, k, y_hi[:, k, :], y_lo[:, k, :], k == 0, k == KD - 1)
                        mm.then_inc(slab_used, 1)
                norm(NORM_S5 + 1)

            pe.wait_ge(ones_set, 1)
            pe.wait_ge(s5_w_ready, 1)
            for part, name in enumerate(("w_r", "w_i")):
                w = tiny[name][:].rearrange("p j a -> p (j a)")
                for half in range(L * PAIRS // P):
                    mm = pe.transpose(bank[7][:, (2 * part + half) * P:(2 * part + half + 1) * P],
                                      w[:, half * P:(half + 1) * P], ident[:])
            mm.then_inc(s5_w_turned, 1)
            norm(0)
            for kind, f, half, s0 in phases:
                t0 = (HALVES * f + half) * KF
                if kind == "in":
                    def tile(t, first, i=0, turn=0):
                        pe.wait_ge(banks_free, t0 + t + 1 + i)
                        for part, out in enumerate((gate_ps[t % 2], up_ps[t % 2])):
                            s = s0 + 2 * t + part
                            pe.wait_ge(slab_lo, split(s) + turn)
                            for k in range(KD):
                                if first and part == 0:
                                    pe.wait_ge(xg_lo_ready, xg_count(NORMS[f], k))
                                mm = product(out[:], s, k, xg_hi[:, k, :], xg_lo[:, k, :], k == 0, k == KD - 1)
                            mm.then_inc(slab_used, 1)

                    with pe.Fori(0, KF // 2) as i:
                        tile(0, True, i * 2, i * RING)
                        tile(1, False, i * 2, i * RING)
                    tile(KF - 1, False)
                elif kind == "out":
                    for d in range(KD):
                        s = s0 + d
                        if d >= 2:
                            if half == HALVES - 1:
                                pe.wait_ge(x_ready, NORMS[f] * KD + d - 1)
                            else:
                                pe.wait_ge(x_half, f * KD + d - 1)
                        pe.wait_ge(slab_lo, split(s))
                        for k in range(KF):
                            if d == 0:
                                pe.wait_ge(hid_lo, t0 + k + 1)
                            mm = product(out_ps[d % 2][:], s, k, h_hi[:, k, :], h_lo[:, k, :], k == 0, k == KF - 1)
                        mm.then_inc(slab_used, 1)
                    if half == HALVES - 1:
                        norm(NORMS[f] + 1)
                elif kind == "mixer1":
                    mixer1(s0)
                elif kind == "mixer0":
                    pe.wait_ge(pool_const, POOL_CONSTS)
                    mixer0(s0)
                elif kind == "mixer0_out":
                    pe.wait_ge(att_lo, NT)
                    pe.wait_ge(mix_lo, BH)
                    for d in range(KD):
                        s = s0 + d
                        if d >= 2:
                            pe.wait_ge(x_ready, NORM_MIX * KD + d - 1)
                        pe.wait_ge(slab_lo, split(s))
                        for k in range(KD):
                            hi, lo = (att_h[:, k, :], att_l[:, k, :]) if k < AT else (rec_h[:, k - AT, :], rec_l[:, k - AT, :])
                            mm = product(out_ps[d % 2][:], s, k, hi, lo, k == 0, k == KD - 1)
                        mm.then_inc(slab_used, 1)
                    norm(NORM_MIX + 1)

        @block.gpsimd
        def _(pool):
            pool.sem_inc(slab_used, RING)
            pool.sem_inc(slab_lo, RING)
            pool.sem_inc(banks_free, 2)
            done = [0]

            def step(ins):
                done[0] += 1
                ins.then_inc(pool_const, 1)
                pool.wait_ge(pool_const, done[0])

            step(pool.memset(ident[:], 0.0))
            step(pool.affine_select(out=ident[:], in_=ident[:], compare_op=ALU.not_equal, fill=1.0, base=0,
                                    pattern=[[-1, P]], channel_multiplier=1))
            step(pool.memset(causal[:], 1.0))
            c3 = causal[:].rearrange("p (c j) -> p c j", j=CH)
            step(pool.affine_select(out=c3, in_=c3, compare_op=ALU.is_ge, fill=0.0, base=0,
                                    pattern=[[CH, CPT], [1, CH]], channel_multiplier=-1))
            step(pool.affine_select(out=c3, in_=c3, compare_op=ALU.is_ge, fill=0.0, base=0,
                                    pattern=[[-CH, CPT], [0, CH]], channel_multiplier=1))
            step(pool.iota(dist[:].bitcast(I32), pattern=[[-1, 2 * P]], base=P, channel_multiplier=1))
            step(pool.tensor_copy(dist[:], dist[:].bitcast(I32)))
            step(pool.affine_select(out=dist[:], in_=dist[:], compare_op=ALU.is_ge, fill=MASKED, base=P,
                                    pattern=[[-1, 2 * P]], channel_multiplier=1))
            step(pool.affine_select(out=dist[:], in_=dist[:], compare_op=ALU.is_ge, fill=MASKED, base=-1,
                                    pattern=[[1, 2 * P]], channel_multiplier=-1))
            assert done[0] == POOL_CONSTS
            step(pool.iota(k_count[:].bitcast(I32), pattern=[[1, L + 1]], base=0, channel_multiplier=0))
            step(pool.tensor_copy(k_count[:], k_count[:].bitcast(I32)))
            assert done[0] == POOL_COUNT
            step(pool.memset(r_sel[:], 0.0))
            step(pool.memset(r_sel[:, (L - 1) * GC:L * GC], 1.0))
            assert done[0] == POOL_ALL

            made = [0]
            loads = [0]
            stores = [0]

            def link(ins):
                made[0] += 1
                ins.then_inc(pool_step, 1)
                pool.wait_ge(pool_step, made[0])

            def fetch(out, src):
                loads[0] += 1
                pool.dma_start(out, src).then_inc(mk_loaded, 16)

            def fetched():
                pool.wait_ge(mk_loaded, 16 * loads[0])

            def store(out, src):
                stores[0] += 1
                pool.dma_start(out, src).then_inc(mk_stored, 16)

            def kept():
                pool.wait_ge(mk_stored, 16 * stores[0])

            tt = pool.tensor_tensor
            pool.wait_ge(s5_w_rows, 1)
            store(dram_w.rearrange("w (h j) (a g) s -> (j a) (w h) (g s)", h=2, g=2), w_rows[:])
            kept()
            for q in range(4):
                gs = slice(q * GQ, (q + 1) * GQ)
                kept()
                for j in range(L):
                    rows = slice(j * GC, (j + 1) * GC)
                    for part, name in enumerate(("wr", "wi")):
                        fetch(mk[name][rows, :], dram_w[part, j, gs, :].rearrange("g s -> (g s)").partition_broadcast(GC))
                    for src, name in ((s5_bt_re, "br"), (s5_bt_im, "bi")):
                        fetch(mk[name][rows, :], src[:, q * GQ * NS:(q + 1) * GQ * NS])
                fetched()
                wr, wi, br, bi, t1, t2 = (mk[n][:] for n in ("wr", "wi", "br", "bi", "t1", "t2"))
                link(tt(t1, wr, br, ALU.mult))
                link(tt(t2, wi, bi, ALU.mult))
                link(tt(t1, t1, t2, ALU.subtract))
                link(tt(t2, wr, bi, ALU.mult))
                link(tt(wr, wi, br, ALU.mult))
                link(tt(t2, t2, wr, ALU.add))
                store(dram_bm[:, 0, gs, :].rearrange("p g s -> p (g s)"), t1)
                store(dram_bm[:, 1, gs, :].rearrange("p g s -> p (g s)"), t2)
            kept()
            fetch(mk["cr"][:], s5_c_re)
            fetch(mk["ci"][:], s5_c_im)
            fetched()
            link(pool.tensor_scalar(mk["ncr"][:], mk["cr"][:], -1.0, None, ALU.mult))
            for q in range(4):
                ps = slice(q * PQ, (q + 1) * PQ)

                def over_k(a):
                    return a[:, ps, :].unsqueeze(2).broadcast_to([P, PQ, L + 1, GC])

                def over_c(a):
                    return a[:, :, ps].rearrange("p k a -> p a k").unsqueeze(3).broadcast_to([P, PQ, L + 1, GC])

                def v(a):
                    return a.rearrange("p a (k c) -> p a k c", c=GC)

                cr, ci, ncr = over_k(mk["cr"][:]), over_k(mk["ci"][:]), over_k(mk["ncr"][:])
                pr, pi = over_c(pow_r[:]), over_c(pow_i[:])
                t1, t2 = v(mk["u1"][:]), v(mk["u2"][:])
                for n in range(PQ):
                    link(tt(t1[:, n], cr[:, n], pr[:, n], ALU.mult))
                    link(tt(t2[:, n], ci[:, n], pi[:, n], ALU.mult))
                kept()
                link(tt(mk_c[:, 0], mk["u1"][:], mk["u2"][:], ALU.subtract))
                for n in range(PQ):
                    link(tt(t1[:, n], ncr[:, n], pi[:, n], ALU.mult))
                    link(tt(t2[:, n], ci[:, n], pr[:, n], ALU.mult))
                link(tt(mk_c[:, 1], mk["u1"][:], mk["u2"][:], ALU.subtract))
                for part in range(2):
                    store(dram_c[:, part, ps, :], mk_c[:, part])
            kept()
            fetch(mk["sr"][:], s5_b_re)
            fetch(mk["si"][:], s5_b_im)
            link(pool.memset(mk_bb[:], 0.0))
            fetched()
            sr, si, t1, t2 = (mk[n][:] for n in ("sr", "si", "s1", "s2"))
            cr = coef[:, 0, :].unsqueeze(2).broadcast_to([P, PAIRS, GC])
            ci = coef[:, 1, :].unsqueeze(2).broadcast_to([P, PAIRS, GC])
            for part, (a, b, op) in enumerate(((sr, si, ALU.subtract), (si, sr, ALU.add))):
                link(tt(t1, cr, a, ALU.mult))
                link(tt(t2, ci, b, ALU.mult))
                for g in range(2):
                    rows = slice(g * NS, (g + 1) * NS)
                    link(tt(mk_bb[rows, :, part, g * GC:(g + 1) * GC], t1[rows], t2[rows], op))
            store(dram_bb, mk_bb[:].rearrange("p a b c -> p (a b c)"))
            link(pool.memset(mk_zero[:], 0.0))
            store(dram_k.rearrange("(t p) c -> p t c", p=P)[:, :, 0:(L - 1) * GC], mk_zero[:])
            kept()
            assert stores[0] == MK_STORES

            pool.wait_ge(hid_lo, 3 * HALVES * KF)
            pool.dma_start(s5_bm[:], dram_bm).then_inc(bm_loaded, 16)
            pool.wait_ge(slab_used, RING + next(s0 for k, _, _, s0 in phases if k == "mixer1"))
            pool.dma_start(s5_c[:], dram_c).then_inc(mats_loaded, 16)
            pool.dma_start(s5_bb[:].rearrange("p a b c -> p (a b c)"), dram_bb).then_inc(mats_loaded, 16)
            for k in range(KD):
                pool.wait_ge(u_tile, k + 1)
                pool.dma_start(dram_u[k * P:(k + 1) * P, :], s5_xg[:, k, :]).then_inc(u_stored, 16)
            du = dram_u.rearrange("(g c) (j t) -> j c g t", c=GC, t=NC)
            pool.wait_ge(u_stored, 16 * KD)
            for j in range(L):
                pool.dma_start(s5_u[j * GC:(j + 1) * GC, :, :], du[j]).then_inc(u_loaded, 16)
            pool.wait_ge(k_diag, KD)
            pool.dma_start(dram_k.rearrange("(t p) c -> p t c", p=P)[:, :, (L - 1) * GC:], s5_k[:])\
                .then_inc(k_stored, 16)
            pool.wait_ge(k_stored, 16)
            pool.wait_ge(st_ready, PAIRS // PPB)
            dk = dram_k.rearrange("(g c) n -> c g n", c=GC)
            for j in range(L):
                pool.dma_start(s5_t[j * GC:(j + 1) * GC, :, :], dk[:, :, (L - 1 - j) * GC:(2 * L - 1 - j) * GC])\
                    .then_inc(t_loaded, 16)
            dy = dram_y.rearrange("(g c) (j t) -> j c g t", c=GC, t=NC)
            n = 2 * PPB
            for q in range(PAIRS // PPB):
                pool.wait_ge(y_taken_a, q + 1)
                pool.wait_ge(y_taken_d, q + 1)
                for j in range(L):
                    pool.dma_start(dy[j][:, q * n:(q + 1) * n, :], s5_y2[j * GC:(j + 1) * GC, q * n:(q + 1) * n, :])\
                        .then_inc(y_stored, 16)
                pool.wait_ge(y_stored, 16 * L * (q + 1))
                pool.dma_start(s5_y[:, 2 * q:2 * q + 2, :],
                               dram_y[2 * q * P:2 * (q + 1) * P, :].rearrange("(k p) t -> p k t", p=P))\
                    .then_inc(y_loaded[q], 16)


def layouts(inputs):
    a = {k: np.asarray(v) for k, v in inputs.items()}
    d = a["x"].shape[2]
    groups, states, gc = a["s5_b_re"].shape[1:]
    pairs, kd = groups // 2, d // P

    def features(v):
        return v.reshape(-1, P).T

    def by_state(v):
        return v[0].reshape(pairs, 2, states).transpose(1, 2, 0).reshape(2 * states, pairs)

    def b_by_state(v):
        return v[0].reshape(pairs, 2, states, gc).transpose(1, 2, 0, 3).reshape(2 * states, pairs, gc)

    def b_by_channel(v):
        return v[0].transpose(2, 0, 1).reshape(gc, groups * states)

    def c_by_state(v):
        return v[0].reshape(pairs, 2, gc, states).transpose(1, 3, 0, 2).reshape(2 * states, pairs, gc)

    return [
        ("x_t", a["x"][0].T), ("norm_g", a["norm_g"].reshape(-1, kd, P).transpose(2, 0, 1)),
        ("ffn_w_in", a["ffn_w_in"]), ("ffn_w_out", a["ffn_w_out"]),
        ("mix_w_in", a["mix_w_in"][0]), ("attn_sinks", a["attn_sinks"]), ("hgrn_lb", features(a["hgrn_lb"])),
        ("mix_w_out", a["mix_w_out"][0]),
        ("s5_a_re", by_state(a["s5_a_re"])), ("s5_a_im", by_state(a["s5_a_im"])),
        ("s5_log_step", a["s5_log_step"].reshape(pairs, 2).T),
        ("s5_b_re", b_by_state(a["s5_b_re"])), ("s5_b_im", b_by_state(a["s5_b_im"])),
        ("s5_bt_re", b_by_channel(a["s5_b_re"])), ("s5_bt_im", b_by_channel(a["s5_b_im"])),
        ("s5_c_re", c_by_state(a["s5_c_re"])), ("s5_c_im", c_by_state(a["s5_c_im"])),
        ("s5_d", features(a["s5_d"])), ("s5_w_glu", a["s5_w_glu"][0]), ("final_g", features(a["final_g"])),
    ]


def kernel(**inputs):
    import concourse.bacc as bacc
    from concourse.bass_utils import run_bass_kernel_spmd

    nc = bacc.Bacc("TRN2", target_bir_lowering=False, num_devices=1)
    arrays, args = {}, []
    for name, v in layouts(inputs):
        v = np.ascontiguousarray(v)
        arrays[name] = v
        args.append(nc.dram_tensor(name, v.shape, mybir.dt.from_np(v.dtype), kind="ExternalInput").ap())
    tokens, d = np.asarray(inputs["x"]).shape[1:]
    args.append(nc.dram_tensor("out_t", (d, tokens), F32, kind="ExternalOutput").ap())
    trunk(nc, *args)
    r = run_bass_kernel_spmd(nc, [arrays], core_ids=[0])
    return np.ascontiguousarray(r.results[0]["out_t"].T)[None]
```

```python
from contextlib import ExitStack

import numpy as np

import concourse.bass as bass
from concourse import mybir

F32 = mybir.dt.float32
F32R = mybir.dt.float32r
I32 = mybir.dt.int32
ACT = mybir.ActivationFunctionType
ALU = mybir.AluOpType
AX = mybir.AxisListType

P = 128
EPS = 1e-6
RING = 4
LEAD = 2
CH = 32
MASKED = 1e30
POOL_CONSTS = 9
POOL_COUNT = 2
POOL_ALL = POOL_CONSTS + 2
S5_SMALL = (1, 0)
S5_KERNELS = (2, 0)
S5_SINES = (2, 1)
MK_STORES = 19
TWO_PI = 6.283185307179586
TWO_PI_PARTS = (6.28125, 0.001934051513671875, 1.2556659146e-06)
ROUND = 12582912.0
ROUND_10 = 12288.0
PI_BELOW = 3.1415925


def trunk(nc, x_t, norm_g, ffn_w_in, ffn_w_out, mix_w_in, attn_sinks, hgrn_lb, mix_w_out, s5_a_re, s5_a_im,
          s5_log_step, s5_b_re, s5_b_im, s5_bt_re, s5_bt_im, s5_c_re, s5_c_im, s5_d, s5_w_glu, final_g, out_t):
    D, T = x_t.shape
    F = ffn_w_out.shape[2]
    KD = D // P
    NT = T // P
    HALVES = 2
    KF = F // P // HALVES
    SLAB_IN, SLAB_OUT = KD * P, KF * P
    SLAB = max(SLAB_IN, SLAB_OUT)
    HEADS = attn_sinks.shape[1]
    AD = 64
    AT = HEADS * AD // P
    BH = hgrn_lb.shape[1]
    KV_W = 2 * AD
    COL_K, COL_V = HEADS * AD, HEADS * AD + KV_W
    COL_BQ = HEADS * AD + 2 * KV_W
    COL_BF, COL_BI, COL_BG = COL_BQ + BH * P, COL_BQ + 2 * BH * P, COL_BQ + 3 * BH * P
    NCH = T // CH
    CPT = P // CH
    NORMS = [0, 2, 3, 5]
    NORM_MIX, NORM_S5, NORM_FIN = 1, 4, 6
    SPLIT_NORMS = [0, 1, 2, 3, 5]

    PAIRS = s5_a_re.shape[1]
    NS = P // 2
    GC = s5_bt_re.shape[0]
    G = 2 * PAIRS
    L = P // GC
    NC = T // L
    PPB = 512 // NC
    PER = PAIRS // KD

    KIB = 1024
    o_x = 16640
    o_xg = o_x + KD * T * 4
    o_h = o_xg + 2 * KD * T * 4
    o_ring = o_h + 2 * KF * T * 4
    o_norm = o_ring + 3 * RING * SLAB * 4
    o_const = o_norm + 4 * T * 4
    o_tmp = o_const + 7808
    o_free = o_tmp + 4 * T * 4
    o_end = 229368

    with ExitStack() as ctx:
        def at(name, shape, offset, dt=F32):
            n = 4
            for d in shape[1:]:
                n *= d
            assert offset + n <= o_end, (name, offset + n)
            return nc.alloc_sbuf_tensor_at(name, shape, dt, offset=offset), offset + -(-n // 32) * 32

        def sem(name):
            return ctx.enter_context(nc.semaphore(name))

        x, _ = at("x", [P, KD, T], o_x)
        xg_hi, o = at("xg_hi", [P, KD, T], o_xg, F32R)
        xg_lo, _ = at("xg_lo", [P, KD, T], o, F32R)
        h_hi, o = at("h_hi", [P, KF, T], o_h, F32R)
        h_lo, _ = at("h_lo", [P, KF, T], o, F32R)
        raw, o = at("raw", [P, RING, SLAB], o_ring)
        w_hi, o = at("w_hi", [P, RING, SLAB], o, F32R)
        w_lo, _ = at("w_lo", [P, RING, SLAB], o, F32R)
        gate_r, o = at("gate_r", [P, T], o_tmp)
        silu_g, o = at("silu_g", [P, T], o)
        up_s, o = at("up_s", [P, T], o)
        hid, _ = at("hid", [P, T], o)
        sq, o = at("sq", [P, T], o_norm)
        ssq, o = at("ssq", [P, T], o)
        rms, o = at("rms", [P, T], o)
        rinv, _ = at("rinv", [P, T], o)
        ones, o = at("ones", [P, P], o_const)
        ident, o = at("ident", [P, P], o)
        causal, o = at("causal", [P, P], o)
        dist, o = at("dist", [P, 2 * P], o)
        dist_i, _ = at("dist_i", [P, 2 * P], o_tmp, I32)
        g_all, o = at("g_all", [P, 7, KD], o)
        sink, o = at("sink", [P, HEADS], o)
        sink_neg, o = at("sink_neg", [P, HEADS], o)
        lb_in, o = at("lb_in", [P, BH], o)
        lb, o = at("lb", [P, BH], o)
        lb_c, o = at("lb_c", [P, BH], o)
        r_col, o = at("r_col", [P, NT], o)
        max_neg, o = at("max_neg", [P, 2, 2], o)
        sink_d, o = at("sink_d", [P, 2, 2], o)
        sink_e, o = at("sink_e", [P, 2, 2], o)
        rowsum, o = at("rowsum", [P, 2, 2], o)
        den, o = at("den", [P, 2, 2], o)
        rden, o = at("rden", [P, 2, 2], o)
        decay, o = at("decay", [P, BH, NCH], o)
        pow_r, o = at("pow_r", [P, L + 1, PAIRS], o)
        pow_i, o = at("pow_i", [P, L + 1, PAIRS], o)
        theta, o = at("theta", [P, PAIRS], o)
        rho, o = at("rho", [P, PAIRS], o)
        coef, o = at("coef", [P, 2, PAIRS], o)
        d_col, o = at("d_col", [P, KD], o)
        diag, o = at("diag", [P, GC], o)
        r_sel, o = at("r_sel", [1, (2 * L - 1) * GC], o)
        r_row, o = at("r_row", [P, NC], o)
        assert o <= o_tmp, o - o_const
        b_k, o = at("b_k", [P, BH, T], o_h)
        b_cum, o = at("b_cum", [P, BH, T], o)
        b_q, o = at("b_q", [P, BH, T], o)
        b_e, o = at("b_e", [P, BH, T], o)
        b_g, o = at("b_g", [P, BH, T], o)
        states, _ = at("states", [P, NCH, P], o_h + BH * T * 4)
        a_q, _ = at("a_q", [P, AT, T], o_h + 3 * BH * T * 4)
        b_kinv, o = at("b_kinv", [P, BH, T], o_free)
        b_o, _ = at("b_o", [P, BH, T], o_free)
        b_v, o = at("b_v", [P, NT, BH * P], o)
        a_k, _ = at("a_k", [P, T], o_norm)
        a_v, o = at("a_v", [P, NT, KV_W], o)
        k_end, o = at("k_end", [P, 2, NT, P], o)
        scores, o = at("scores", [P, 2, NT, P], o)
        prob, _ = at("prob", [P, 2, 2, 2 * P], o_tmp)
        prob_t, _ = at("prob_t", [P, 2, 2, 2, P], o_tmp + 2 * T * 4)
        b_tmp, _ = at("b_tmp", [P, 2, T], o_tmp)
        att_h, _ = at("att_h", [P, AT, T], o_h, F32R)
        rec_h, _ = at("rec_h", [P, BH, T], o_h + BH * T * 4, F32R)
        rec_l, _ = at("rec_l", [P, BH, T], o_h + 2 * BH * T * 4, F32R)
        att_l, _ = at("att_l", [P, AT, T], o_free + BH * T * 4, F32R)
        squares, _ = at("squares", [P, BH, T], o_tmp)
        rec, _ = at("rec", [P, 2, T], o_tmp + 2 * T * 4)

        QUARTERS = 4
        GQ = G // QUARTERS
        PQ = PAIRS // QUARTERS
        o = o_free
        tiny = {}
        for name in ["lam_r", "lam_i", "log_dt", "den_l", "num_a", "num_b", "abr1"]:
            tiny[name], o = at("s5_" + name, [P, PAIRS], o)
        for name in ["angle", "turns", "angle_c", "fold", "mag"]:
            tiny[name], o = at("s5_" + name, [P, L + 1, PAIRS], o)
        k_count, o = at("k_count", [P, L + 1], o)
        for name in ["w_r", "w_i", "w_t"]:
            tiny[name], o = at("s5_" + name, [P, L, PAIRS], o)
        w_rows, _ = at("w_rows", [P, 4, P], o)
        o = o_free
        mk = {}
        mk_w, o = at("mk_w", [P, 2, GQ * NS], o)
        for name in ["br", "bi", "t1", "t2"]:
            mk[name], o = at("mk_" + name, [P, GQ * NS], o)
        o = o_free
        mk_c, o = at("mk_c", [P, 2, PQ, (L + 1) * GC], o)
        for name in ["cr", "ci", "ncr"]:
            mk[name], o = at("mk_" + name, [P, PAIRS, GC], o)
        for name in ["u1", "u2"]:
            mk[name], o = at("mk_" + name, [P, PQ, (L + 1) * GC], o)
        mk_bb, _ = at("mk_bb", [P, PAIRS, 2, 2 * GC], o_free + 12 * KIB)
        mk["sr"], o = at("mk_sr", [P, PAIRS, GC], o_free)
        mk["si"], o = at("mk_si", [P, PAIRS, GC], o)
        mk["s1"], o = at("mk_s1", [P, PAIRS, GC], o)
        mk["s2"], o = at("mk_s2", [P, PAIRS, GC], o)
        mk_zero, _ = at("mk_zero", [P, KD, (L - 1) * GC], o_free + 20 * KIB)
        s5_bb, o = at("s5_bb", [P, PAIRS, 2, 2 * GC], o_free)
        s5_cq, o = at("s5_cq", [P, 2, 2, PQ, L * GC], o)
        s5_k, _ = at("s5_k", [P, 2, KD // QUARTERS, L * GC], o)
        o = o_free
        turn_s, o = at("turn_s", [P, PAIRS, NC], o)
        turn_c, o = at("turn_c", [P, PAIRS, NC], o)
        turn_t, o = at("turn_t", [P, PAIRS, NC], o)
        c_count, o = at("c_count", [P, NC], o)
        theta_hi, o = at("theta_hi", [P, PAIRS], o)
        theta_lo, o = at("theta_lo", [P, PAIRS], o)
        s5_bm, _ = at("s5_bm", [P, G, 2, NS], o_tmp)
        s5_c, _ = at("s5_c", [P, PAIRS, 2, L * GC], o_tmp)
        s5_t, o = at("s5_t", [P, G, P], o_h)
        rot = []
        for name in "abc":
            r, o = at("rot_" + name, [P, 2, PPB * NC], o)
            rot.append(r)
        assert o <= o_ring
        y_hi, o = at("y_hi", [P, KD, T], o_h, F32R)
        y_lo, o = at("y_lo", [P, KD, T], o, F32R)
        sig, o = at("sig", [P, 2, T], o)
        glu, o = at("glu", [P, 2, T], o)
        assert o <= o_ring
        s5_xg, _ = at("s5_xg", [P, KD, T], o_xg)
        s5_y, _ = at("s5_y", [P, KD, L, PER * GC], o_xg)
        s5_u, _ = at("s5_u", [P, G, NC], o_xg + KD * T * 4)
        sines, o = at("sines", [P, 2, PAIRS, NC], o_ring)
        decays, o = at("decays", [P, 2, PPB, NC], o)
        assert o <= o_ring + RING * SLAB * 4
        s5_x, o = at("s5_x", [P, 2, PAIRS, NC], o_ring + 2 * RING * SLAB * 4)
        assert o <= o_norm

        def dram(name, *shape):
            return nc.dram_tensor(name, shape, F32).ap()

        dram_w = dram("dram_w", 2, L, G, NS)
        dram_bm = dram("dram_bm", P, G, 2, NS)
        dram_c = dram("dram_c", P, 2, PAIRS, (L + 1) * GC)
        dram_bb = dram("dram_bb", P, PAIRS * 2 * 2 * GC)
        dram_k = dram("dram_k", D, (2 * L - 1) * GC)
        dram_u = dram("dram_u", D, T)
        dram_sines = dram("dram_sines", P, 2, PAIRS * NC)

        bank = [ctx.enter_context(nc.psum_tensor(f"bank{i}", [P, 512], F32)) for i in range(8)]
        gate_ps, up_ps, out_ps, norm_ps = bank[0:2], bank[2:4], bank[4:6], bank[6]

        const_loaded = sem("const_loaded")
        s5_count = sem("s5_count")
        small_loaded = sem("small_loaded")
        x_loaded = [sem(f"x_loaded{k}") for k in range(KD)]
        ones_set = sem("ones_set")
        pool_const = sem("pool_const")
        slab_loaded = [sem(f"slab_loaded{i}") for i in range(RING)]
        slab_hi = sem("slab_hi")
        slab_lo = sem("slab_lo")
        slab_used = sem("slab_used")
        gate_scaled = sem("gate_scaled")
        silu_ready = sem("silu_ready")
        banks_free = sem("banks_free")
        hid_ready = sem("hid_ready")
        hid_hi = sem("hid_hi")
        hid_lo = sem("hid_lo")
        x_half = sem("x_half")
        x_ready = sem("x_ready")
        xg_hi_ready = sem("xg_hi_ready")
        xg_lo_ready = sem("xg_lo_ready")
        sq_ready = sem("sq_ready")
        ssq_ready = sem("ssq_ready")
        norm_sum = sem("norm_sum")
        mean_ready = sem("mean_ready")
        rms_ready = sem("rms_ready")
        rinv_ready = sem("rinv_ready")
        stored = sem("stored")
        fin_ready = sem("fin_ready")
        dve_step = sem("dve_step")
        act_step = sem("act_step")
        lb_exp = sem("lb_exp")
        col_ready = sem("col_ready")
        col_taken = sem("col_taken")
        proj_scaled = sem("proj_scaled")
        proj_free = sem("proj_free")
        nat_taken = sem("nat_taken")
        sig_ready = sem("sig_ready")
        sig_used = sem("sig_used")
        f_one = sem("f_one")
        f_ready = sem("f_ready")
        logf_ready = sem("logf_ready")
        cum_ready = sem("cum_ready")
        exp_ready = sem("exp_ready")
        exp_used = sem("exp_used")
        b_ready = sem("b_ready")
        sc_ready = sem("sc_ready")
        sc_masked = sem("sc_masked")
        kt_ready = sem("kt_ready")
        kt_taken = sem("kt_taken")
        kv_ready = sem("kv_ready")
        state_ready = sem("state_ready")
        inter_done = sem("inter_done")
        o_taken = sem("o_taken")
        o_sq = sem("o_sq")
        o_sum = sem("o_sum")
        o_mean = sem("o_mean")
        o_rms = sem("o_rms")
        o_rinv = sem("o_rinv")
        o_bcast = sem("o_bcast")
        rec_ready = sem("rec_ready")
        mix_hi = sem("mix_hi")
        mix_lo = sem("mix_lo")
        s_ready = sem("s_ready")
        s_taken = sem("s_taken")
        m_ready = sem("m_ready")
        p_exp = sem("p_exp")
        p_ready = sem("p_ready")
        pt_ready = sem("pt_ready")
        pt_taken = sem("pt_taken")
        pv_done = sem("pv_done")
        att_hi = sem("att_hi")
        att_lo = sem("att_lo")

        s5_loaded = sem("s5_loaded")
        d_loaded = sem("d_loaded")
        s5_dt = sem("s5_dt")
        s5_angles = sem("s5_angles")
        s5_trig = sem("s5_trig")
        s5_w_ready = sem("s5_w_ready")
        s5_w_turned = sem("s5_w_turned")
        s5_w_rows = sem("s5_w_rows")
        s5_w_stored = sem("s5_w_stored")
        mk_loaded = sem("mk_loaded")
        mk_stored = sem("mk_stored")
        pool_step = sem("pool_step")
        bb_loaded = sem("bb_loaded")
        cq_loaded = [sem(f"cq_loaded{i}") for i in range(2)]
        c_loaded = [sem(f"c_loaded{q}") for q in range(QUARTERS)]
        turns_ready = sem("turns_ready")
        sines_ready = sem("sines_ready")
        sines_loaded = sem("sines_loaded")
        decays_ready = sem("decays_ready")
        k_summed = sem("k_summed")
        k_ready = sem("k_ready")
        k_diag = sem("k_diag")
        k_stored = sem("k_stored")
        bm_loaded = [sem(f"bm_loaded{i}") for i in range(2)]
        t_loaded = sem("t_loaded")
        u_tile = sem("u_tile")
        u_stored = sem("u_stored")
        u_loaded = [sem(f"u_loaded{q}") for q in range(PAIRS // PPB)]
        row_ready = sem("row_ready")
        row_taken = sem("row_taken")
        u_ready = sem("u_ready")
        st_ready = sem("st_ready")
        st_taken = sem("st_taken")
        scanned = sem("scanned")
        x_scanned = sem("x_scanned")
        y_ready = sem("y_ready")
        y_taken_a = sem("y_taken_a")
        y_taken_d = sem("y_taken_d")
        yt_ready = sem("yt_ready")
        gelu_ready = sem("gelu_ready")
        y_hi_ready = sem("y_hi_ready")
        y_lo_ready = sem("y_lo_ready")
        glu_sig = sem("glu_sig")
        glu_mul = sem("glu_mul")

        phases = []
        sizes = []

        def phase(kind, f=0, half=0, count=0, size=0):
            phases.append((kind, f, half, len(sizes)))
            sizes.extend([size] * count)

        def swiglu(f):
            for half in range(HALVES):
                phase("in", f, half, 2 * KF, SLAB_IN)
                phase("out", f, half, KD, SLAB_OUT)

        MIX_COLS = [COL_BF + i * P for i in range(BH)] + [COL_BQ + i * P for i in range(BH)] \
            + [COL_BG + i * P for i in range(BH)] + [COL_BI + i * P for i in range(BH)]
        swiglu(0)
        phase("mixer0", count=len(MIX_COLS) + AT + 2, size=SLAB_IN)
        phase("mixer0_out", count=KD, size=KD * P)
        swiglu(1)
        swiglu(2)
        phase("mixer1", count=2 * KD, size=SLAB_IN)
        swiglu(3)
        total = len(sizes)

        w_in = [ffn_w_in[f // 2, f % 2].rearrange("(k p) c -> p k c", p=P) for f in range(4)]
        w_out = [ffn_w_out[f // 2, f % 2].rearrange("(k p) c -> p k c", p=P) for f in range(4)]
        w_glu = s5_w_glu.rearrange("(k p) c -> p k c", p=P)
        w_mix = mix_w_in.rearrange("(k p) c -> p k c", p=P)
        w_mix_out = mix_w_out.rearrange("(k p) c -> p k c", p=P)

        late = [s0 + i for kind, _, _, s0 in phases if kind == "mixer1" for i in range(LEAD)]

        def group(pair, g):
            return 2 * PER * (pair // PER) + PER * g + pair % PER

        def y_bank(k):
            return bank[k // 2 + QUARTERS * (k % 2)]

        def slot(s):
            return s % RING

        def arrived(s, per=1):
            return 16 * (s // RING + 1)

        def split(s):
            return RING + s + 1

        def used(s):
            return RING + s + 1

        def xg_count(n, k):
            return SPLIT_NORMS.index(n) * KD + k + 1

        UNITS = [(n, tp, g) for n in range(NT) for tp in range(AT // 2) for g in range(2)]
        SLOPES = [2.0 ** (-8.0 * (h + 1) / HEADS) for h in range(HEADS)]

        def taken(v):
            return sum(2 if n else 1 for n, _, _ in UNITS[:v + 1])

        block = ctx.enter_context(nc.Block())

        @block.sync
        def _(sp):
            def load(s, src, n, turn=0):
                sp.wait_ge(slab_lo, s + 1 + turn)
                sp.dma_start(raw[:, slot(s), 0:n * P].rearrange("p (k c) -> p k c", c=P), src)\
                  .then_inc(slab_loaded[slot(s)], 16)

            for kind, f, half, s0 in phases:
                if kind == "in":
                    def tile(t, i=0):
                        for part in range(2):
                            c = part * F + (half * KF + t) * P
                            load(s0 + 2 * t + part, w_in[f][:, :, bass.ds(c + i * 2 * P, P)], KD, i * RING)

                    tile(0)
                    with sp.Fori(0, KF // 2) as i:
                        tile(1, i)
                        tile(2, i)
                elif kind == "out":
                    with sp.Fori(0, KD // RING) as i:
                        for d in range(RING):
                            load(s0 + d, w_out[f][:, half * KF:(half + 1) * KF, bass.ds(d * P + i * RING * P, P)],
                                 KF, i * RING)
                elif kind == "mixer0":
                    for n, c in enumerate(MIX_COLS):
                        load(s0 + n, w_mix[:, :, c:c + P], KD)
                    s = s0 + len(MIX_COLS)
                    for t in range(AT):
                        sp.wait_ge(slab_lo, s + t + 1)
                        for g in range(2):
                            c = (t + g * AT) * AD
                            sp.dma_start(raw[:, slot(s + t), 0:SLAB_IN].rearrange("p (k c) -> p k c", c=P)
                                         [:, :, g * AD:(g + 1) * AD], w_mix[:, :, c:c + AD])\
                              .then_inc(slab_loaded[slot(s + t)], 8 * 2 if g else 16)
                    load(s + AT, w_mix[:, :, COL_K:COL_K + P], KD)
                    load(s + AT + 1, w_mix[:, :, COL_V:COL_V + P], KD)
                elif kind == "mixer0_out":
                    for d in range(KD):
                        s = s0 + d
                        sp.wait_ge(slab_lo, s + 1)
                        dst = raw[:, slot(s), 0:SLAB_IN].rearrange("p (k c) -> p k c", c=P)
                        for g in range(2):
                            sp.dma_start(dst[g * AD:(g + 1) * AD, 0:AT, :],
                                         mix_w_out[g * AT * AD:(g + 1) * AT * AD, d * P:(d + 1) * P]
                                         .rearrange("(t r) c -> r t c", r=AD)).then_inc(slab_loaded[slot(s)], 16)
                        sp.dma_start(dst[:, AT:KD, :], w_mix_out[:, AT:KD, d * P:(d + 1) * P])\
                          .then_inc(slab_loaded[slot(s)], 16)
                elif kind == "mixer1":
                    def glu_slab(n):
                        c = (n % 2) * D + n // 2 * P
                        load(s0 + n, w_glu[:, :, c:c + P], KD)

                    du = dram_u.rearrange("(g c) (j t) -> j c g t", c=GC, t=NC)
                    gq = 2 * PPB
                    for k in range(KD):
                        sp.wait_ge(u_tile, k + 1)
                        sp.dma_start(dram_u[k * P:(k + 1) * P, :], s5_xg[:, k, :]).then_inc(u_stored, 16)
                        if k % 2 == 1:
                            q = k // 2
                            sp.wait_ge(u_stored, 16 * (k + 1))
                            for j in range(L):
                                sp.dma_start(s5_u[j * GC:(j + 1) * GC, q * gq:(q + 1) * gq, :],
                                             du[j][:, q * gq:(q + 1) * gq, :]).then_inc(u_loaded[q], 16)
                    for q in range(QUARTERS):
                        sp.wait_ge(st_ready, q + 1)
                        for part in range(2):
                            sp.dma_start(s5_c[:, q * PQ:(q + 1) * PQ, part, :],
                                         dram_c[:, part, q * PQ:(q + 1) * PQ, GC:]).then_inc(c_loaded[q], 16)
                    sp.wait_ge(scanned, 2 * QUARTERS)
                    for n in range(2 * KD):
                        glu_slab(n)
            for k in range(KD):
                sp.wait_ge(fin_ready, k + 1)
                sp.dma_start(out_t[k * P:(k + 1) * P, :], x[:, k, :]).then_inc(stored, 16)
            sp.wait_ge(stored, 16 * KD)

        parts = [1] * total
        for kind, f, half, s0 in phases:
            if kind == "mixer0":
                for t in range(AT):
                    parts[s0 + len(MIX_COLS) + t] = 2
            if kind == "mixer0_out":
                for d in range(KD):
                    parts[s0 + d] = 3

        def in_ring(s):
            return 16 * sum(parts[slot(s):s + 1:RING])

        @block.scalar
        def _(act):
            steps = [0]

            def split_hi(s, n, i=0):
                act.wait_ge(slab_loaded[slot(s)], in_ring(s) + i * 16)
                act.wait_ge(slab_used, s + 1 + i * RING)
                act.activation(w_hi[:, slot(s), 0:n], raw[:, slot(s), 0:n], ACT.Copy).then_inc(slab_hi, 1)

            def split_ahead(s, count):
                for q in range(s + LEAD, min(s + LEAD + count, total)):
                    if q not in late:
                        split_hi(q, sizes[q])

            def norm_tile(n, k):
                if n:
                    act.wait_ge(x_ready, (n - 1) * KD + k + 1)
                if n == NORM_S5:
                    act.activation(s5_xg[:, k, :].rearrange("p (j c) -> p j c", j=L),
                                   x[:, k, :].rearrange("p (c j) -> p j c", j=L), ACT.Copy,
                                   scale=g_all[:, n, k:k + 1]).then_inc(u_tile, 1)
                if n in SPLIT_NORMS:
                    act.activation(xg_hi[:, k, :], x[:, k, :], ACT.Copy, scale=g_all[:, n, k:k + 1])\
                       .then_inc(xg_hi_ready, 1)
                if n * KD + k:
                    act.wait_ge(ssq_ready, n * KD + k)
                act.activation(sq[:], x[:, k, :], ACT.Square).then_inc(sq_ready, 1)

            def norm_root(n):
                if n == NORM_S5:
                    act.wait_ge(row_ready, 1)
                    act.activation(r_row[:], bank[7][:, 0:NC], ACT.Sqrt).then_inc(rms_ready, 1)
                    return
                act.wait_ge(mean_ready, n + 1)
                act.activation(rms[:], rms[:], ACT.Sqrt).then_inc(rms_ready, 1)

            def hidden(t, hi, i=0):
                act.wait_ge(gate_scaled, t + 1 + i)
                act.activation(silu_g[:], gate_r[:], ACT.Silu).then_inc(silu_ready, 1)
                act.wait_ge(hid_ready, t + 1 + i)
                act.activation(hi, hid[:], ACT.Copy).then_inc(hid_hi, 1)

            def mixer0(s0):
                for n in range(3 * BH):
                    split_ahead(s0 + n, 1)
                    act.wait_ge(proj_scaled, n + 1)
                    src = (b_e, b_q, b_g)[n // BH][:, n % BH, :]
                    dst = b_k[:, n % BH, :] if n < BH else b_tmp[:, n % 2, :]
                    if n >= BH + 2:
                        act.wait_ge(sig_used, n - BH - 1)
                    act.activation(dst, src, ACT.Sigmoid).then_inc(sig_ready, 1)
                act.wait_ge(f_ready, 1)
                act.activation(b_cum[:], b_k[:], ACT.Ln).then_inc(logf_ready, 1)
                s = s0 + 3 * BH
                for pair in range(BH // 2):
                    split_ahead(s + 2 * pair, 2)
                    act.wait_ge(slab_used, used(s + 2 * pair + 1))
                    for m in range(NT):
                        src = bank[2 * pair + m // 2][:, (m % 2) * 2 * P:(m % 2 + 1) * 2 * P]
                        act.activation(b_v[:, m, 2 * pair * P:2 * (pair + 1) * P], src, ACT.Copy,
                                       scale=r_col[:, m:m + 1]).then_inc(nat_taken, 1)
                    if pair == 0:
                        act.wait_ge(cum_ready, 1)
                        act.wait_ge(f_ready, 2)
                        act.activation(b_e[:], b_cum[:], ACT.Exp).then_inc(exp_ready, 1)
                        act.wait_ge(exp_used, 1)
                        act.activation(b_e[:], b_cum[:], ACT.Exp, scale=-1.0).then_inc(exp_ready, 1)
                    else:
                        act.wait_ge(cum_ready, 2)
                        act.activation(b_cum[:], b_cum[:], ACT.Exp).then_inc(exp_ready, 1)
                s = s0 + 4 * BH
                for n in range(AT + 2):
                    split_ahead(s + n, 1)
                act.wait_ge(slab_used, used(s + AT + 1))
                act.activation(a_v[:, 0, :], bank[1][:, 0:P], ACT.Copy, scale=r_col[:, 0:1]).then_inc(nat_taken, 1)
                for m in range(1, NT):
                    act.activation(a_v[:, m, :], bank[1][:, m * P:(m + 1) * P], ACT.Copy,
                                   scale=r_col[:, m:m + 1]).then_inc(nat_taken, 1)
                for h in range(BH):
                    act.wait_ge(kt_ready, h + 1)
                    if h >= 2:
                        act.wait_ge(kv_ready, h - 1)
                    act.activation(k_end[:, h % 2, :, :], bank[1][:].rearrange("p (m d) -> p m d", d=P), ACT.Copy)\
                       .then_inc(kt_taken, 1)
                    if h >= 1:
                        o_out(h - 1)
                o_out(BH - 1)
                act.wait_ge(o_mean, 1)
                act.activation(rms[:], rms[:], ACT.Sqrt).then_inc(o_rms, 1)
                for h in range(BH):
                    act.wait_ge(rec_ready, h + 1)
                    act.activation(rec_h[:, h, :], rec[:, h % 2, :], ACT.Copy).then_inc(mix_hi, 1)
                for u in range(len(UNITS) + 2):
                    if u < len(UNITS):
                        n, tp, g = UNITS[u]
                        k0 = 0 if n else P
                        act.wait_ge(m_ready, u + 1)
                        for j in range(2):
                            act.activation(prob[:, u % 2, j, k0:], prob[:, u % 2, j, k0:], ACT.Exp,
                                           bias=max_neg[:, u % 2, j:j + 1], accum_out=rowsum[:, u % 2, j:j + 1])\
                               .then_inc(p_exp, 1)
                        act.activation(sink_e[:, u % 2, :], sink_d[:, u % 2, :], ACT.Exp).then_inc(p_exp, 1)
                    if 1 <= u <= len(UNITS):
                        v = u - 1
                        n = UNITS[v][0]
                        act.wait_ge(pt_ready, v + 1)
                        if v >= 2:
                            act.wait_ge(pv_done, v - 1)
                        for kt in range(0 if n else 1, 2):
                            act.activation(prob_t[:, v % 2, :, kt, :],
                                           bank[2 + v % 2][:].rearrange("p (j k q) -> p j k q", j=2, k=2)[:, :, kt, :],
                                           ACT.Copy).then_inc(pt_taken, 1)
                    if u >= 2 and (u - 2) % 4 == 3:
                        n = (u - 2) // 4
                        act.wait_ge(pv_done, 4 * (n + 1))
                        act.activation(att_h[:, :, n * P:(n + 1) * P],
                                       bank[4 + n % 2][:].rearrange("p (t q) -> p t q", q=P), ACT.Copy).then_inc(att_hi, 1)

            def mixer1(s0):
                for q in range(QUARTERS):
                    if q == 0:
                        act.wait_ge(decays_ready, 1)
                    if q >= 2:
                        act.wait_ge(x_scanned, q - 1)
                    act.activation(decays[:, q % 2, :, 1:], rho[:, q * PQ:(q + 1) * PQ].unsqueeze(2)
                                   .broadcast_to([P, PQ, NC - 1]), ACT.Copy).then_inc(decays_ready, 1)

                def y_half(q):
                    act.wait_ge(y_ready, 2 * q + 1)
                    act.activation(s5_y[:, 2 * q, :, :].rearrange("p j (a c) -> p a j c", c=GC),
                                   y_bank(2 * q)[:].rearrange("p (a j c) -> p a j c", j=L, c=GC), ACT.Copy)\
                       .then_inc(y_taken_a, 1)

                def y_gelu(k):
                    act.wait_ge(yt_ready, k + 1)
                    if k >= 2:
                        act.wait_ge(y_lo_ready, k - 1)
                    gelu = (sq, ssq)[k % 2]
                    act.activation(gelu[:], y_bank(k)[:], ACT.Gelu_apprx_tanh).then_inc(gelu_ready, 1)
                    act.wait_ge(gelu_ready, k + 1)
                    act.activation(y_hi[:, k, :], gelu[:], ACT.Copy).then_inc(y_hi_ready, 1)

                y_half(0)
                for q in range(1, QUARTERS):
                    y_half(q)
                    y_gelu(2 * q - 2)
                    y_gelu(2 * q - 1)
                for s in late:
                    split_hi(s, sizes[s])
                y_gelu(KD - 2)
                y_gelu(KD - 1)
                for d in range(KD):
                    split_ahead(s0 + 2 * d, 2)
                    act.wait_ge(slab_used, used(s0 + 2 * d + 1))
                    if d >= 2:
                        act.wait_ge(glu_mul, d - 1)
                    act.activation(sig[:, d % 2, :], up_ps[d % 2][:], ACT.Sigmoid).then_inc(glu_sig, 1)
                    if d:
                        norm_tile(NORM_S5 + 1, d - 1)
                norm_tile(NORM_S5 + 1, KD - 1)
                norm_root(NORM_S5 + 1)

            def s5_part(d):
                if d == 0:
                    act.wait_ge(s5_loaded, 16 * 4)
                    act.activation(tiny["log_dt"][:], tiny["log_dt"][:], ACT.Exp).then_inc(s5_dt, 1)
                if d == 2:
                    act.wait_ge(s5_angles, 1)
                    act.activation(tiny["mag"][:], tiny["mag"][:], ACT.Exp).then_inc(s5_trig, 1)
                    act.activation(tiny["angle"][:], tiny["angle"][:], ACT.Sin).then_inc(s5_trig, 1)
                    act.activation(tiny["angle_c"][:], tiny["angle_c"][:], ACT.Sin).then_inc(s5_trig, 1)
                if d == KD - 1:
                    act.wait_ge(s5_w_turned, 1)
                    act.activation(w_rows[:], bank[7][:].rearrange("p (a c) -> p a c", c=P), ACT.Copy)\
                       .then_inc(s5_w_rows, 1)

            def k_out(q):
                act.wait_ge(k_summed, q + 1)
                if q >= 2:
                    act.wait_ge(k_stored, 16 * (q - 1))
                act.activation(s5_k[:, q % 2, :, :],
                               bank[7][:, 0:KD // QUARTERS * P].rearrange("p (t c) -> p t c", c=P), ACT.Copy)\
                   .then_inc(k_ready, 1)

            def o_out(h):
                act.wait_ge(inter_done, h + 1)
                act.activation(b_o[:, h, :], bank[2 + h % 2][:], ACT.Copy).then_inc(o_taken, 1)
                act.activation(squares[:, h, :], bank[2 + h % 2][:], ACT.Square).then_inc(o_sq, 1)

            act.dma_start(g_all[:, 0:6, :], norm_g).then_inc(const_loaded, 16)
            act.dma_start(g_all[:, 6, :], final_g).then_inc(const_loaded, 16)
            for k in range(KD):
                act.dma_start(x[:, k, :], x_t[k * P:(k + 1) * P, :]).then_inc(x_loaded[k], 16)
            act.dma_start(d_col[:], s5_d).then_inc(d_loaded, 16)
            act.dma_start(sink[:], attn_sinks[0].partition_broadcast(P)).then_inc(small_loaded, 16)
            act.dma_start(lb_in[:], hgrn_lb).then_inc(small_loaded, 16)
            split_hi(0, sizes[0])
            act.wait_ge(const_loaded, 32)
            for k in range(KD):
                act.wait_ge(x_loaded[k], 16)
                norm_tile(0, k)
            split_hi(1, sizes[1])
            norm_root(0)
            for kind, f, half, s0 in phases:
                if kind == "in":
                    t0 = (HALVES * f + half) * KF
                    split_ahead(s0, 2)
                    hidden(t0, h_hi[:, 0, :])
                    with act.Fori(0, KF // 2 - 1) as i:
                        for t in (1, 2):
                            for part in range(2):
                                split_hi(s0 + 2 * t + part + LEAD, SLAB_IN, i)
                            hidden(t0 + t, h_hi[:, bass.ds(i * 2 + t, 1), :].squeeze(1), i * 2)
                    for t in (KF - 2, KF - 1):
                        split_ahead(s0 + 2 * t, 2)
                        hidden(t0 + t, h_hi[:, t, :])
                elif kind == "out":
                    for d in range(KD):
                        split_ahead(s0 + d, 1)
                        if (f, half) == S5_SMALL:
                            s5_part(d)
                        if (f, half) == S5_KERNELS and d % 2 == 1:
                            k_out(d // 2)
                        if (f, half) == S5_SINES and d == 2:
                            act.wait_ge(turns_ready, 1)
                            act.activation(turn_s[:], turn_s[:], ACT.Sin).then_inc(sines_ready, 1)
                            act.activation(turn_c[:], turn_c[:], ACT.Sin).then_inc(sines_ready, 1)
                        if half == HALVES - 1:
                            norm_tile(NORMS[f] + 1, d)
                    if half == HALVES - 1:
                        norm_root(NORMS[f] + 1)
                elif kind == "mixer1":
                    mixer1(s0)
                elif kind == "mixer0":
                    act.wait_ge(lb_exp, 1)
                    act.activation(lb[:], lb_c[:], ACT.Exp).then_inc(act_step, 1)
                    mixer0(s0)
                elif kind == "mixer0_out":
                    for d in range(KD):
                        split_ahead(s0 + d, 1)
                        norm_tile(NORM_MIX + 1, d)
                    norm_root(NORM_MIX + 1)

        @block.vector
        def _(dve):
            count = [0]

            def step(ins):
                count[0] += 1
                ins.then_inc(dve_step, 1)
                dve.wait_ge(dve_step, count[0])

            def link(ins):
                count[0] += 1
                ins.then_inc(dve_step, 1)

            def settle():
                dve.wait_ge(dve_step, count[0])

            def split_lo(s, n, i=0):
                dve.wait_ge(slab_hi, s + 1 + i * RING)
                dve.tensor_tensor(w_lo[:, slot(s), 0:n], raw[:, slot(s), 0:n],
                                  w_hi[:, slot(s), 0:n].bitcast(F32), ALU.subtract).then_inc(slab_lo, 1)

            def split_ahead(s, count):
                for q in range(s + LEAD, min(s + LEAD + count, total)):
                    if q not in late:
                        split_lo(q, sizes[q])

            def norm_tile(n, k):
                if n in SPLIT_NORMS:
                    dve.wait_ge(xg_hi_ready, xg_count(n, k))
                    dve.scalar_tensor_tensor(out=xg_lo[:, k, :], in0=x[:, k, :], scalar=g_all[:, n, k:k + 1],
                                             in1=xg_hi[:, k, :].bitcast(F32), op0=ALU.mult,
                                             op1=ALU.subtract).then_inc(xg_lo_ready, 1)
                dve.wait_ge(sq_ready, n * KD + k + 1)
                if k == 0:
                    if n:
                        dve.wait_ge(norm_sum, n)
                    dve.tensor_copy(ssq[:], sq[:]).then_inc(ssq_ready, 1)
                else:
                    dve.wait_ge(ssq_ready, n * KD + k)
                    dve.tensor_tensor(ssq[:], ssq[:], sq[:], ALU.add).then_inc(ssq_ready, 1)

            def norm_root(n):
                dve.wait_ge(norm_sum, n + 1)
                dve.tensor_scalar(rms[:], norm_ps[:], 1.0 / D, EPS, ALU.mult, ALU.add).then_inc(mean_ready, 1)
                if n == NORM_S5:
                    dve.wait_ge(rms_ready, n + 1)
                    dve.reciprocal(r_row[:], r_row[:]).then_inc(rinv_ready, 1)
                    dve.wait_ge(rinv_ready, n + 1)
                    return
                dve.wait_ge(rms_ready, n + 1)
                dve.reciprocal(rinv[:], rms[:]).then_inc(rinv_ready, 1)
                dve.wait_ge(rinv_ready, n + 1)

            def hidden(t, s, b, hi, lo, i=0, turn=0):
                dve.wait_ge(slab_used, used(s) + turn)
                dve.tensor_tensor(gate_r[:], gate_ps[b][:], rinv[:], ALU.mult).then_inc(gate_scaled, 1)
                dve.wait_ge(slab_used, used(s + 1) + turn)
                dve.wait_ge(silu_ready, t + 1 + i)
                dve.tensor_tensor(up_s[:], up_ps[b][:], silu_g[:], ALU.mult).then_inc(banks_free, 1)
                dve.wait_ge(banks_free, 2 + t + 1 + i)
                dve.tensor_tensor(hid[:], up_s[:], rinv[:], ALU.mult).then_inc(hid_ready, 1)
                dve.wait_ge(hid_hi, t + 1 + i)
                dve.tensor_tensor(lo, hid[:], hi.bitcast(F32), ALU.subtract).then_inc(hid_lo, 1)

            def s5_part(d):
                t = tiny
                dt, lr, li = t["log_dt"][:], t["lam_r"][:], t["lam_i"][:]
                if d == 0:
                    dve.wait_ge(s5_count, POOL_COUNT)
                    dve.wait_ge(s5_dt, 1)
                    kk = k_count[:].unsqueeze(2).broadcast_to([P, L + 1, PAIRS])

                    def times_k(a):
                        return a.unsqueeze(1).broadcast_to([P, L + 1, PAIRS])

                    step(dve.tensor_tensor(t["num_a"][:], lr, dt, ALU.mult))
                    step(dve.tensor_tensor(t["num_b"][:], li, dt, ALU.mult))
                    step(dve.tensor_tensor(t["mag"][:], kk, times_k(t["num_a"][:]), ALU.mult))
                    step(dve.tensor_tensor(t["angle"][:], kk, times_k(t["num_b"][:]), ALU.mult))
                    step(dve.tensor_scalar(t["turns"][:], t["angle"][:], 1.0 / TWO_PI, ROUND, ALU.mult, ALU.add))
                    step(dve.tensor_scalar(t["turns"][:], t["turns"][:], -ROUND, None, ALU.add))
                if d == 1:
                    for part in TWO_PI_PARTS:
                        step(dve.scalar_tensor_tensor(out=t["angle"][:], in0=t["turns"][:], scalar=-part,
                                                      in1=t["angle"][:], op0=ALU.mult, op1=ALU.add))
                    step(dve.tensor_copy(theta[:], t["angle"][:, L, :]))
                    step(dve.tensor_scalar(t["angle_c"][:], t["angle"][:], TWO_PI / 4, None, ALU.add))
                    step(dve.tensor_scalar(t["fold"][:], t["angle_c"][:], TWO_PI / 2, -TWO_PI, ALU.is_gt, ALU.mult))
                    step(dve.tensor_tensor(t["angle_c"][:], t["angle_c"][:], t["fold"][:], ALU.add))
                    step(dve.tensor_scalar(t["angle_c"][:], t["angle_c"][:], PI_BELOW, -PI_BELOW, ALU.min, ALU.max))
                    dve.tensor_scalar(t["angle"][:], t["angle"][:], PI_BELOW, -PI_BELOW, ALU.min, ALU.max)\
                       .then_inc(s5_angles, 1)
                if d == 2:
                    step(dve.tensor_tensor(t["den_l"][:], lr, lr, ALU.mult))
                    step(dve.tensor_tensor(t["abr1"][:], li, li, ALU.mult))
                    step(dve.tensor_tensor(t["den_l"][:], t["den_l"][:], t["abr1"][:], ALU.add))
                    step(dve.reciprocal(t["den_l"][:], t["den_l"][:]))
                ar, ai = pow_r[:, 1, :], pow_i[:, 1, :]
                if d == 3:
                    dve.wait_ge(s5_trig, 3)
                    step(dve.tensor_tensor(pow_r[:], t["mag"][:], t["angle_c"][:], ALU.mult))
                    step(dve.tensor_tensor(pow_i[:], t["mag"][:], t["angle"][:], ALU.mult))
                    step(dve.tensor_scalar(t["abr1"][:], ar, -1.0, None, ALU.add))
                    step(dve.tensor_tensor(t["num_a"][:], t["abr1"][:], lr, ALU.mult))
                    step(dve.tensor_tensor(t["num_b"][:], ai, li, ALU.mult))
                    step(dve.tensor_tensor(t["num_a"][:], t["num_a"][:], t["num_b"][:], ALU.add))
                    step(dve.tensor_tensor(coef[:, 0, :], t["num_a"][:], t["den_l"][:], ALU.mult))
                if d == 4:
                    step(dve.tensor_tensor(t["num_a"][:], ai, lr, ALU.mult))
                    step(dve.tensor_tensor(t["num_b"][:], t["abr1"][:], li, ALU.mult))
                    step(dve.tensor_tensor(t["num_a"][:], t["num_a"][:], t["num_b"][:], ALU.subtract))
                    step(dve.tensor_tensor(coef[:, 1, :], t["num_a"][:], t["den_l"][:], ALU.mult))
                    step(dve.tensor_copy(rho[:], t["mag"][:, L, :]))
                    step(dve.tensor_reduce(diag[:], ident[:].rearrange("p (b c) -> p c b", c=GC), AX.X, ALU.add))
                if d == 5:
                    cr, ci = (coef[:, part, :].unsqueeze(1).broadcast_to([P, L, PAIRS]) for part in range(2))
                    pr, pi = pow_r[:, 0:L, :], pow_i[:, 0:L, :]
                    wr, wi, wt = t["w_r"][:], t["w_i"][:], t["w_t"][:]
                    step(dve.tensor_tensor(wr, cr, pr, ALU.mult))
                    step(dve.tensor_tensor(wt, ci, pi, ALU.mult))
                    step(dve.tensor_tensor(wr, wr, wt, ALU.subtract))
                    step(dve.tensor_tensor(wi, cr, pi, ALU.mult))
                    step(dve.tensor_tensor(wt, ci, pr, ALU.mult))
                    dve.tensor_tensor(wi, wi, wt, ALU.add).then_inc(s5_w_ready, 1)

            def k_skip(q):
                if q == 0:
                    dve.wait_ge(d_loaded, 16)
                dve.wait_ge(k_ready, q + 1)
                for t in range(KD // QUARTERS):
                    k0 = s5_k[:, q % 2, t, 0:GC]
                    tile = q * (KD // QUARTERS) + t
                    dve.scalar_tensor_tensor(out=k0, in0=diag[:], scalar=d_col[:, tile:tile + 1], in1=k0,
                                             op0=ALU.mult, op1=ALU.add).then_inc(k_diag, 1)

            def mixer1(s0):
                dve.memset(decays[:, :, :, 0], 0.0).then_inc(decays_ready, 1)
                def scale_u(q):
                    n = 2 * PPB
                    dve.wait_ge(u_loaded[q], 16 * L)
                    u = s5_u[:, q * n:(q + 1) * n, :]
                    dve.tensor_tensor(u, u, r_row[:].unsqueeze(1).broadcast_to([P, n, NC]), ALU.mult)\
                       .then_inc(u_ready, 1)

                scale_u(0)
                scale_u(1)
                step(dve.memset(s5_x[:, :, :, 0], 0.0))
                dve.wait_ge(sines_loaded, 16)
                a, b, v = (r[:].rearrange("p w (n c) -> p w n c", c=NC) for r in rot)
                for q in range(QUARTERS):
                    ps = slice(q * PQ, (q + 1) * PQ)
                    sn, cs = sines[:, 0, ps, :], sines[:, 1, ps, :]
                    s_r, s_i = (bank[4 * part + q][:].rearrange("p (n c) -> p n c", c=NC) for part in range(2))
                    dve.wait_ge(st_ready, q + 1)
                    link(dve.tensor_tensor(a[:, 0], s_r, cs, ALU.mult))
                    link(dve.tensor_tensor(a[:, 1], s_i, cs, ALU.mult))
                    link(dve.tensor_tensor(b[:, 0], s_r, sn, ALU.mult))
                    dve.tensor_tensor(b[:, 1], s_i, sn, ALU.mult).then_inc(st_taken, 1)
                    settle()
                    dve.wait_ge(st_taken, q + 1)
                    link(dve.tensor_tensor(v[:, 0], a[:, 0], b[:, 1], ALU.add))
                    link(dve.tensor_tensor(v[:, 1], a[:, 1], b[:, 0], ALU.subtract))
                    settle()
                    dve.wait_ge(decays_ready, q + 2)
                    rho_q = decays[:, q % 2, :, :].rearrange("p n c -> p (n c)")
                    link(dve.tensor_tensor_scan(rot[0][:, 0, :], rho_q, rot[2][:, 0, :], 0.0, ALU.mult, ALU.add))
                    dve.tensor_tensor_scan(rot[0][:, 1, :], rho_q, rot[2][:, 1, :], 0.0, ALU.mult, ALU.add)\
                       .then_inc(x_scanned, 1)
                    settle()
                    if q == 0:
                        scale_u(2)
                    dve.wait_ge(x_scanned, q + 1)
                    link(dve.tensor_tensor(b, a, cs.unsqueeze(1).broadcast_to([P, 2, PQ, NC]), ALU.mult))
                    link(dve.tensor_tensor(v, a, sn.unsqueeze(1).broadcast_to([P, 2, PQ, NC]), ALU.mult))
                    settle()
                    last = slice(0, NC - 1)
                    dve.tensor_tensor(s5_x[:, 0, ps, 1:], b[:, 0, :, last], v[:, 1, :, last], ALU.subtract)\
                       .then_inc(scanned, 1)
                    dve.tensor_tensor(s5_x[:, 1, ps, 1:], v[:, 0, :, last], b[:, 1, :, last], ALU.add)\
                       .then_inc(scanned, 1)
                    dve.wait_ge(scanned, 2 * (q + 1))
                    if q == 0:
                        scale_u(3)

                def y_half(q):
                    dve.wait_ge(y_ready, 2 * q + 2)
                    dve.tensor_copy(s5_y[:, 2 * q + 1, :, :].rearrange("p j (a c) -> p a j c", c=GC),
                                    y_bank(2 * q + 1)[:].rearrange("p (a j c) -> p a j c", j=L, c=GC))\
                       .then_inc(y_taken_d, 1)

                def y_split(k):
                    gelu = (sq, ssq)[k % 2]
                    dve.wait_ge(y_hi_ready, k + 1)
                    dve.tensor_tensor(y_lo[:, k, :], gelu[:], y_hi[:, k, :].bitcast(F32), ALU.subtract)\
                       .then_inc(y_lo_ready, 1)

                y_half(0)
                for q in range(1, QUARTERS):
                    y_half(q)
                    y_split(2 * q - 2)
                    y_split(2 * q - 1)
                for s in late:
                    split_lo(s, sizes[s])
                y_split(KD - 2)
                y_split(KD - 1)
                for d in range(KD):
                    split_ahead(s0 + 2 * d, 2)
                    dve.wait_ge(glu_sig, d + 1)
                    dve.tensor_tensor(glu[:, d % 2, :], gate_ps[d % 2][:], sig[:, d % 2, :], ALU.mult).then_inc(glu_mul, 1)
                    dve.wait_ge(glu_mul, d + 1)
                    xv = x[:, d, :].rearrange("p (c j) -> p j c", j=L)
                    dve.tensor_tensor(xv, xv, glu[:, d % 2, :].rearrange("p (j c) -> p j c", j=L), ALU.add).then_inc(x_ready, 1)
                    if d:
                        norm_tile(NORM_S5 + 1, d - 1)
                norm_tile(NORM_S5 + 1, KD - 1)
                norm_root(NORM_S5 + 1)

            def mixer0(s0):
                dve.wait_ge(col_ready, 1)
                dve.tensor_copy(r_col[:], bank[7][:, 0:NT]).then_inc(col_taken, 1)
                for n in range(3 * BH):
                    split_ahead(s0 + n, 1)
                    dve.wait_ge(slab_used, used(s0 + n))
                    dst = (b_e, b_q, b_g)[n // BH]
                    dve.tensor_tensor(dst[:, n % BH, :], bank[n % 4][:], rinv[:], ALU.mult).then_inc(proj_scaled, 1)
                    dve.wait_ge(sig_ready, n + 1)
                    if n < BH:
                        f = b_k[:, n, :]
                        dve.tensor_scalar(f, f, lb_c[:, n:n + 1], lb[:, n:n + 1], ALU.mult, ALU.add)\
                           .then_inc(f_one, 1)
                        if n == BH - 1:
                            dve.wait_ge(f_one, BH)
                            dve.memset(scores[:], 0.0).then_inc(f_ready, 1)
                    else:
                        dve.tensor_tensor(dst[:, n % BH, :], dst[:, n % BH, :], b_tmp[:, n % 2, :], ALU.mult)\
                           .then_inc(sig_used, 1)
                dve.wait_ge(logf_ready, 1)
                step(dve.tensor_scalar(b_k[:], b_k[:], -1.0, 1.0, ALU.mult, ALU.add))
                cum = b_cum[:].rearrange("p h (c j) -> p (h c) j", j=CH)
                for j in range(1, CH):
                    ins = dve.tensor_tensor(cum[:, :, j], cum[:, :, j], cum[:, :, j - 1], ALU.add)
                    if j < CH - 1:
                        step(ins)
                    else:
                        ins.then_inc(cum_ready, 1)
                s = s0 + 3 * BH
                split_ahead(s, 2)
                dve.wait_ge(cum_ready, 1)
                dve.tensor_copy(decay[:].rearrange("p h c -> p (h c)"), cum[:, :, CH - 1]).then_inc(f_ready, 1)
                dve.wait_ge(exp_ready, 1)
                step(dve.tensor_tensor(b_q[:], b_q[:], b_e[:], ALU.mult))
                dve.tensor_copy(decay[:], b_e[:].rearrange("p h (c j) -> p h c j", j=CH)[:, :, :, CH - 1])\
                   .then_inc(exp_used, 1)
                dve.wait_ge(exp_ready, 2)
                step(dve.tensor_tensor(b_kinv[:], b_k[:], b_e[:], ALU.mult))
                for h in range(BH):
                    c3 = b_cum[:, h, :].rearrange("p (c j) -> p c j", j=CH)
                    dve.wait_ge(dve_step, count[0])
                    ins = dve.tensor_tensor(c3, c3[:, :, CH - 1:CH].broadcast_to([P, NCH, CH]), c3, ALU.subtract)
                    if h < BH - 1:
                        step(ins)
                    else:
                        ins.then_inc(cum_ready, 1)
                split_ahead(s + 2, 2)
                dve.wait_ge(exp_ready, 3)
                dve.tensor_tensor(b_k[:], b_k[:], b_cum[:], ALU.mult).then_inc(b_ready, 1)
                s = s0 + 4 * BH
                for t in range(AT):
                    split_ahead(s + t, 1)
                    dve.wait_ge(slab_used, used(s + t))
                    dve.scalar_tensor_tensor(out=a_q[:, t, :], in0=bank[t % 4][:], scalar=AD ** -0.5, in1=rinv[:],
                                             op0=ALU.mult, op1=ALU.mult).then_inc(proj_scaled, 1)
                split_ahead(s + AT, 1)
                dve.wait_ge(slab_used, used(s + AT))
                dve.tensor_tensor(a_k[:], bank[0][:], rinv[:], ALU.mult).then_inc(proj_scaled, 1)
                split_ahead(s + AT + 1, 1)
                mask = causal[:].bitcast(I32).unsqueeze(1).broadcast_to([P, NT, P])
                for h in range(BH):
                    dve.wait_ge(sc_ready, h + 1)
                    dve.copy_predicated(scores[:, h % 2, :, :], mask,
                                        bank[0][:].rearrange("p (m q) -> p m q", q=P)).then_inc(sc_masked, 1)
                    dve.wait_ge(kv_ready, h + 1)
                    if h:
                        dve.wait_ge(inter_done, h)
                    kv = [bank[4 + i][:].rearrange("p (m v) -> p m v", v=P) for i in range(CPT)]
                    dve.tensor_copy(states[:, 1, :], kv[0][:, 0, :]).then_inc(state_ready, 1)
                    for c in range(1, NCH - 1):
                        dve.wait_ge(state_ready, h * (NCH - 1) + c)
                        dve.scalar_tensor_tensor(out=states[:, c + 1, :], in0=states[:, c, :],
                                                 scalar=decay[:, h, c:c + 1], in1=kv[c % CPT][:, c // CPT, :],
                                                 op0=ALU.mult, op1=ALU.add).then_inc(state_ready, 1)
                dve.wait_ge(o_sum, BH)
                dve.tensor_scalar(rms[:], bank[1][:], 1.0 / P, EPS, ALU.mult, ALU.add).then_inc(o_mean, 1)
                dve.wait_ge(o_rms, 1)
                dve.reciprocal(ssq[:], rms[:]).then_inc(o_rinv, 1)
                for h in range(BH):
                    dve.wait_ge(o_taken, h + 1)
                    step(dve.tensor_tensor(b_g[:, h, :], b_g[:, h, :], b_o[:, h, :], ALU.mult))
                    dve.wait_ge(o_bcast, h + 1)
                    dve.tensor_tensor(rec[:, h % 2, :], bank[4 + h][:], b_g[:, h, :], ALU.mult).then_inc(rec_ready, 1)
                    dve.wait_ge(mix_hi, h + 1)
                    dve.tensor_tensor(rec_l[:, h, :], rec[:, h % 2, :], rec_h[:, h, :].bitcast(F32),
                                      ALU.subtract).then_inc(mix_lo, 1)
                for u in range(len(UNITS) + 3):
                    if u < len(UNITS):
                        n, tp, g = UNITS[u]
                        k0 = 0 if n else P
                        b = u % 2
                        h0 = AT * g + 2 * tp
                        dve.wait_ge(s_ready, u + 1)
                        if u >= 2:
                            dve.wait_ge(pt_ready, u - 1)
                        for j in range(2):
                            ins = dve.scalar_tensor_tensor(
                                out=prob[:, b, j, k0:], in0=dist[:, k0:], scalar=-SLOPES[h0 + j],
                                in1=bank[g][:, j * 2 * P + k0:(j + 1) * 2 * P], op0=ALU.mult, op1=ALU.add)
                            if j:
                                ins.then_inc(s_taken, 1)
                            else:
                                ins.then_inc(dve_step, 1)
                                count[0] += 1
                        dve.wait_ge(s_taken, u + 1)
                        dve.wait_ge(dve_step, count[0])
                        step(dve.tensor_reduce(max_neg[:, b, :], prob[:, b, :, k0:], AX.X, ALU.max, negate=True))
                        step(dve.tensor_tensor(max_neg[:, b, :], max_neg[:, b, :], sink_neg[:, h0:h0 + 2], ALU.min))
                        dve.tensor_tensor(sink_d[:, b, :], sink[:, h0:h0 + 2], max_neg[:, b, :], ALU.add)\
                           .then_inc(m_ready, 1)
                    if 1 <= u <= len(UNITS):
                        v = u - 1
                        b = v % 2
                        k0 = 0 if UNITS[v][0] else P
                        dve.wait_ge(p_exp, 3 * (v + 1))
                        step(dve.tensor_tensor(den[:, b, :], rowsum[:, b, :], sink_e[:, b, :], ALU.add))
                        step(dve.reciprocal(rden[:, b, :], den[:, b, :]))
                        for j in range(2):
                            dve.tensor_scalar(prob[:, b, j, k0:], prob[:, b, j, k0:], rden[:, b, j:j + 1], None,
                                              ALU.mult).then_inc(p_ready, 1)
                    if u >= 3 and (u - 3) % 4 == 3:
                        n = (u - 3) // 4
                        dve.wait_ge(att_hi, n + 1)
                        dve.tensor_tensor(att_l[:, :, n * P:(n + 1) * P],
                                          bank[4 + n % 2][:].rearrange("p (t q) -> p t q", q=P),
                                          att_h[:, :, n * P:(n + 1) * P].bitcast(F32), ALU.subtract)\
                           .then_inc(att_lo, 1)

            dve.memset(ones[:], 1.0).then_inc(ones_set, 1)
            dve.wait_ge(const_loaded, 32)
            split_lo(0, sizes[0])
            for k in range(KD):
                dve.wait_ge(x_loaded[k], 16)
                norm_tile(0, k)
            split_lo(1, sizes[1])
            norm_root(0)
            for kind, f, half, s0 in phases:
                if kind == "in":
                    t0 = (HALVES * f + half) * KF
                    split_ahead(s0, 2)
                    hidden(t0, s0, 0, h_hi[:, 0, :], h_lo[:, 0, :])
                    with dve.Fori(0, KF // 2 - 1) as i:
                        for t in (1, 2):
                            for part in range(2):
                                split_lo(s0 + 2 * t + part + LEAD, SLAB_IN, i)
                            hidden(t0 + t, s0 + 2 * t, t % 2, h_hi[:, bass.ds(i * 2 + t, 1), :].squeeze(1),
                                   h_lo[:, bass.ds(i * 2 + t, 1), :].squeeze(1), i * 2, i * RING)
                    for t in (KF - 2, KF - 1):
                        split_ahead(s0 + 2 * t, 2)
                        hidden(t0 + t, s0 + 2 * t, t % 2, h_hi[:, t, :], h_lo[:, t, :])
                elif kind == "out":
                    for d in range(KD):
                        split_ahead(s0 + d, 1)
                        if (f, half) == S5_SMALL:
                            s5_part(d)
                        if (f, half) == S5_KERNELS and d % 2 == 1:
                            k_skip(d // 2)
                        dve.wait_ge(slab_used, used(s0 + d))
                        add = dve.scalar_tensor_tensor(out=x[:, d, :], in0=out_ps[d % 2][:], scalar=0.5,
                                                       in1=x[:, d, :], op0=ALU.mult, op1=ALU.add)
                        if half == HALVES - 1:
                            add.then_inc(x_ready, 1)
                            norm_tile(NORMS[f] + 1, d)
                        else:
                            add.then_inc(x_half, 1)
                    if half == HALVES - 1:
                        norm_root(NORMS[f] + 1)
                elif kind == "mixer1":
                    mixer1(s0)
                elif kind == "mixer0":
                    dve.wait_ge(small_loaded, 32)
                    step(dve.tensor_tensor(lb_c[:], lb_in[:], lb_in[:], ALU.subtract))
                    dve.tensor_scalar(sink_neg[:], sink[:], -1.0, None, ALU.mult).then_inc(lb_exp, 1)
                    dve.wait_ge(act_step, 1)
                    step(dve.reciprocal(lb_c[:], lb[:]))
                    step(dve.tensor_tensor(lb_in[:], lb[:], lb_c[:], ALU.mult))
                    step(dve.tensor_tensor(lb[:], lb_in[:], lb_in[:], ALU.subtract))
                    step(dve.tensor_scalar(lb_c[:], lb[:], -1.0, 1.0, ALU.mult, ALU.add))
                    mixer0(s0)
                elif kind == "mixer0_out":
                    for d in range(KD):
                        split_ahead(s0 + d, 1)
                        dve.wait_ge(slab_used, used(s0 + d))
                        dve.tensor_tensor(x[:, d, :], out_ps[d % 2][:], x[:, d, :], ALU.add).then_inc(x_ready, 1)
                        norm_tile(NORM_MIX + 1, d)
                    norm_root(NORM_MIX + 1)
            for k in range(KD):
                dve.scalar_tensor_tensor(out=x[:, k, :], in0=x[:, k, :], scalar=g_all[:, NORM_FIN, k:k + 1],
                                         in1=rinv[:], op0=ALU.mult, op1=ALU.mult).then_inc(fin_ready, 1)

        @block.tensor
        def _(pe):
            def product(out, s, k, hi, lo, start, stop):
                wh = w_hi[:, slot(s), k * P:(k + 1) * P]
                wl = w_lo[:, slot(s), k * P:(k + 1) * P]
                pe.matmul(out, wh, hi, start=start, stop=False)
                pe.matmul(out, wh, lo, start=False, stop=False)
                return pe.matmul(out, wl, hi, start=False, stop=stop)

            def norm(n):
                pe.wait_ge(ssq_ready, (n + 1) * KD)
                if n:
                    pe.wait_ge(mean_ready, n)
                pe.matmul(norm_ps[:], ones[:], ssq[:], start=True, stop=True).then_inc(norm_sum, 1)

            def natural(s, count, out):
                for m in range(NT):
                    for k in range(KD):
                        xh = xg_hi[:, k, m * P:(m + 1) * P]
                        xl = xg_lo[:, k, m * P:(m + 1) * P]
                        wh = w_hi[:, slot(s):slot(s) + count, k * P:(k + 1) * P]
                        wl = w_lo[:, slot(s):slot(s) + count, k * P:(k + 1) * P]
                        pe.matmul(out(m), xh, wh, start=k == 0, stop=False)
                        pe.matmul(out(m), xh, wl, start=False, stop=False)
                        mm = pe.matmul(out(m), xl, wh, start=False, stop=k == KD - 1)
                return mm

            def mixer0(s0):
                for n in range(3 * BH):
                    s = s0 + n
                    if n >= 4:
                        pe.wait_ge(proj_scaled, n - 3)
                    pe.wait_ge(slab_lo, split(s))
                    for k in range(KD):
                        if n == 0:
                            pe.wait_ge(xg_lo_ready, xg_count(NORM_MIX, k))
                        mm = product(bank[n % 4][:], s, k, xg_hi[:, k, :], xg_lo[:, k, :], k == 0, k == KD - 1)
                    mm.then_inc(slab_used, 1)
                    if n == 0:
                        pe.wait_ge(rinv_ready, NORM_MIX + 1)
                        for m in range(NT):
                            mm = pe.matmul(bank[7][:, m:m + 1], rinv[0:1, m * P:(m + 1) * P], ones[0:1, 0:1],
                                           start=True, stop=True)
                        mm.then_inc(col_ready, 1)
                s = s0 + 3 * BH
                for pair in range(BH // 2):
                    pe.wait_ge(proj_scaled, 3 * BH)
                    pe.wait_ge(slab_lo, split(s + 2 * pair + 1))
                    assert slot(s + 2 * pair) % 2 == 0

                    def out(m):
                        return bank[2 * pair + m // 2][:, (m % 2) * 2 * P:(m % 2 + 1) * 2 * P]\
                            .rearrange("p (a c) -> p a c", a=2)
                    natural(s + 2 * pair, 2, out).then_inc(slab_used, 2)
                s = s0 + 4 * BH
                for n in range(AT + 1):
                    pe.wait_ge(nat_taken, min(2 * NT, NT * (n // 2 + 1)) if n < AT else 2 * NT)
                    if n == AT:
                        pe.wait_ge(proj_scaled, 3 * BH + 1)
                    pe.wait_ge(slab_lo, split(s + n))
                    for k in range(KD):
                        mm = product(bank[n % 4][:], s + n, k, xg_hi[:, k, :], xg_lo[:, k, :], k == 0, k == KD - 1)
                    mm.then_inc(slab_used, 1)
                pe.wait_ge(proj_scaled, 3 * BH + 2)
                pe.wait_ge(slab_lo, split(s + AT + 1))
                natural(s + AT + 1, 1, lambda m: bank[1][:, m * P:(m + 1) * P]).then_inc(slab_used, 1)

                def head_scores(h):
                    if h:
                        pe.wait_ge(sc_masked, h)
                    for m in range(NT):
                        t = slice(m * P, (m + 1) * P)
                        mm = pe.matmul(bank[0][:, t], b_kinv[:, h, t], b_q[:, h, t], start=True, stop=True)
                    mm.then_inc(sc_ready, 1)
                    if h:
                        pe.wait_ge(kt_taken, h)
                    for m in range(NT):
                        t = slice(m * P, (m + 1) * P)
                        mm = pe.transpose(bank[1][:, t], b_k[:, h, t], ident[:])
                    mm.then_inc(kt_ready, 1)

                def head_chunks(h):
                    v = b_v[:, :, h * P:(h + 1) * P]
                    pe.wait_ge(kt_taken, h + 1)
                    if h:
                        pe.wait_ge(state_ready, h * (NCH - 1))
                    for m in range(NT):
                        for i in range(CPT):
                            rows = slice(i * CH, (i + 1) * CH)
                            mm = pe.matmul(bank[4 + i][:, m * P:(m + 1) * P], k_end[rows, h % 2, m, :], v[rows, m, :],
                                           start=True, stop=True)
                    mm.then_inc(kv_ready, 1)
                    pe.wait_ge(sc_masked, h + 1)
                    if h >= 2:
                        pe.wait_ge(o_sq, h - 1)
                    ob = bank[2 + h % 2]
                    for m in range(NT):
                        pe.matmul(ob[:, m * P:(m + 1) * P], v[:, m, :], scores[:, h % 2, m, :], start=m == 0,
                                  stop=False, skip_group_check=True)
                    for c in range(1, NCH):
                        pe.wait_ge(state_ready, h * (NCH - 1) + c)
                        mm = pe.matmul(ob[:, c * CH:(c + 1) * CH], states[:, c, :], b_q[:, h, c * CH:(c + 1) * CH],
                                       start=False, stop=c == NCH - 1, skip_group_check=True)
                    mm.then_inc(inter_done, 1)

                def head_square(h):
                    pe.wait_ge(o_sq, h + 1)
                    if h == 0:
                        pe.wait_ge(kt_taken, BH)
                    pe.matmul(bank[1][h * CH:(h + 1) * CH, :], ones[:, 0:CH], squares[:, h, :], start=True, stop=True)\
                      .then_inc(o_sum, 1)

                pe.wait_ge(b_ready, 1)
                pe.wait_ge(nat_taken, 3 * NT)
                pe.wait_ge(proj_scaled, 3 * BH + AT + 1)
                head_scores(0)
                for h in range(BH):
                    head_chunks(h)
                    if h + 1 < BH:
                        head_scores(h + 1)
                    else:
                        for g in range(BH):
                            head_square(g)
                pe.wait_ge(o_rinv, 1)
                for h in range(BH):
                    pe.matmul(bank[4 + h][:], ones[h * CH:h * CH + 1, :], ssq[h * CH:h * CH + 1, :], start=True, stop=True)\
                      .then_inc(o_bcast, 1)

                for u in range(len(UNITS) + 2):
                    if u < len(UNITS):
                        n, tp, g = UNITS[u]
                        rows = slice(g * AD, (g + 1) * AD)
                        k0 = 0 if n else P
                        if u == 0:
                            pe.wait_ge(sc_masked, BH)
                            pe.wait_ge(o_mean, 1)
                        if u >= 2:
                            pe.wait_ge(s_taken, u - 1)
                        for j in range(2):
                            mm = pe.matmul(bank[g][:, j * 2 * P + k0:(j + 1) * 2 * P],
                                           a_q[rows, 2 * tp + j, n * P:(n + 1) * P],
                                           a_k[rows, (n - 1) * P + k0:(n + 1) * P], start=True, stop=True)
                        mm.then_inc(s_ready, 1)
                    if 1 <= u <= len(UNITS):
                        v = u - 1
                        n, tp, g = UNITS[v]
                        pe.wait_ge(p_ready, 2 * (v + 1))
                        if v >= 2:
                            pe.wait_ge(pt_taken, taken(v - 2))
                        else:
                            pe.wait_ge(o_sq, BH - 1 + v)
                        for j in range(2):
                            for kt in range(0 if n else 1, 2):
                                mm = pe.transpose(bank[2 + v % 2][:, (2 * j + kt) * P:(2 * j + kt + 1) * P],
                                                  prob[:, v % 2, j, kt * P:(kt + 1) * P], ident[:])
                        mm.then_inc(pt_ready, 1)
                    if u >= 2:
                        v = u - 2
                        n, tp, g = UNITS[v]
                        pe.wait_ge(pt_taken, taken(v))
                        if v % 4 == 0:
                            if n >= 2:
                                pe.wait_ge(att_lo, n - 1)
                            else:
                                pe.wait_ge(rec_ready, n + 1)
                        kts = range(0 if n else 1, 2)
                        for j in range(2):
                            for kt in kts:
                                mm = pe.matmul(bank[4 + n % 2][g * AD:(g + 1) * AD, (2 * tp + j) * P:(2 * tp + j + 1) * P],
                                               a_v[:, n - 1 + kt, g * AD:(g + 1) * AD], prob_t[:, v % 2, j, kt, :],
                                               start=kt == kts[0], stop=kt == 1)
                        mm.then_inc(pv_done, 1)

            def w_turn():
                pe.wait_ge(s5_w_ready, 1)
                for part, name in enumerate(("w_r", "w_i")):
                    w = tiny[name][:].rearrange("p j a -> p (j a)")
                    for half in range(L * PAIRS // P):
                        mm = pe.transpose(bank[7][:, (2 * part + half) * P:(2 * part + half + 1) * P],
                                          w[:, half * P:(half + 1) * P], ident[:])
                mm.then_inc(s5_w_turned, 1)

            def kernels(q):
                if q == 0:
                    pe.wait_ge(bb_loaded, 16)
                else:
                    pe.wait_ge(k_ready, q)
                pe.wait_ge(cq_loaded[q % 2], 32 * (q // 2 + 1))
                per = PAIRS // KD
                for t in range(KD // QUARTERS):
                    for i in range(per):
                        for part in range(2):
                            mm = pe.matmul(bank[7][i * 2 * GC:(i + 1) * 2 * GC, t * P:(t + 1) * P],
                                           s5_bb[:, q * PQ + t * per + i, part, :], s5_cq[:, q % 2, part, t * per + i, :],
                                           start=part == 0, stop=part == 1)
                mm.then_inc(k_summed, 1)

            def mixer1(s0):
                pe.wait_ge(mean_ready, NORM_S5 + 1)
                m3 = rms[0:1, :].rearrange("p (c j) -> p j c", j=L)
                pe.wait_ge(pool_const, POOL_ALL)
                for j in range(L):
                    mm = pe.matmul(bank[7][:, 0:NC], r_sel[:, (L - 1 - j) * GC:(2 * L - 1 - j) * GC], m3[:, j, :],
                                   start=j == 0, stop=j == L - 1)
                mm.then_inc(row_ready, 1)
                pe.wait_ge(bm_loaded[0], 16)
                pe.wait_ge(bm_loaded[1], 16)
                for b in range(PAIRS // PPB):
                    pe.wait_ge(u_ready, b + 1)
                    for part in range(2):
                        for a in range(PPB):
                            for g in range(2):
                                pair = b * PPB + a
                                mm = pe.matmul(bank[4 * part + b][g * NS:(g + 1) * NS, a * NC:(a + 1) * NC],
                                               s5_bm[:, 2 * pair + g, part, :], s5_u[:, group(pair, g), :],
                                               start=True, stop=True)
                    mm.then_inc(st_ready, 1)
                pe.wait_ge(t_loaded, 16 * L)

                def within(q):
                    pe.wait_ge(st_taken, q + 1)
                    for i in range(2):
                        k = 2 * q + i
                        for a in range(PER):
                            for g in range(2):
                                pair = k * PER + a
                                pe.matmul(y_bank(k)[g * NC:(g + 1) * NC, a * P:(a + 1) * P],
                                          s5_u[:, group(pair, g), :], s5_t[:, 2 * pair + g, :],
                                          start=a == 0, stop=False, skip_group_check=True)

                def from_states(q):
                    pe.wait_ge(c_loaded[q], 16 * 2)
                    pe.wait_ge(scanned, 2 * (q + 1))
                    for turn in range(2):
                        for a in range(PER):
                            for part in range(2):
                                for i in range(2):
                                    k, g = 2 * q + i, i ^ turn
                                    pair = k * PER + a
                                    rows = slice(g * NS, (g + 1) * NS)
                                    last = a == PER - 1 and part == 1
                                    mm = pe.matmul(y_bank(k)[g * NC:(g + 1) * NC, a * P:(a + 1) * P],
                                                   s5_x[rows, part, pair, :], s5_c[rows, pair, part, :],
                                                   start=False, stop=last, skip_group_check=True)
                                    if last and turn:
                                        mm.then_inc(y_ready, 1)

                def y_turned(q):
                    pe.wait_ge(y_taken_a, q + 1)
                    pe.wait_ge(y_taken_d, q + 1)
                    for turn in range(2):
                        for j in range(L):
                            for i in range(2):
                                k, g = 2 * q + i, i ^ turn
                                rows = slice(g * NC, (g + 1) * NC)
                                out = y_bank(k)[g * NS:(g + 1) * NS, j * NC:(j + 1) * NC]
                                if g == 0:
                                    mm = pe.transpose(out, s5_y[rows, k, j, :], ident[rows, rows])
                                else:
                                    mm = pe.matmul(out, s5_y[rows, k, j, :], ident[rows, rows], start=True, stop=True)
                                if turn and j == L - 1:
                                    mm.then_inc(yt_ready, 1)

                within(0)
                within(1)
                from_states(0)
                for q in range(2, QUARTERS):
                    within(q)
                    from_states(q - 1)
                    y_turned(q - 2)
                from_states(QUARTERS - 1)
                y_turned(QUARTERS - 2)
                y_turned(QUARTERS - 1)
                for d in range(KD):
                    if d >= 2:
                        pe.wait_ge(glu_mul, d - 1)
                    for part, out in enumerate((gate_ps[d % 2], up_ps[d % 2])):
                        s = s0 + 2 * d + part
                        pe.wait_ge(slab_lo, split(s))
                        for k in range(KD):
                            if d == 0 and part == 0:
                                pe.wait_ge(y_lo_ready, k + 1)
                            mm = product(out[:], s, k, y_hi[:, k, :], y_lo[:, k, :], k == 0, k == KD - 1)
                        mm.then_inc(slab_used, 1)

            pe.wait_ge(ones_set, 1)
            for kind, f, half, s0 in phases:
                t0 = (HALVES * f + half) * KF
                if kind == "in":
                    def tile(t, n, i=0, turn=0):
                        pe.wait_ge(banks_free, t0 + t + 1 + i)
                        for part, out in enumerate((gate_ps[t % 2], up_ps[t % 2])):
                            s = s0 + 2 * t + part
                            pe.wait_ge(slab_lo, split(s) + turn)
                            for k in range(KD):
                                if n is not None and part == 0:
                                    pe.wait_ge(xg_lo_ready, xg_count(n, k))
                                mm = product(out[:], s, k, xg_hi[:, k, :], xg_lo[:, k, :], k == 0, k == KD - 1)
                            mm.then_inc(slab_used, 1)
                            if n is not None and part == 0:
                                norm(n)

                    tile(0, NORMS[f] if half == 0 else None)
                    with pe.Fori(0, KF // 2) as i:
                        tile(1, None, i * 2, i * RING)
                        tile(2, None, i * 2, i * RING)
                elif kind == "out":
                    for d in range(KD):
                        s = s0 + d
                        if d >= 2:
                            if half == HALVES - 1:
                                pe.wait_ge(x_ready, NORMS[f] * KD + d - 1)
                            else:
                                pe.wait_ge(x_half, f * KD + d - 1)
                        pe.wait_ge(slab_lo, split(s))
                        for k in range(KF):
                            if d == 0:
                                pe.wait_ge(hid_lo, t0 + k + 1)
                            mm = product(out_ps[d % 2][:], s, k, h_hi[:, k, :], h_lo[:, k, :], k == 0, k == KF - 1)
                        mm.then_inc(slab_used, 1)
                        if (f, half) == S5_SMALL and d == KD - 2:
                            w_turn()
                        if (f, half) == S5_KERNELS and d % 2 == 0:
                            kernels(d // 2)
                    if half == HALVES - 1 and NORMS[f] + 1 not in NORMS:
                        norm(NORMS[f] + 1)
                elif kind == "mixer1":
                    mixer1(s0)
                elif kind == "mixer0":
                    pe.wait_ge(pool_const, POOL_CONSTS)
                    mixer0(s0)
                elif kind == "mixer0_out":
                    pe.wait_ge(att_lo, NT)
                    pe.wait_ge(mix_lo, BH)
                    for d in range(KD):
                        s = s0 + d
                        if d >= 2:
                            pe.wait_ge(x_ready, NORM_MIX * KD + d - 1)
                        pe.wait_ge(slab_lo, split(s))
                        for k in range(KD):
                            hi, lo = (att_h[:, k, :], att_l[:, k, :]) if k < AT else (rec_h[:, k - AT, :], rec_l[:, k - AT, :])
                            mm = product(out_ps[d % 2][:], s, k, hi, lo, k == 0, k == KD - 1)
                        mm.then_inc(slab_used, 1)

        @block.gpsimd
        def _(pool):
            pool.sem_inc(slab_used, RING)
            pool.sem_inc(slab_lo, RING)
            pool.sem_inc(banks_free, 2)
            done = [0]

            def step(ins):
                done[0] += 1
                ins.then_inc(pool_const, 1)
                pool.wait_ge(pool_const, done[0])

            step(pool.memset(ident[:], 0.0))
            step(pool.affine_select(out=ident[:], in_=ident[:], compare_op=ALU.not_equal, fill=1.0, base=0,
                                    pattern=[[-1, P]], channel_multiplier=1))
            step(pool.memset(causal[:], 1.0))
            c3 = causal[:].rearrange("p (c j) -> p c j", j=CH)
            step(pool.affine_select(out=c3, in_=c3, compare_op=ALU.is_ge, fill=0.0, base=0,
                                    pattern=[[CH, CPT], [1, CH]], channel_multiplier=-1))
            step(pool.affine_select(out=c3, in_=c3, compare_op=ALU.is_ge, fill=0.0, base=0,
                                    pattern=[[-CH, CPT], [0, CH]], channel_multiplier=1))
            step(pool.iota(dist[:].bitcast(I32), pattern=[[-1, 2 * P]], base=P, channel_multiplier=1))
            step(pool.tensor_copy(dist[:], dist[:].bitcast(I32)))
            step(pool.affine_select(out=dist[:], in_=dist[:], compare_op=ALU.is_ge, fill=MASKED, base=P,
                                    pattern=[[-1, 2 * P]], channel_multiplier=1))
            step(pool.affine_select(out=dist[:], in_=dist[:], compare_op=ALU.is_ge, fill=MASKED, base=-1,
                                    pattern=[[1, 2 * P]], channel_multiplier=-1))
            assert done[0] == POOL_CONSTS
            step(pool.memset(r_sel[:], 0.0))
            step(pool.memset(r_sel[:, (L - 1) * GC:L * GC], 1.0))
            assert done[0] == POOL_ALL

            pool.wait_ge(slab_used, used(next(s0 for k, _, _, s0 in phases if k == "mixer0_out") + KD - 1))
            pool.iota(k_count[:].bitcast(I32), pattern=[[1, L + 1]], base=0, channel_multiplier=0)\
                .then_inc(s5_count, 1)
            pool.wait_ge(s5_count, 1)
            pool.tensor_copy(k_count[:], k_count[:].bitcast(I32)).then_inc(s5_count, 1)
            pool.dma_start(tiny["lam_r"][:], s5_a_re).then_inc(s5_loaded, 16)
            pool.dma_start(tiny["lam_i"][:], s5_a_im).then_inc(s5_loaded, 16)
            for g in range(2):
                pool.dma_start(tiny["log_dt"][g * NS:(g + 1) * NS, :], s5_log_step[g].partition_broadcast(NS))\
                    .then_inc(s5_loaded, 16)

            made = [0]
            loads = [0]
            stores = [0]

            def link(ins):
                made[0] += 1
                ins.then_inc(pool_step, 1)
                pool.wait_ge(pool_step, made[0])

            def fetch(out, src):
                loads[0] += 1
                pool.dma_start(out, src).then_inc(mk_loaded, 16)

            def fetched():
                pool.wait_ge(mk_loaded, 16 * loads[0])

            def store(out, src):
                stores[0] += 1
                pool.dma_start(out, src).then_inc(mk_stored, 16)

            def kept():
                pool.wait_ge(mk_stored, 16 * stores[0])

            tt = pool.tensor_tensor
            pool.wait_ge(s5_w_rows, 1)
            store(dram_w.rearrange("w (h j) (a g) s -> (j a) (w h) (g s)", h=2, g=2), w_rows[:])
            kept()
            for q in range(4):
                gs = slice(q * GQ, (q + 1) * GQ)
                kept()
                for j in range(L):
                    fetch(mk_w[j * GC:(j + 1) * GC, :, :], dram_w[:, L - 1 - j, gs, :].rearrange("w g s -> w (g s)")
                          .partition_broadcast(GC))
                for src, name in ((s5_bt_re, "br"), (s5_bt_im, "bi")):
                    fetch(mk[name][:], src[:, q * GQ * NS:(q + 1) * GQ * NS].unsqueeze(0)
                          .broadcast_to([L, GC, GQ * NS]))
                fetched()
                wr, wi = mk_w[:, 0, :], mk_w[:, 1, :]
                br, bi, t1, t2 = (mk[n][:] for n in ("br", "bi", "t1", "t2"))
                link(tt(t1, wr, br, ALU.mult))
                link(tt(t2, wi, bi, ALU.mult))
                link(tt(t1, t1, t2, ALU.subtract))
                link(tt(t2, wr, bi, ALU.mult))
                link(tt(wr, wi, br, ALU.mult))
                link(tt(t2, t2, wr, ALU.add))
                store(dram_bm[:, gs, 0, :], mk["t1"][:].rearrange("p (g s) -> p g s", s=NS))
                store(dram_bm[:, gs, 1, :], mk["t2"][:].rearrange("p (g s) -> p g s", s=NS))
            kept()
            fetch(mk["cr"][:], s5_c_re)
            fetch(mk["ci"][:], s5_c_im)
            fetched()
            link(pool.tensor_scalar(mk["ncr"][:], mk["cr"][:], -1.0, None, ALU.mult))
            for q in range(4):
                ps = slice(q * PQ, (q + 1) * PQ)

                def over_k(a):
                    return a[:, ps, :].unsqueeze(2).broadcast_to([P, PQ, L + 1, GC])

                def over_c(a):
                    return a[:, :, ps].rearrange("p k a -> p a k").unsqueeze(3).broadcast_to([P, PQ, L + 1, GC])

                def v(a):
                    return a.rearrange("p a (k c) -> p a k c", c=GC)

                cr, ci, ncr = over_k(mk["cr"][:]), over_k(mk["ci"][:]), over_k(mk["ncr"][:])
                pr, pi = over_c(pow_r[:]), over_c(pow_i[:])
                t1, t2 = v(mk["u1"][:]), v(mk["u2"][:])
                for n in range(PQ):
                    link(tt(t1[:, n], cr[:, n], pr[:, n], ALU.mult))
                    link(tt(t2[:, n], ci[:, n], pi[:, n], ALU.mult))
                kept()
                link(tt(mk_c[:, 0], mk["u1"][:], mk["u2"][:], ALU.subtract))
                for n in range(PQ):
                    link(tt(t1[:, n], ncr[:, n], pi[:, n], ALU.mult))
                    link(tt(t2[:, n], ci[:, n], pr[:, n], ALU.mult))
                link(tt(mk_c[:, 1], mk["u1"][:], mk["u2"][:], ALU.subtract))
                for part in range(2):
                    store(dram_c[:, part, ps, :], mk_c[:, part])
            kept()
            fetch(mk["sr"][:], s5_b_re)
            fetch(mk["si"][:], s5_b_im)
            link(pool.memset(mk_bb[:], 0.0))
            fetched()
            sr, si, t1, t2 = (mk[n][:] for n in ("sr", "si", "s1", "s2"))
            cr = coef[:, 0, :].unsqueeze(2).broadcast_to([P, PAIRS, GC])
            ci = coef[:, 1, :].unsqueeze(2).broadcast_to([P, PAIRS, GC])
            for part, (a, b, op) in enumerate(((sr, si, ALU.subtract), (si, sr, ALU.add))):
                link(tt(t1, cr, a, ALU.mult))
                link(tt(t2, ci, b, ALU.mult))
                for g in range(2):
                    rows = slice(g * NS, (g + 1) * NS)
                    link(tt(mk_bb[rows, :, part, g * GC:(g + 1) * GC], t1[rows], t2[rows], op))
            store(dram_bb, mk_bb[:].rearrange("p a b c -> p (a b c)"))
            link(pool.memset(mk_zero[:], 0.0))
            store(dram_k.rearrange("(t p) c -> p t c", p=P)[:, :, 0:(L - 1) * GC], mk_zero[:])
            kept()
            assert stores[0] == MK_STORES

            pool.dma_start(s5_bb[:].rearrange("p a b c -> p (a b c)"), dram_bb).then_inc(bb_loaded, 16)
            dk = dram_k.rearrange("(t p) c -> p t c", p=P)
            n = KD // QUARTERS

            def load_c(q):
                for part in range(2):
                    pool.dma_start(s5_cq[:, q % 2, part, :, :],
                                   dram_c[:, part, q * PQ:(q + 1) * PQ, 0:L * GC]).then_inc(cq_loaded[q % 2], 16)

            load_c(0)
            load_c(1)
            for q in range(QUARTERS):
                pool.wait_ge(k_diag, n * (q + 1))
                pool.dma_start(dk[:, q * n:(q + 1) * n, (L - 1) * GC:], s5_k[:, q % 2, :, :]).then_inc(k_stored, 16)
                pool.wait_ge(k_stored, 16 * (q + 1))
                if q + 2 < QUARTERS:
                    load_c(q + 2)

            link(pool.iota(c_count[:].bitcast(I32), pattern=[[1, NC]], base=0, channel_multiplier=0))
            link(pool.tensor_copy(c_count[:], c_count[:].bitcast(I32)))
            link(pool.tensor_scalar(theta_hi[:], theta[:], ROUND_10, -ROUND_10, ALU.add, ALU.add))
            link(tt(theta_lo[:], theta[:], theta_hi[:], ALU.subtract))
            cc = c_count[:].unsqueeze(1).broadcast_to([P, PAIRS, NC])

            def over_chunks(a):
                return a[:].unsqueeze(2).broadcast_to([P, PAIRS, NC])

            link(tt(turn_s[:], cc, over_chunks(theta_hi), ALU.mult))
            link(tt(turn_c[:], cc, over_chunks(theta), ALU.mult))
            link(pool.tensor_scalar(turn_c[:], turn_c[:], 1.0 / TWO_PI, ROUND, ALU.mult, ALU.add))
            link(pool.tensor_scalar(turn_c[:], turn_c[:], -ROUND, None, ALU.add))
            link(pool.tensor_scalar(turn_t[:], turn_c[:], -TWO_PI_PARTS[0], None, ALU.mult))
            link(tt(turn_s[:], turn_s[:], turn_t[:], ALU.add))
            link(tt(turn_t[:], cc, over_chunks(theta_lo), ALU.mult))
            link(tt(turn_s[:], turn_s[:], turn_t[:], ALU.add))
            for part in TWO_PI_PARTS[1:]:
                link(pool.tensor_scalar(turn_t[:], turn_c[:], -part, None, ALU.mult))
                link(tt(turn_s[:], turn_s[:], turn_t[:], ALU.add))
            link(pool.tensor_scalar(turn_c[:], turn_s[:], TWO_PI / 4, None, ALU.add))
            link(pool.tensor_scalar(turn_t[:], turn_c[:], TWO_PI / 2, -TWO_PI, ALU.is_gt, ALU.mult))
            link(tt(turn_c[:], turn_c[:], turn_t[:], ALU.add))
            link(pool.tensor_scalar(turn_c[:], turn_c[:], PI_BELOW, -PI_BELOW, ALU.min, ALU.max))
            pool.tensor_scalar(turn_s[:], turn_s[:], PI_BELOW, -PI_BELOW, ALU.min, ALU.max).then_inc(turns_ready, 1)
            for part, turn in enumerate((turn_s, turn_c)):
                pool.wait_ge(sines_ready, part + 1)
                store(dram_sines[:, part, :], turn[:].rearrange("p a c -> p (a c)"))
            kept()
            early = GQ
            pool.dma_start(s5_bm[:, early:, :, :], dram_bm[:, early:, :, :]).then_inc(bm_loaded[0], 16)
            pool.wait_ge(hid_lo, 3 * HALVES * KF)
            pool.dma_start(s5_bm[:, 0:early, :, :], dram_bm[:, 0:early, :, :]).then_inc(bm_loaded[1], 16)
            first = next(s0 for k, _, _, s0 in phases if k == "mixer1")
            pool.wait_ge(slab_lo, split(first - 1))
            pool.dma_start(sines[:].rearrange("p w a c -> p w (a c)"), dram_sines).then_inc(sines_loaded, 16)
            pool.wait_ge(slab_used, used(first - 1))
            for q in range(QUARTERS):
                pool.wait_ge(u_loaded[q], 16 * L)
            dk = dram_k.rearrange("(g c) n -> c g n", c=GC)
            for j in range(L):
                pool.dma_start(s5_t[j * GC:(j + 1) * GC, :, :], dk[:, :, (L - 1 - j) * GC:(2 * L - 1 - j) * GC])\
                    .then_inc(t_loaded, 16)


def layouts(inputs):
    a = {k: np.asarray(v) for k, v in inputs.items()}
    d = a["x"].shape[2]
    groups, states, gc = a["s5_b_re"].shape[1:]
    pairs, kd = groups // 2, d // P

    def features(v):
        return v.reshape(-1, P).T

    per = pairs // kd

    def by_state(v):
        return v[0].reshape(kd, 2, per, states).transpose(1, 3, 0, 2).reshape(2 * states, pairs)

    def b_by_state(v):
        return v[0].reshape(kd, 2, per, states, gc).transpose(1, 3, 0, 2, 4).reshape(2 * states, pairs, gc)

    def b_by_channel(v):
        return v[0].reshape(kd, 2, per, states, gc).transpose(4, 0, 2, 1, 3).reshape(gc, groups * states)

    def c_by_state(v):
        return v[0].reshape(kd, 2, per, gc, states).transpose(1, 4, 0, 2, 3).reshape(2 * states, pairs, gc)

    return [
        ("x_t", a["x"][0].T), ("norm_g", a["norm_g"].reshape(-1, kd, P).transpose(2, 0, 1)),
        ("ffn_w_in", a["ffn_w_in"]), ("ffn_w_out", a["ffn_w_out"]),
        ("mix_w_in", a["mix_w_in"][0]), ("attn_sinks", a["attn_sinks"]), ("hgrn_lb", features(a["hgrn_lb"])),
        ("mix_w_out", a["mix_w_out"][0]),
        ("s5_a_re", by_state(a["s5_a_re"])), ("s5_a_im", by_state(a["s5_a_im"])),
        ("s5_log_step", a["s5_log_step"].reshape(kd, 2, per).transpose(1, 0, 2).reshape(2, pairs)),
        ("s5_b_re", b_by_state(a["s5_b_re"])), ("s5_b_im", b_by_state(a["s5_b_im"])),
        ("s5_bt_re", b_by_channel(a["s5_b_re"])), ("s5_bt_im", b_by_channel(a["s5_b_im"])),
        ("s5_c_re", c_by_state(a["s5_c_re"])), ("s5_c_im", c_by_state(a["s5_c_im"])),
        ("s5_d", a["s5_d"].reshape(kd, 2, per, gc).transpose(2, 1, 3, 0).reshape(P, kd)), ("s5_w_glu", a["s5_w_glu"][0]), ("final_g", features(a["final_g"])),
    ]


def kernel(**inputs):
    import concourse.bacc as bacc
    from concourse.bass_utils import run_bass_kernel_spmd

    nc = bacc.Bacc("TRN2", target_bir_lowering=False, num_devices=1)
    arrays, args = {}, []
    for name, v in layouts(inputs):
        v = np.ascontiguousarray(v)
        arrays[name] = v
        args.append(nc.dram_tensor(name, v.shape, mybir.dt.from_np(v.dtype), kind="ExternalInput").ap())
    tokens, d = np.asarray(inputs["x"]).shape[1:]
    args.append(nc.dram_tensor("out_t", (d, tokens), F32, kind="ExternalOutput").ap())
    trunk(nc, *args)
    r = run_bass_kernel_spmd(nc, [arrays], core_ids=[0])
    return np.ascontiguousarray(r.results[0]["out_t"].T)[None]
```

```python
from contextlib import ExitStack

import numpy as np

import concourse.bass as bass
from concourse import mybir

F32 = mybir.dt.float32
F32R = mybir.dt.float32r
I32 = mybir.dt.int32
ACT = mybir.ActivationFunctionType
ALU = mybir.AluOpType
AX = mybir.AxisListType

P = 128
EPS = 1e-6
RING = 4
LEAD = 2
CH = 32
MASKED = 1e30
POOL_CONSTS = 9
POOL_COUNT = 2
POOL_ALL = POOL_CONSTS + 2
S5_SMALL = (1, 0)
S5_KERNELS = (2, 0)
S5_SINES = (2, 1)
MK_STORES = 19
TWO_PI = 6.283185307179586
TWO_PI_PARTS = (6.28125, 0.001934051513671875, 1.2556659146e-06)
ROUND = 12582912.0
ROUND_10 = 12288.0
PI_BELOW = 3.1415925


def trunk(nc, x_t, norm_g, ffn_w_in, ffn_w_out, mix_w_in, attn_sinks, hgrn_lb, mix_w_out, s5_a_re, s5_a_im,
          s5_log_step, s5_b_re, s5_b_im, s5_bt_re, s5_bt_im, s5_c_re, s5_c_im, s5_d, s5_w_glu, final_g, out_t):
    D, T = x_t.shape
    F = ffn_w_out.shape[2]
    KD = D // P
    NT = T // P
    HALVES = 2
    KF = F // P // HALVES
    SLAB_IN, SLAB_OUT = KD * P, KF * P
    SLAB = max(SLAB_IN, SLAB_OUT)
    HEADS = attn_sinks.shape[1]
    AD = 64
    AT = HEADS * AD // P
    BH = hgrn_lb.shape[1]
    KV_W = 2 * AD
    COL_K, COL_V = HEADS * AD, HEADS * AD + KV_W
    COL_BQ = HEADS * AD + 2 * KV_W
    COL_BF, COL_BI, COL_BG = COL_BQ + BH * P, COL_BQ + 2 * BH * P, COL_BQ + 3 * BH * P
    NCH = T // CH
    CPT = P // CH
    NORMS = [0, 2, 3, 5]
    NORM_MIX, NORM_S5, NORM_FIN = 1, 4, 6
    SPLIT_NORMS = [0, 1, 2, 3, 5]

    PAIRS = s5_a_re.shape[1]
    NS = P // 2
    GC = s5_bt_re.shape[0]
    G = 2 * PAIRS
    L = P // GC
    NC = T // L
    PPB = 512 // NC
    PER = PAIRS // KD

    KIB = 1024
    o_x = 16640
    o_xg = o_x + KD * T * 4
    o_h = o_xg + 2 * KD * T * 4
    o_ring = o_h + 2 * KF * T * 4
    o_norm = o_ring + 3 * RING * SLAB * 4
    o_const = o_norm + 4 * T * 4
    o_tmp = o_const + 7808
    o_free = o_tmp + 4 * T * 4
    o_end = 229368

    with ExitStack() as ctx:
        def at(name, shape, offset, dt=F32):
            n = 4
            for d in shape[1:]:
                n *= d
            assert offset + n <= o_end, (name, offset + n)
            return nc.alloc_sbuf_tensor_at(name, shape, dt, offset=offset), offset + -(-n // 32) * 32

        def sem(name):
            return ctx.enter_context(nc.semaphore(name))

        x, _ = at("x", [P, KD, T], o_x)
        xg_hi, o = at("xg_hi", [P, KD, T], o_xg, F32R)
        xg_lo, _ = at("xg_lo", [P, KD, T], o, F32R)
        h_hi, o = at("h_hi", [P, KF, T], o_h, F32R)
        h_lo, _ = at("h_lo", [P, KF, T], o, F32R)
        raw, o = at("raw", [P, RING, SLAB], o_ring)
        w_hi, o = at("w_hi", [P, RING, SLAB], o, F32R)
        w_lo, _ = at("w_lo", [P, RING, SLAB], o, F32R)
        gate_r, o = at("gate_r", [P, T], o_tmp)
        silu_g, o = at("silu_g", [P, T], o)
        up_s, o = at("up_s", [P, T], o)
        hid, _ = at("hid", [P, T], o)
        sq, o = at("sq", [P, T], o_norm)
        ssq, o = at("ssq", [P, T], o)
        rms, o = at("rms", [P, T], o)
        rinv, _ = at("rinv", [P, T], o)
        ones, o = at("ones", [P, P], o_const)
        ident, o = at("ident", [P, P], o)
        causal, o = at("causal", [P, P], o)
        dist, o = at("dist", [P, 2 * P], o)
        dist_i, _ = at("dist_i", [P, 2 * P], o_tmp, I32)
        g_all, o = at("g_all", [P, 7, KD], o)
        sink, o = at("sink", [P, HEADS], o)
        sink_neg, o = at("sink_neg", [P, HEADS], o)
        lb_in, o = at("lb_in", [P, BH], o)
        lb, o = at("lb", [P, BH], o)
        lb_c, o = at("lb_c", [P, BH], o)
        r_col, o = at("r_col", [P, NT], o)
        max_neg, o = at("max_neg", [P, 2, 2], o)
        sink_d, o = at("sink_d", [P, 2, 2], o)
        sink_e, o = at("sink_e", [P, 2, 2], o)
        rowsum, o = at("rowsum", [P, 2, 2], o)
        den, o = at("den", [P, 2, 2], o)
        rden, o = at("rden", [P, 2, 2], o)
        o_ss, o = at("o_ss", [P, 2, NT], o)
        decay, o = at("decay", [P, BH, NCH], o)
        pow_r, o = at("pow_r", [P, L + 1, PAIRS], o)
        pow_i, o = at("pow_i", [P, L + 1, PAIRS], o)
        theta, o = at("theta", [P, PAIRS], o)
        rho, o = at("rho", [P, PAIRS], o)
        coef, o = at("coef", [P, 2, PAIRS], o)
        d_col, o = at("d_col", [P, KD], o)
        diag, o = at("diag", [P, GC], o)
        r_sel, o = at("r_sel", [1, (2 * L - 1) * GC], o)
        r_row, o = at("r_row", [P, NC], o)
        assert o <= o_tmp, o - o_const
        b_k, o = at("b_k", [P, BH, T], o_h)
        b_cum, o = at("b_cum", [P, BH, T], o)
        b_q, o = at("b_q", [P, BH, T], o)
        b_g, o = at("b_g", [P, BH, T], o)
        att_h, o = at("att_h", [P, AT, T], o, F32R)
        b_tmp, o = at("b_tmp", [P, 2, T], o_ring - 2 * T * 4)
        assert o <= o_ring
        b_e, _ = at("b_e", [P, 2, T], o_ring - 2 * T * 4)
        b_kinv, _ = at("b_kinv", [P, 2, T], o_norm + 2 * T * 4)
        square_out, _ = at("square_out", [P, P], o_free + NT * BH * P * 4)
        rec_l, _ = at("rec_l", [P, BH, T], o_h, F32R)
        rec_h, _ = at("rec_h", [P, BH, T], o_h + BH * T * 4, F32R)
        b_v, o = at("b_v", [P, NT, BH * P], o_free)
        a_q, o = at("a_q", [P, AT, T], o)
        att_l, o = at("att_l", [P, AT, T], o, F32R)
        a_v, o = at("a_v", [P, NT, KV_W], o)
        a_k, _ = at("a_k", [P, T], o_norm)
        carry, _ = at("carry", [P, T], o_norm + T * 4)
        prob, _ = at("prob", [P, 2, 2, 2 * P], o_tmp)
        prob_t, _ = at("prob_t", [P, 2, 2, 2, P], o_tmp + 2 * T * 4)
        o_norm_h, _ = at("o_norm_h", [P, 2, NT, P], o_tmp)
        rec, _ = at("rec", [P, 2, T], o_tmp + 2 * T * 4)
        k_end, o = at("k_end", [P, 2, NT, P], o_xg)
        scores, o = at("scores", [P, 2, NT, P], o)
        states, o = at("states", [P, 2, NCH, P], o)
        late_e, o = at("late_e", [P, 2, T], o)
        late_kinv, o = at("late_kinv", [P, 2, T], o)
        assert o <= o_h

        QUARTERS = 4
        GQ = G // QUARTERS
        PQ = PAIRS // QUARTERS
        o = o_free
        tiny = {}
        for name in ["lam_r", "lam_i", "log_dt", "den_l", "num_a", "num_b", "abr1"]:
            tiny[name], o = at("s5_" + name, [P, PAIRS], o)
        for name in ["angle", "turns", "angle_c", "fold", "mag"]:
            tiny[name], o = at("s5_" + name, [P, L + 1, PAIRS], o)
        k_count, o = at("k_count", [P, L + 1], o)
        for name in ["w_r", "w_i", "w_t"]:
            tiny[name], o = at("s5_" + name, [P, L, PAIRS], o)
        w_rows, _ = at("w_rows", [P, 4, P], o)
        o = o_free
        mk = {}
        mk_w, o = at("mk_w", [P, 2, GQ * NS], o)
        for name in ["br", "bi", "t1", "t2"]:
            mk[name], o = at("mk_" + name, [P, GQ * NS], o)
        o = o_free
        mk_c, o = at("mk_c", [P, 2, PQ, (L + 1) * GC], o)
        for name in ["cr", "ci", "ncr"]:
            mk[name], o = at("mk_" + name, [P, PAIRS, GC], o)
        for name in ["u1", "u2"]:
            mk[name], o = at("mk_" + name, [P, PQ, (L + 1) * GC], o)
        mk_bb, _ = at("mk_bb", [P, PAIRS, 2, 2 * GC], o_free + 12 * KIB)
        mk["sr"], o = at("mk_sr", [P, PAIRS, GC], o_free)
        mk["si"], o = at("mk_si", [P, PAIRS, GC], o)
        mk["s1"], o = at("mk_s1", [P, PAIRS, GC], o)
        mk["s2"], o = at("mk_s2", [P, PAIRS, GC], o)
        mk_zero, _ = at("mk_zero", [P, KD, (L - 1) * GC], o_free + 20 * KIB)
        s5_bb, o = at("s5_bb", [P, PAIRS, 2, 2 * GC], o_free)
        s5_cq, o = at("s5_cq", [P, 2, 2, PQ, L * GC], o)
        s5_k, _ = at("s5_k", [P, 2, KD // QUARTERS, L * GC], o)
        o = o_free
        turn_s, o = at("turn_s", [P, PAIRS, NC], o)
        turn_c, o = at("turn_c", [P, PAIRS, NC], o)
        turn_t, o = at("turn_t", [P, PAIRS, NC], o)
        c_count, o = at("c_count", [P, NC], o)
        theta_hi, o = at("theta_hi", [P, PAIRS], o)
        theta_lo, o = at("theta_lo", [P, PAIRS], o)
        s5_bm, _ = at("s5_bm", [P, G, 2, NS], o_tmp)
        s5_c, _ = at("s5_c", [P, PAIRS, 2, L * GC], o_tmp)
        s5_t, o = at("s5_t", [P, G, P], o_h)
        rot = []
        for name in "abc":
            r, o = at("rot_" + name, [P, 2, PPB * NC], o)
            rot.append(r)
        assert o <= o_ring
        turned, _ = at("turned", [P, 2, 2, PPB * NC], o_ring + RING * SLAB * 4)
        y_hi, o = at("y_hi", [P, KD, T], o_h, F32R)
        y_lo, o = at("y_lo", [P, KD, T], o, F32R)
        sig, o = at("sig", [P, 2, T], o)
        glu, o = at("glu", [P, 2, T], o)
        assert o <= o_ring
        s5_xg, _ = at("s5_xg", [P, KD, T], o_xg)
        s5_y, _ = at("s5_y", [P, KD, L, PER * GC], o_xg)
        s5_u, _ = at("s5_u", [P, G, NC], o_xg + KD * T * 4)
        sines, o = at("sines", [P, 2, PAIRS, NC], o_ring)
        decays, o = at("decays", [P, 2, PPB, NC], o)
        assert o <= o_ring + RING * SLAB * 4
        s5_x, o = at("s5_x", [P, 2, PAIRS, NC], o_ring + 2 * RING * SLAB * 4)
        assert o <= o_norm

        def dram(name, *shape):
            return nc.dram_tensor(name, shape, F32).ap()

        dram_w = dram("dram_w", 2, L, G, NS)
        dram_bm = dram("dram_bm", P, G, 2, NS)
        dram_c = dram("dram_c", P, 2, PAIRS, (L + 1) * GC)
        dram_bb = dram("dram_bb", P, PAIRS * 2 * 2 * GC)
        dram_k = dram("dram_k", D, (2 * L - 1) * GC)
        dram_u = dram("dram_u", D, T)
        dram_sines = dram("dram_sines", P, 2, PAIRS * NC)

        bank = [ctx.enter_context(nc.psum_tensor(f"bank{i}", [P, 512], F32)) for i in range(8)]
        gate_ps, up_ps, out_ps, norm_ps = bank[0:2], bank[2:4], bank[4:6], bank[6]

        const_loaded = sem("const_loaded")
        s5_count = sem("s5_count")
        small_loaded = sem("small_loaded")
        x_loaded = [sem(f"x_loaded{k}") for k in range(KD)]
        ones_set = sem("ones_set")
        pool_const = sem("pool_const")
        slab_loaded = [sem(f"slab_loaded{i}") for i in range(RING)]
        slab_hi = sem("slab_hi")
        slab_lo = sem("slab_lo")
        slab_used = sem("slab_used")
        gate_scaled = sem("gate_scaled")
        silu_ready = sem("silu_ready")
        banks_free = sem("banks_free")
        hid_ready = sem("hid_ready")
        hid_hi = sem("hid_hi")
        hid_lo = sem("hid_lo")
        x_half = sem("x_half")
        x_ready = sem("x_ready")
        xg_hi_ready = sem("xg_hi_ready")
        xg_lo_ready = sem("xg_lo_ready")
        sq_ready = sem("sq_ready")
        ssq_ready = sem("ssq_ready")
        norm_sum = sem("norm_sum")
        mean_ready = sem("mean_ready")
        rms_ready = sem("rms_ready")
        rinv_ready = sem("rinv_ready")
        stored = sem("stored")
        fin_ready = sem("fin_ready")
        dve_step = sem("dve_step")
        act_step = sem("act_step")
        lb_exp = sem("lb_exp")
        col_ready = sem("col_ready")
        col_taken = sem("col_taken")
        proj_scaled = sem("proj_scaled")
        nat_taken = sem("nat_taken")
        v_ready = sem("v_ready")
        sig_ready = sem("sig_ready")
        sig_used = sem("sig_used")
        f_one = sem("f_one")
        f_ready = sem("f_ready")
        logf_ready = sem("logf_ready")
        cum_ready = sem("cum_ready")
        exp_ready = sem("exp_ready")
        exp_used = sem("exp_used")
        b_ready = sem("b_ready")
        sc_ready = sem("sc_ready")
        sc_masked = sem("sc_masked")
        kt_ready = sem("kt_ready")
        kt_taken = sem("kt_taken")
        kv_ready = sem("kv_ready")
        state_ready = sem("state_ready")
        inter_done = sem("inter_done")
        o_scaled = sem("o_scaled")
        ot_ready = sem("ot_ready")
        qdec_ready = sem("qdec_ready")
        rest_ready = sem("rest_ready")
        rest_exp = sem("rest_exp")
        zeroed = sem("zeroed")
        decay_ready = sem("decay_ready")
        o_sq = sem("o_sq")
        o_mean = sem("o_mean")
        o_rms = sem("o_rms")
        rec_ready = sem("rec_ready")
        mix_hi = sem("mix_hi")
        mix_lo = sem("mix_lo")
        s_ready = sem("s_ready")
        s_taken = sem("s_taken")
        m_ready = sem("m_ready")
        p_exp = sem("p_exp")
        p_ready = sem("p_ready")
        pt_ready = sem("pt_ready")
        pt_taken = sem("pt_taken")
        pv_done = sem("pv_done")
        att_hi = sem("att_hi")
        att_lo = sem("att_lo")

        s5_loaded = sem("s5_loaded")
        d_loaded = sem("d_loaded")
        s5_dt = sem("s5_dt")
        s5_angles = sem("s5_angles")
        s5_trig = sem("s5_trig")
        s5_w_ready = sem("s5_w_ready")
        s5_w_turned = sem("s5_w_turned")
        s5_w_rows = sem("s5_w_rows")
        s5_w_stored = sem("s5_w_stored")
        mk_loaded = sem("mk_loaded")
        mk_stored = sem("mk_stored")
        pool_step = sem("pool_step")
        bb_loaded = sem("bb_loaded")
        cq_loaded = [sem(f"cq_loaded{i}") for i in range(2)]
        c_loaded = [sem(f"c_loaded{q}") for q in range(QUARTERS)]
        turns_ready = sem("turns_ready")
        sines_ready = sem("sines_ready")
        sines_loaded = sem("sines_loaded")
        decays_ready = sem("decays_ready")
        k_summed = sem("k_summed")
        k_ready = sem("k_ready")
        k_diag = sem("k_diag")
        k_stored = sem("k_stored")
        bm_loaded = [sem(f"bm_loaded{i}") for i in range(2)]
        t_loaded = sem("t_loaded")
        u_tile = sem("u_tile")
        u_stored = sem("u_stored")
        u_loaded = [sem(f"u_loaded{q}") for q in range(PAIRS // PPB)]
        row_ready = sem("row_ready")
        row_taken = sem("row_taken")
        u_ready = [sem(f"u_ready{q}") for q in range(QUARTERS)]
        x_zeroed = sem("x_zeroed")
        rotated = sem("rotated")
        st_ready = sem("st_ready")
        st_taken = sem("st_taken")
        scanned = sem("scanned")
        x_scanned = sem("x_scanned")
        y_ready = sem("y_ready")
        y_taken_a = sem("y_taken_a")
        y_taken_d = sem("y_taken_d")
        yt_ready = sem("yt_ready")
        gelu_ready = sem("gelu_ready")
        y_hi_ready = sem("y_hi_ready")
        y_lo_ready = sem("y_lo_ready")
        glu_sig = sem("glu_sig")
        glu_mul = sem("glu_mul")

        phases = []
        sizes = []

        def phase(kind, f=0, half=0, count=0, size=0):
            phases.append((kind, f, half, len(sizes)))
            sizes.extend([size] * count)

        def swiglu(f):
            for half in range(HALVES):
                phase("in", f, half, 2 * KF, SLAB_IN)
                phase("out", f, half, KD, SLAB_OUT)

        MIX_COLS = [COL_BF + i * P for i in range(BH)] + [COL_BQ + i * P for i in range(BH)] \
            + [COL_BG + i * P for i in range(BH)] + [COL_BI + i * P for i in range(BH)]
        swiglu(0)
        phase("mixer0", count=len(MIX_COLS) + AT + 2, size=SLAB_IN)
        phase("mixer0_out", count=KD, size=KD * P)
        swiglu(1)
        swiglu(2)
        phase("mixer1", count=2 * KD, size=SLAB_IN)
        swiglu(3)
        total = len(sizes)

        w_in = [ffn_w_in[f // 2, f % 2].rearrange("(k p) c -> p k c", p=P) for f in range(4)]
        w_out = [ffn_w_out[f // 2, f % 2].rearrange("(k p) c -> p k c", p=P) for f in range(4)]
        w_glu = s5_w_glu.rearrange("(k p) c -> p k c", p=P)
        w_mix = mix_w_in.rearrange("(k p) c -> p k c", p=P)
        w_mix_out = mix_w_out.rearrange("(k p) c -> p k c", p=P)

        late = [s0 + i for kind, _, _, s0 in phases if kind == "mixer1" for i in range(LEAD)]

        def group(pair, g):
            return 2 * PER * (pair // PER) + PER * g + pair % PER

        def scale_u(engine, q):
            n = 2 * PPB
            engine.wait_ge(u_loaded[q], 16 * L)
            u = s5_u[:, q * n:(q + 1) * n, :]
            engine.tensor_tensor(u, u, r_row[:].unsqueeze(1).broadcast_to([P, n, NC]), ALU.mult)\
                  .then_inc(u_ready[q], 1)

        def exps(h):
            return (b_e, b_kinv) if h < 2 else (late_e, late_kinv)

        def y_bank(k):
            return bank[k // 2 + QUARTERS * (k % 2)]

        def slot(s):
            return s % RING

        def arrived(s, per=1):
            return 16 * (s // RING + 1)

        def split(s):
            return RING + s + 1

        def used(s):
            return RING + s + 1

        def xg_count(n, k):
            return SPLIT_NORMS.index(n) * KD + k + 1

        STEPS = 4 * BH
        UNITS = [(n, tp, g) for n in range(NT) for tp in range(AT // 2) for g in range(2)]
        SLOPES = [2.0 ** (-8.0 * (h + 1) / HEADS) for h in range(HEADS)]

        def taken(v):
            return sum(2 if n else 1 for n, _, _ in UNITS[:v + 1])

        block = ctx.enter_context(nc.Block())

        @block.sync
        def _(sp):
            def load(s, src, n, turn=0):
                sp.wait_ge(slab_lo, s + 1 + turn)
                sp.dma_start(raw[:, slot(s), 0:n * P].rearrange("p (k c) -> p k c", c=P), src)\
                  .then_inc(slab_loaded[slot(s)], 16)

            for kind, f, half, s0 in phases:
                if kind == "in":
                    def tile(t, i=0):
                        for part in range(2):
                            c = part * F + (half * KF + t) * P
                            load(s0 + 2 * t + part, w_in[f][:, :, bass.ds(c + i * 2 * P, P)], KD, i * RING)
                            if s0 + t + part == 0:
                                for k in range(KD):
                                    sp.dma_start(x[:, k, :], x_t[k * P:(k + 1) * P, :]).then_inc(x_loaded[k], 16)

                    tile(0)
                    with sp.Fori(0, KF // 2) as i:
                        tile(1, i)
                        tile(2, i)
                elif kind == "out":
                    with sp.Fori(0, KD // RING) as i:
                        for d in range(RING):
                            load(s0 + d, w_out[f][:, half * KF:(half + 1) * KF, bass.ds(d * P + i * RING * P, P)],
                                 KF, i * RING)
                elif kind == "mixer0":
                    s = s0
                    for t in range(AT):
                        sp.wait_ge(slab_lo, s + t + 1)
                        for g in range(2):
                            c = (t + g * AT) * AD
                            sp.dma_start(raw[:, slot(s + t), 0:SLAB_IN].rearrange("p (k c) -> p k c", c=P)
                                         [:, :, g * AD:(g + 1) * AD], w_mix[:, :, c:c + AD])\
                              .then_inc(slab_loaded[slot(s + t)], 8 * 2 if g else 16)
                    load(s + AT, w_mix[:, :, COL_K:COL_K + P], KD)
                    load(s + AT + 1, w_mix[:, :, COL_V:COL_V + P], KD)
                    for n, c in enumerate(MIX_COLS):
                        load(s + AT + 2 + n, w_mix[:, :, c:c + P], KD)
                elif kind == "mixer0_out":
                    for d in range(KD):
                        s = s0 + d
                        sp.wait_ge(slab_lo, s + 1)
                        dst = raw[:, slot(s), 0:SLAB_IN].rearrange("p (k c) -> p k c", c=P)
                        for g in range(2):
                            sp.dma_start(dst[g * AD:(g + 1) * AD, 0:AT, :],
                                         mix_w_out[g * AT * AD:(g + 1) * AT * AD, d * P:(d + 1) * P]
                                         .rearrange("(t r) c -> r t c", r=AD)).then_inc(slab_loaded[slot(s)], 16)
                        sp.dma_start(dst[:, AT:KD, :], w_mix_out[:, AT:KD, d * P:(d + 1) * P])\
                          .then_inc(slab_loaded[slot(s)], 16)
                elif kind == "mixer1":
                    def glu_slab(n):
                        c = (n % 2) * D + n // 2 * P
                        load(s0 + n, w_glu[:, :, c:c + P], KD)

                    du = dram_u.rearrange("(g c) (j t) -> j c g t", c=GC, t=NC)
                    gq = 2 * PPB
                    for k in range(KD):
                        sp.wait_ge(u_tile, k + 1)
                        sp.dma_start(dram_u[k * P:(k + 1) * P, :], s5_xg[:, k, :]).then_inc(u_stored, 16)
                        if k % 2 == 1:
                            q = k // 2
                            sp.wait_ge(u_stored, 16 * (k + 1))
                            for j in range(L):
                                sp.dma_start(s5_u[j * GC:(j + 1) * GC, q * gq:(q + 1) * gq, :],
                                             du[j][:, q * gq:(q + 1) * gq, :]).then_inc(u_loaded[q], 16)
                    for q in range(QUARTERS):
                        sp.wait_ge(st_ready, q + 1)
                        for part in range(2):
                            sp.dma_start(s5_c[:, q * PQ:(q + 1) * PQ, part, :],
                                         dram_c[:, part, q * PQ:(q + 1) * PQ, GC:]).then_inc(c_loaded[q], 16)
                    sp.wait_ge(scanned, 2 * QUARTERS)
                    for n in range(2 * KD):
                        glu_slab(n)
            for k in range(KD):
                sp.wait_ge(fin_ready, k + 1)
                sp.dma_start(out_t[k * P:(k + 1) * P, :], x[:, k, :]).then_inc(stored, 16)
            sp.wait_ge(stored, 16 * KD)

        parts = [1] * total
        for kind, f, half, s0 in phases:
            if kind == "mixer0":
                for t in range(AT):
                    parts[s0 + t] = 2
            if kind == "mixer0_out":
                for d in range(KD):
                    parts[s0 + d] = 3

        def in_ring(s):
            return 16 * sum(parts[slot(s):s + 1:RING])

        @block.scalar
        def _(act):
            steps = [0]

            def split_hi(s, n, i=0):
                act.wait_ge(slab_loaded[slot(s)], in_ring(s) + i * 16)
                act.wait_ge(slab_used, s + 1 + i * RING)
                act.activation(w_hi[:, slot(s), 0:n], raw[:, slot(s), 0:n], ACT.Copy).then_inc(slab_hi, 1)

            def split_ahead(s, count):
                for q in range(s + LEAD, min(s + LEAD + count, total)):
                    if q not in late:
                        split_hi(q, sizes[q])

            def norm_tile(n, k):
                if n:
                    act.wait_ge(x_ready, (n - 1) * KD + k + 1)
                if n == NORM_S5:
                    act.activation(s5_xg[:, k, :].rearrange("p (j c) -> p j c", j=L),
                                   x[:, k, :].rearrange("p (c j) -> p j c", j=L), ACT.Copy,
                                   scale=g_all[:, n, k:k + 1]).then_inc(u_tile, 1)
                if n in SPLIT_NORMS:
                    act.activation(xg_hi[:, k, :], x[:, k, :], ACT.Copy, scale=g_all[:, n, k:k + 1])\
                       .then_inc(xg_hi_ready, 1)
                if n:
                    norm_square(n, k)

            def norm_square(n, k):
                if n == 0:
                    if k >= 2:
                        act.wait_ge(ssq_ready, k - 1)
                else:
                    act.wait_ge(ssq_ready, n * KD + k)
                act.activation((sq if n or k % 2 == 0 else hid)[:], x[:, k, :], ACT.Square).then_inc(sq_ready, 1)

            def norm_root(n):
                if n == NORM_S5:
                    act.wait_ge(row_ready, 1)
                    act.activation(r_row[:], bank[7][:, 0:NC], ACT.Sqrt).then_inc(rms_ready, 1)
                    return
                act.wait_ge(mean_ready, n + 1)
                act.activation(rms[:], rms[:], ACT.Sqrt).then_inc(rms_ready, 1)

            def hidden(t, hi, i=0):
                act.wait_ge(gate_scaled, t + 1 + i)
                act.activation(silu_g[:], gate_r[:], ACT.Silu).then_inc(silu_ready, 1)
                act.wait_ge(hid_ready, t + 1 + i)
                act.activation(hi, hid[:], ACT.Copy).then_inc(hid_hi, 1)

            def attention(u):
                if u < len(UNITS):
                    n, tp, g = UNITS[u]
                    k0 = 0 if n else P
                    act.wait_ge(m_ready, u + 1)
                    for j in range(2):
                        act.activation(prob[:, u % 2, j, k0:], prob[:, u % 2, j, k0:], ACT.Exp,
                                       bias=max_neg[:, u % 2, j:j + 1], accum_out=rowsum[:, u % 2, j:j + 1])\
                           .then_inc(p_exp, 1)
                    act.activation(sink_e[:, u % 2, :], sink_d[:, u % 2, :], ACT.Exp).then_inc(p_exp, 1)
                if 1 <= u <= len(UNITS):
                    v = u - 1
                    n = UNITS[v][0]
                    act.wait_ge(pt_ready, v + 1)
                    if v >= 2:
                        act.wait_ge(pv_done, v - 1)
                    for kt in range(0 if n else 1, 2):
                        act.activation(prob_t[:, v % 2, :, kt, :],
                                       bank[2 + v % 2][:].rearrange("p (j k q) -> p j k q", j=2, k=2)[:, :, kt, :],
                                       ACT.Copy).then_inc(pt_taken, 1)
                if u >= 2 and (u - 2) % 4 == 3:
                    n = (u - 2) // 4
                    act.wait_ge(pv_done, 4 * (n + 1))
                    act.activation(att_h[:, :, n * P:(n + 1) * P],
                                   bank[4 + n % 2][:].rearrange("p (t q) -> p t q", q=P), ACT.Copy).then_inc(att_hi, 1)

            def mixer0(s0):
                split_ahead(s0, 2)
                norm_root(NORM_MIX)
                for n in range(2, AT + 2):
                    split_ahead(s0 + n, 1)
                act.wait_ge(slab_used, used(s0 + AT + 1))
                act.wait_ge(col_taken, 1)
                for m in range(NT):
                    act.activation(a_v[:, m, :], bank[4][:, m * P:(m + 1) * P], ACT.Copy,
                                   scale=r_col[:, m:m + 1]).then_inc(nat_taken, 1)
                def prepare(h):
                    if h == 0:
                        act.wait_ge(cum_ready, BH)
                        act.wait_ge(sig_used, 2 * BH)
                    if h:
                        act.wait_ge(qdec_ready, h)
                        act.wait_ge(rest_ready, h)
                    if h == 2:
                        act.wait_ge(v_ready, STEPS - 3 * BH)
                    e, _ = exps(h)
                    act.activation(e[:, 0, :], b_cum[:, h, :], ACT.Exp).then_inc(exp_ready, 1)
                    act.activation(e[:, 1, :], b_cum[:, h, :], ACT.Exp, scale=-1.0).then_inc(exp_ready, 1)
                    act.wait_ge(rest_ready, h + 1)
                    act.activation(b_cum[:, h, :], b_cum[:, h, :], ACT.Exp).then_inc(rest_exp, 1)

                s = s0 + AT + 2
                for n in range(STEPS):
                    split_ahead(s + n, 1)
                    if n < 3 * BH:
                        act.wait_ge(proj_scaled, AT + 1 + n + 1)
                        if n < BH:
                            src, dst = b_tmp[:, n % 2, :], b_k[:, n, :]
                        else:
                            src, dst = (b_q, b_g)[n // BH - 1][:, n % BH, :], b_tmp[:, n % 2, :]
                            if n >= BH + 2:
                                act.wait_ge(sig_used, n - BH - 1)
                        act.activation(dst, src, ACT.Sigmoid).then_inc(sig_ready, 1)
                    else:
                        pair, half = (n - 3 * BH) // 2, n % 2
                        act.wait_ge(v_ready, n - 3 * BH + 1)
                        for i in range(2):
                            act.activation(b_v[:, 2 * half + i, 2 * pair * P:2 * (pair + 1) * P],
                                           bank[6 + half][:, i * 2 * P:(i + 1) * 2 * P], ACT.Copy,
                                           scale=r_col[:, 2 * half + i:2 * half + i + 1]).then_inc(nat_taken, 1)
                    attention(n)
                    if n == BH + 1:
                        act.wait_ge(f_ready, BH)
                        act.activation(b_cum[:], b_k[:], ACT.Ln).then_inc(logf_ready, 1)
                    if n in (STEPS - 3, STEPS - 2):
                        prepare(n - STEPS + 3)


                def keys(h):
                    act.wait_ge(kt_ready, h + 1)
                    if h >= 2:
                        act.wait_ge(kv_ready, h - 1)
                    act.activation(k_end[:, h % 2, :, :], bank[1][:].rearrange("p (m d) -> p m d", d=P), ACT.Copy)\
                       .then_inc(kt_taken, 1)

                def high(h):
                    act.wait_ge(rec_ready, h + 1)
                    act.activation(rec_h[:, h, :], rec[:, h % 2, :], ACT.Copy).then_inc(mix_hi, 1)

                attention(STEPS)
                keys(0)
                attention(STEPS + 1)
                prepare(2)
                for h in range(BH):
                    if h + 1 < BH:
                        keys(h + 1)
                    if h + 3 < BH:
                        prepare(h + 3)
                    act.wait_ge(inter_done, h + 1)
                    if h >= 2:
                        act.wait_ge(o_scaled, h - 1)
                    for m in range(NT):
                        if h * NT + m:
                            act.wait_ge(o_sq, h * NT + m)
                        act.activation(square_out[:], bank[2 + h % 2][:, m * P:(m + 1) * P], ACT.Square,
                                       accum_out=o_ss[:, h % 2, m:m + 1]).then_inc(o_sq, 1)
                    act.wait_ge(o_mean, h + 1)
                    act.activation(o_ss[:, h % 2, :], o_ss[:, h % 2, :], ACT.Sqrt).then_inc(o_rms, 1)
                    if h:
                        high(h - 1)
                high(BH - 1)

            def mixer1(s0):
                act.wait_ge(k_stored, 16 * QUARTERS)
                act.wait_ge(slab_used, used(s0 - 1))
                for q in range(QUARTERS):
                    act.wait_ge(u_loaded[q], 16 * L)
                dk = dram_k.rearrange("(g c) n -> c g n", c=GC)
                for j in range(L):
                    act.dma_start(s5_t[j * GC:(j + 1) * GC, :, :], dk[:, :, (L - 1 - j) * GC:(2 * L - 1 - j) * GC])\
                        .then_inc(t_loaded, 16)
                for q in range(QUARTERS):
                    if q == 0:
                        act.wait_ge(decays_ready, 1)
                    if q >= 2:
                        act.wait_ge(x_scanned, q - 1)
                    act.activation(decays[:, q % 2, :, 1:], rho[:, q * PQ:(q + 1) * PQ].unsqueeze(2)
                                   .broadcast_to([P, PQ, NC - 1]), ACT.Copy).then_inc(decays_ready, 1)

                def y_half(q):
                    act.wait_ge(y_ready, 2 * q + 1)
                    act.activation(s5_y[:, 2 * q, :, :].rearrange("p j (a c) -> p a j c", c=GC),
                                   y_bank(2 * q)[:].rearrange("p (a j c) -> p a j c", j=L, c=GC), ACT.Copy)\
                       .then_inc(y_taken_a, 1)

                def y_gelu(k):
                    act.wait_ge(yt_ready, k + 1)
                    if k >= 2:
                        act.wait_ge(y_lo_ready, k - 1)
                    gelu = (sq, ssq)[k % 2]
                    act.activation(gelu[:], y_bank(k)[:], ACT.Gelu_apprx_tanh).then_inc(gelu_ready, 1)
                    act.wait_ge(gelu_ready, k + 1)
                    act.activation(y_hi[:, k, :], gelu[:], ACT.Copy).then_inc(y_hi_ready, 1)

                y_half(0)
                for q in range(1, QUARTERS):
                    y_half(q)
                    y_gelu(2 * q - 2)
                    y_gelu(2 * q - 1)
                    if q == QUARTERS - 2:
                        act.wait_ge(scanned, 2 * QUARTERS)
                        for s in late:
                            split_hi(s, sizes[s])
                y_gelu(KD - 2)
                y_gelu(KD - 1)
                for d in range(KD):
                    split_ahead(s0 + 2 * d, 2)
                    act.wait_ge(slab_used, used(s0 + 2 * d + 1))
                    if d >= 2:
                        act.wait_ge(glu_mul, d - 1)
                    act.activation(sig[:, d % 2, :], up_ps[d % 2][:], ACT.Sigmoid).then_inc(glu_sig, 1)
                    if d:
                        norm_tile(NORM_S5 + 1, d - 1)
                norm_tile(NORM_S5 + 1, KD - 1)

            def s5_part(d):
                if d == 0:
                    act.wait_ge(s5_loaded, 16 * 4)
                    act.activation(tiny["log_dt"][:], tiny["log_dt"][:], ACT.Exp).then_inc(s5_dt, 1)
                if d == 2:
                    act.wait_ge(s5_angles, 1)
                    act.activation(tiny["mag"][:], tiny["mag"][:], ACT.Exp).then_inc(s5_trig, 1)
                    act.activation(tiny["angle"][:], tiny["angle"][:], ACT.Sin).then_inc(s5_trig, 1)
                    act.activation(tiny["angle_c"][:], tiny["angle_c"][:], ACT.Sin).then_inc(s5_trig, 1)
                if d == KD - 1:
                    act.wait_ge(s5_w_turned, 1)
                    act.activation(w_rows[:], bank[7][:].rearrange("p (a c) -> p a c", c=P), ACT.Copy)\
                       .then_inc(s5_w_rows, 1)

            def k_out(q):
                act.wait_ge(k_summed, q + 1)
                if q >= 2:
                    act.wait_ge(k_stored, 16 * (q - 1))
                act.activation(s5_k[:, q % 2, :, :],
                               bank[7][:, 0:KD // QUARTERS * P].rearrange("p (t c) -> p t c", c=P), ACT.Copy)\
                   .then_inc(k_ready, 1)

            act.dma_start(g_all[:, 0:6, :], norm_g).then_inc(const_loaded, 16)
            act.dma_start(g_all[:, 6, :], final_g).then_inc(const_loaded, 16)
            split_hi(0, sizes[0])
            act.wait_ge(const_loaded, 32)
            for k in range(KD):
                act.wait_ge(x_loaded[k], 16)
                norm_tile(0, k)
            split_hi(1, sizes[1])
            act.dma_start(d_col[:], s5_d).then_inc(d_loaded, 16)
            act.dma_start(sink[:], attn_sinks[0].partition_broadcast(P)).then_inc(small_loaded, 16)
            act.dma_start(lb_in[:], hgrn_lb).then_inc(small_loaded, 16)
            for k in range(KD):
                norm_square(0, k)
            for kind, f, half, s0 in phases:
                if kind == "in":
                    t0 = (HALVES * f + half) * KF
                    split_ahead(s0, 2)
                    if half == 0:
                        norm_root(NORMS[f])
                    hidden(t0, h_hi[:, 0, :])
                    with act.Fori(0, KF // 2 - 1) as i:
                        for t in (1, 2):
                            for part in range(2):
                                split_hi(s0 + 2 * t + part + LEAD, SLAB_IN, i)
                            hidden(t0 + t, h_hi[:, bass.ds(i * 2 + t, 1), :].squeeze(1), i * 2)
                    for t in (KF - 2, KF - 1):
                        split_ahead(s0 + 2 * t, 2)
                        hidden(t0 + t, h_hi[:, t, :])
                elif kind == "out":
                    for d in range(KD):
                        split_ahead(s0 + d, 1)
                        if (f, half) == S5_SMALL:
                            s5_part(d)
                        if (f, half) == S5_KERNELS and d % 2 == 1:
                            k_out(d // 2)
                        if (f, half) == S5_SINES and d == 2:
                            act.wait_ge(turns_ready, 1)
                            act.activation(turn_s[:], turn_s[:], ACT.Sin).then_inc(sines_ready, 1)
                            act.activation(turn_c[:], turn_c[:], ACT.Sin).then_inc(sines_ready, 1)
                        if half == HALVES - 1:
                            norm_tile(NORMS[f] + 1, d)
                    if half == HALVES - 1 and NORMS[f] + 1 in (NORM_S5, NORM_FIN):
                        norm_root(NORMS[f] + 1)
                elif kind == "mixer1":
                    mixer1(s0)
                elif kind == "mixer0":
                    act.wait_ge(lb_exp, 1)
                    act.activation(lb[:], lb_c[:], ACT.Exp).then_inc(act_step, 1)
                    mixer0(s0)
                elif kind == "mixer0_out":
                    for d in range(KD):
                        split_ahead(s0 + d, 1)
                        norm_tile(NORM_MIX + 1, d)

        @block.vector
        def _(dve):
            count = [0]

            def step(ins):
                count[0] += 1
                ins.then_inc(dve_step, 1)
                dve.wait_ge(dve_step, count[0])

            def link(ins):
                count[0] += 1
                ins.then_inc(dve_step, 1)

            def settle():
                dve.wait_ge(dve_step, count[0])

            def split_lo(s, n, i=0):
                dve.wait_ge(slab_hi, s + 1 + i * RING)
                dve.tensor_tensor(w_lo[:, slot(s), 0:n], raw[:, slot(s), 0:n],
                                  w_hi[:, slot(s), 0:n].bitcast(F32), ALU.subtract).then_inc(slab_lo, 1)

            def split_ahead(s, count):
                for q in range(s + LEAD, min(s + LEAD + count, total)):
                    if q not in late:
                        split_lo(q, sizes[q])

            def norm_tile(n, k):
                if n in SPLIT_NORMS:
                    dve.wait_ge(xg_hi_ready, xg_count(n, k))
                    dve.scalar_tensor_tensor(out=xg_lo[:, k, :], in0=x[:, k, :], scalar=g_all[:, n, k:k + 1],
                                             in1=xg_hi[:, k, :].bitcast(F32), op0=ALU.mult,
                                             op1=ALU.subtract).then_inc(xg_lo_ready, 1)
                if n:
                    norm_square(n, k)

            def norm_square(n, k):
                sq_k = sq if n or k % 2 == 0 else hid
                dve.wait_ge(sq_ready, n * KD + k + 1)
                if k == 0:
                    if n:
                        dve.wait_ge(norm_sum, n)
                    dve.tensor_copy(ssq[:], sq_k[:]).then_inc(ssq_ready, 1)
                else:
                    dve.wait_ge(ssq_ready, n * KD + k)
                    dve.tensor_tensor(ssq[:], ssq[:], sq_k[:], ALU.add).then_inc(ssq_ready, 1)

            def norm_root(n):
                dve.wait_ge(norm_sum, n + 1)
                dve.tensor_scalar(rms[:], norm_ps[:], 1.0 / D, EPS, ALU.mult, ALU.add).then_inc(mean_ready, 1)
                if n == NORM_S5:
                    dve.wait_ge(rms_ready, n + 1)
                    dve.reciprocal(r_row[:], r_row[:]).then_inc(rinv_ready, 1)
                    dve.wait_ge(rinv_ready, n + 1)
                    return
                dve.wait_ge(rms_ready, n + 1)
                dve.reciprocal(rinv[:], rms[:]).then_inc(rinv_ready, 1)
                dve.wait_ge(rinv_ready, n + 1)

            def hidden(t, s, b, hi, lo, i=0, turn=0):
                dve.wait_ge(slab_used, used(s) + turn)
                dve.tensor_tensor(gate_r[:], gate_ps[b][:], rinv[:], ALU.mult).then_inc(gate_scaled, 1)
                dve.wait_ge(slab_used, used(s + 1) + turn)
                dve.wait_ge(silu_ready, t + 1 + i)
                dve.tensor_tensor(up_s[:], up_ps[b][:], silu_g[:], ALU.mult).then_inc(banks_free, 1)
                dve.wait_ge(banks_free, 2 + t + 1 + i)
                dve.tensor_tensor(hid[:], up_s[:], rinv[:], ALU.mult).then_inc(hid_ready, 1)
                dve.wait_ge(hid_hi, t + 1 + i)
                dve.tensor_tensor(lo, hid[:], hi.bitcast(F32), ALU.subtract).then_inc(hid_lo, 1)

            def s5_part(d):
                t = tiny
                dt, lr, li = t["log_dt"][:], t["lam_r"][:], t["lam_i"][:]
                if d == 0:
                    dve.wait_ge(s5_count, POOL_COUNT)
                    dve.wait_ge(s5_dt, 1)
                    kk = k_count[:].unsqueeze(2).broadcast_to([P, L + 1, PAIRS])

                    def times_k(a):
                        return a.unsqueeze(1).broadcast_to([P, L + 1, PAIRS])

                    step(dve.tensor_tensor(t["num_a"][:], lr, dt, ALU.mult))
                    step(dve.tensor_tensor(t["num_b"][:], li, dt, ALU.mult))
                    step(dve.tensor_tensor(t["mag"][:], kk, times_k(t["num_a"][:]), ALU.mult))
                    step(dve.tensor_tensor(t["angle"][:], kk, times_k(t["num_b"][:]), ALU.mult))
                    step(dve.tensor_scalar(t["turns"][:], t["angle"][:], 1.0 / TWO_PI, ROUND, ALU.mult, ALU.add))
                    step(dve.tensor_scalar(t["turns"][:], t["turns"][:], -ROUND, None, ALU.add))
                if d == 1:
                    for part in TWO_PI_PARTS:
                        step(dve.scalar_tensor_tensor(out=t["angle"][:], in0=t["turns"][:], scalar=-part,
                                                      in1=t["angle"][:], op0=ALU.mult, op1=ALU.add))
                    step(dve.tensor_copy(theta[:], t["angle"][:, L, :]))
                    step(dve.tensor_scalar(t["angle_c"][:], t["angle"][:], TWO_PI / 4, None, ALU.add))
                    step(dve.tensor_scalar(t["fold"][:], t["angle_c"][:], TWO_PI / 2, -TWO_PI, ALU.is_gt, ALU.mult))
                    step(dve.tensor_tensor(t["angle_c"][:], t["angle_c"][:], t["fold"][:], ALU.add))
                    step(dve.tensor_scalar(t["angle_c"][:], t["angle_c"][:], PI_BELOW, -PI_BELOW, ALU.min, ALU.max))
                    dve.tensor_scalar(t["angle"][:], t["angle"][:], PI_BELOW, -PI_BELOW, ALU.min, ALU.max)\
                       .then_inc(s5_angles, 1)
                if d == 2:
                    step(dve.tensor_tensor(t["den_l"][:], lr, lr, ALU.mult))
                    step(dve.tensor_tensor(t["abr1"][:], li, li, ALU.mult))
                    step(dve.tensor_tensor(t["den_l"][:], t["den_l"][:], t["abr1"][:], ALU.add))
                    step(dve.reciprocal(t["den_l"][:], t["den_l"][:]))
                ar, ai = pow_r[:, 1, :], pow_i[:, 1, :]
                if d == 3:
                    dve.wait_ge(s5_trig, 3)
                    step(dve.tensor_tensor(pow_r[:], t["mag"][:], t["angle_c"][:], ALU.mult))
                    step(dve.tensor_tensor(pow_i[:], t["mag"][:], t["angle"][:], ALU.mult))
                    step(dve.tensor_scalar(t["abr1"][:], ar, -1.0, None, ALU.add))
                    step(dve.tensor_tensor(t["num_a"][:], t["abr1"][:], lr, ALU.mult))
                    step(dve.tensor_tensor(t["num_b"][:], ai, li, ALU.mult))
                    step(dve.tensor_tensor(t["num_a"][:], t["num_a"][:], t["num_b"][:], ALU.add))
                    step(dve.tensor_tensor(coef[:, 0, :], t["num_a"][:], t["den_l"][:], ALU.mult))
                if d == 4:
                    step(dve.tensor_tensor(t["num_a"][:], ai, lr, ALU.mult))
                    step(dve.tensor_tensor(t["num_b"][:], t["abr1"][:], li, ALU.mult))
                    step(dve.tensor_tensor(t["num_a"][:], t["num_a"][:], t["num_b"][:], ALU.subtract))
                    step(dve.tensor_tensor(coef[:, 1, :], t["num_a"][:], t["den_l"][:], ALU.mult))
                    step(dve.tensor_copy(rho[:], t["mag"][:, L, :]))
                    step(dve.tensor_reduce(diag[:], ident[:].rearrange("p (b c) -> p c b", c=GC), AX.X, ALU.add))
                if d == 5:
                    cr, ci = (coef[:, part, :].unsqueeze(1).broadcast_to([P, L, PAIRS]) for part in range(2))
                    pr, pi = pow_r[:, 0:L, :], pow_i[:, 0:L, :]
                    wr, wi, wt = t["w_r"][:], t["w_i"][:], t["w_t"][:]
                    step(dve.tensor_tensor(wr, cr, pr, ALU.mult))
                    step(dve.tensor_tensor(wt, ci, pi, ALU.mult))
                    step(dve.tensor_tensor(wr, wr, wt, ALU.subtract))
                    step(dve.tensor_tensor(wi, cr, pi, ALU.mult))
                    step(dve.tensor_tensor(wt, ci, pr, ALU.mult))
                    dve.tensor_tensor(wi, wi, wt, ALU.add).then_inc(s5_w_ready, 1)

            def k_skip(q):
                if q == 0:
                    dve.wait_ge(d_loaded, 16)
                dve.wait_ge(k_ready, q + 1)
                for t in range(KD // QUARTERS):
                    k0 = s5_k[:, q % 2, t, 0:GC]
                    tile = q * (KD // QUARTERS) + t
                    dve.scalar_tensor_tensor(out=k0, in0=diag[:], scalar=d_col[:, tile:tile + 1], in1=k0,
                                             op0=ALU.mult, op1=ALU.add).then_inc(k_diag, 1)

            def mixer1(s0):
                dve.memset(decays[:, :, :, 0], 0.0).then_inc(decays_ready, 1)
                scale_u(dve, 0)
                scale_u(dve, 1)
                dve.memset(s5_x[:, :, :, 0], 0.0).then_inc(x_zeroed, 1)
                dve.wait_ge(x_zeroed, 1)
                dve.wait_ge(sines_loaded, 16)
                a, b, v = (r[:].rearrange("p w (n c) -> p w n c", c=NC) for r in rot)
                for q in range(QUARTERS):
                    ps = slice(q * PQ, (q + 1) * PQ)
                    sn, cs = sines[:, 0, ps, :], sines[:, 1, ps, :]
                    s_r, s_i = (bank[4 * part + q][:].rearrange("p (n c) -> p n c", c=NC) for part in range(2))
                    dve.wait_ge(st_ready, q + 1)
                    link(dve.tensor_tensor(a[:, 0], s_r, cs, ALU.mult))
                    link(dve.tensor_tensor(a[:, 1], s_i, cs, ALU.mult))
                    link(dve.tensor_tensor(b[:, 0], s_r, sn, ALU.mult))
                    dve.tensor_tensor(b[:, 1], s_i, sn, ALU.mult).then_inc(st_taken, 1)
                    settle()
                    dve.wait_ge(st_taken, q + 1)
                    link(dve.tensor_tensor(v[:, 0], a[:, 0], b[:, 1], ALU.add))
                    link(dve.tensor_tensor(v[:, 1], a[:, 1], b[:, 0], ALU.subtract))
                    settle()
                    dve.wait_ge(decays_ready, q + 2)
                    rho_q = decays[:, q % 2, :, :].rearrange("p n c -> p (n c)")
                    link(dve.tensor_tensor_scan(rot[0][:, 0, :], rho_q, rot[2][:, 0, :], 0.0, ALU.mult, ALU.add))
                    dve.tensor_tensor_scan(rot[0][:, 1, :], rho_q, rot[2][:, 1, :], 0.0, ALU.mult, ALU.add)\
                       .then_inc(x_scanned, 1)
                    settle()
                    dve.wait_ge(x_scanned, q + 1)
                    if q:
                        dve.wait_ge(scanned, 2 * q)
                    b2, v2 = (turned[:, i].rearrange("p w (n c) -> p w n c", c=NC) for i in range(2))
                    dve.tensor_tensor(b2, a, cs.unsqueeze(1).broadcast_to([P, 2, PQ, NC]), ALU.mult)\
                       .then_inc(rotated, 1)
                    dve.tensor_tensor(v2, a, sn.unsqueeze(1).broadcast_to([P, 2, PQ, NC]), ALU.mult)\
                       .then_inc(rotated, 1)
                    dve.wait_ge(rotated, 2 * (q + 1))

                def y_half(q):
                    dve.wait_ge(y_ready, 2 * q + 2)
                    dve.tensor_copy(s5_y[:, 2 * q + 1, :, :].rearrange("p j (a c) -> p a j c", c=GC),
                                    y_bank(2 * q + 1)[:].rearrange("p (a j c) -> p a j c", j=L, c=GC))\
                       .then_inc(y_taken_d, 1)

                def y_split(k):
                    gelu = (sq, ssq)[k % 2]
                    dve.wait_ge(y_hi_ready, k + 1)
                    dve.tensor_tensor(y_lo[:, k, :], gelu[:], y_hi[:, k, :].bitcast(F32), ALU.subtract)\
                       .then_inc(y_lo_ready, 1)

                y_half(0)
                for q in range(1, QUARTERS):
                    y_half(q)
                    if q == QUARTERS - 1:
                        split_lo(late[0], sizes[late[0]])
                    y_split(2 * q - 2)
                    y_split(2 * q - 1)
                y_split(KD - 2)
                y_split(KD - 1)
                split_lo(late[1], sizes[late[1]])
                for d in range(KD):
                    split_ahead(s0 + 2 * d, 2)
                    dve.wait_ge(glu_sig, d + 1)
                    dve.tensor_tensor(glu[:, d % 2, :], gate_ps[d % 2][:], sig[:, d % 2, :], ALU.mult).then_inc(glu_mul, 1)
                    dve.wait_ge(glu_mul, d + 1)
                    xv = x[:, d, :].rearrange("p (c j) -> p j c", j=L)
                    dve.tensor_tensor(xv, xv, glu[:, d % 2, :].rearrange("p (j c) -> p j c", j=L), ALU.add).then_inc(x_ready, 1)
                    if d:
                        norm_tile(NORM_S5 + 1, d - 1)
                norm_tile(NORM_S5 + 1, KD - 1)

            def normalised(u):
                if 1 <= u <= len(UNITS):
                    v = u - 1
                    b = v % 2
                    k0 = 0 if UNITS[v][0] else P
                    dve.wait_ge(p_exp, 3 * (v + 1))
                    step(dve.tensor_tensor(den[:, b, :], rowsum[:, b, :], sink_e[:, b, :], ALU.add))
                    step(dve.reciprocal(rden[:, b, :], den[:, b, :]))
                    for j in range(2):
                        dve.tensor_scalar(prob[:, b, j, k0:], prob[:, b, j, k0:], rden[:, b, j:j + 1], None,
                                          ALU.mult).then_inc(p_ready, 1)

            def attention(u):
                if u < len(UNITS):
                    n, tp, g = UNITS[u]
                    k0 = 0 if n else P
                    b = u % 2
                    h0 = AT * g + 2 * tp
                    dve.wait_ge(s_ready, u + 1)
                    if u >= 2:
                        dve.wait_ge(pt_ready, u - 1)
                    for j in range(2):
                        ins = dve.scalar_tensor_tensor(
                            out=prob[:, b, j, k0:], in0=dist[:, k0:], scalar=-SLOPES[h0 + j],
                            in1=bank[g][:, j * 2 * P + k0:(j + 1) * 2 * P], op0=ALU.mult, op1=ALU.add)
                        if j:
                            ins.then_inc(s_taken, 1)
                        else:
                            link(ins)
                    dve.wait_ge(s_taken, u + 1)
                    settle()
                    step(dve.tensor_reduce(max_neg[:, b, :], prob[:, b, :, k0:], AX.X, ALU.max, negate=True))
                    step(dve.tensor_tensor(max_neg[:, b, :], max_neg[:, b, :], sink_neg[:, h0:h0 + 2], ALU.min))
                    dve.tensor_tensor(sink_d[:, b, :], sink[:, h0:h0 + 2], max_neg[:, b, :], ALU.add)\
                       .then_inc(m_ready, 1)
                if u >= 3 and (u - 3) % 4 == 3:
                    n = (u - 3) // 4
                    dve.wait_ge(att_hi, n + 1)
                    dve.tensor_tensor(att_l[:, :, n * P:(n + 1) * P],
                                      bank[4 + n % 2][:].rearrange("p (t q) -> p t q", q=P),
                                      att_h[:, :, n * P:(n + 1) * P].bitcast(F32), ALU.subtract)\
                       .then_inc(att_lo, 1)

            def mixer0(s0):
                split_ahead(s0, 2)
                norm_root(NORM_MIX)
                step(dve.memset(carry[:], 1.0))
                link(dve.memset(carry[:].rearrange("p (c j) -> p c j", j=CH)[:, :, 0], 0.0))
                for t in range(AT):
                    if t >= 2:
                        split_ahead(s0 + t, 1)
                    dve.wait_ge(slab_used, used(s0 + t))
                    dve.scalar_tensor_tensor(out=a_q[:, t, :], in0=bank[t][:], scalar=AD ** -0.5, in1=rinv[:],
                                             op0=ALU.mult, op1=ALU.mult).then_inc(proj_scaled, 1)
                dve.wait_ge(col_ready, 1)
                dve.tensor_copy(r_col[:], bank[7][:, 0:NT]).then_inc(col_taken, 1)
                split_ahead(s0 + AT, 1)
                dve.wait_ge(slab_used, used(s0 + AT))
                dve.tensor_tensor(a_k[:], bank[0][:], rinv[:], ALU.mult).then_inc(proj_scaled, 1)
                split_ahead(s0 + AT + 1, 1)
                s = s0 + AT + 2

                def activated(n):
                    dve.wait_ge(sig_ready, n + 1)
                    if n < BH:
                        f = b_k[:, n, :]
                        dve.tensor_scalar(f, f, lb_c[:, n:n + 1], lb[:, n:n + 1], ALU.mult, ALU.add)\
                           .then_inc(f_ready, 1)
                    else:
                        out = (b_q, b_g)[n // BH - 1][:, n % BH, :]
                        dve.tensor_tensor(out, out, b_tmp[:, n % 2, :], ALU.mult).then_inc(sig_used, 1)

                def prepare(h):
                    settle()
                    if h == 0:
                        dve.wait_ge(cum_ready, BH)
                    dve.wait_ge(exp_ready, 2 * h + 1)
                    e3 = b_e[:, 0, :].rearrange("p (c j) -> p c j", j=CH)
                    link(dve.tensor_copy(decay[:, h, :], e3[:, :, CH - 1]))
                    dve.tensor_tensor(b_q[:, h, :], b_q[:, h, :], b_e[:, 0, :], ALU.mult).then_inc(qdec_ready, 1)
                    dve.wait_ge(exp_ready, 2 * h + 2)
                    c3 = b_cum[:, h, :].rearrange("p (c j) -> p c j", j=CH)
                    link(dve.tensor_tensor(b_kinv[:, h % 2, :], b_k[:, h, :], b_e[:, 1, :], ALU.mult))
                    settle()
                    dve.tensor_tensor(c3, c3[:, :, CH - 1:CH].broadcast_to([P, NCH, CH]), c3, ALU.subtract)\
                       .then_inc(rest_ready, 1)
                    dve.wait_ge(rest_exp, h + 1)
                    dve.tensor_tensor(b_k[:, h, :], b_k[:, h, :], b_cum[:, h, :], ALU.mult).then_inc(b_ready, 1)

                for n in range(STEPS):
                    normalised(n)
                    split_ahead(s + n, 1)
                    if n < 3 * BH:
                        dve.wait_ge(slab_used, used(s + n))
                        out = b_tmp[:, n % 2, :] if n < BH else (b_q, b_g)[n // BH - 1][:, n % BH, :]
                        if 2 <= n < BH:
                            dve.wait_ge(sig_ready, n - 1)
                        dve.tensor_tensor(out, bank[6 + n % 2][:], rinv[:], ALU.mult).then_inc(proj_scaled, 1)
                    if 1 <= n <= 3 * BH:
                        activated(n - 1)
                    if n == BH + 3:
                        dve.wait_ge(logf_ready, 1)
                        settle()
                        for h in range(BH):
                            c = b_cum[:, h, :]
                            dve.tensor_tensor_scan(c, carry[:], c, 0.0, ALU.mult, ALU.add).then_inc(cum_ready, 1)
                    if n == BH + 4:
                        link(dve.tensor_scalar(b_k[:], b_k[:], -1.0, 1.0, ALU.mult, ALU.add))
                    attention(n)
                    if n in (STEPS - 3, STEPS - 2):
                        prepare(n - STEPS + 3)

                mask = causal[:].bitcast(I32).unsqueeze(1).broadcast_to([P, NT, P])

                def masked(h):
                    dve.wait_ge(sc_ready, h + 1)
                    if h >= 2:
                        dve.wait_ge(inter_done, h - 1)
                    dve.copy_predicated(scores[:, h % 2, :, :], mask,
                                        bank[0][:].rearrange("p (m q) -> p m q", q=P)).then_inc(sc_masked, 1)

                def gated(h):
                    dve.wait_ge(ot_ready, h + 1)
                    if h >= 2:
                        dve.wait_ge(mix_lo, h - 1)
                    dve.tensor_tensor(rec[:, h % 2, :], bank[2 + h % 2][:], b_g[:, h, :], ALU.mult).then_inc(rec_ready, 1)
                    dve.wait_ge(mix_hi, h + 1)
                    dve.tensor_tensor(rec_l[:, h, :], rec[:, h % 2, :], rec_h[:, h, :].bitcast(F32),
                                      ALU.subtract).then_inc(mix_lo, 1)

                normalised(STEPS)
                dve.wait_ge(zeroed, 1)
                masked(0)
                attention(STEPS + 2)
                for h in range(BH):
                    dve.wait_ge(kv_ready, h + 1)
                    if h >= 2:
                        dve.wait_ge(b_ready, h + 1)
                    kv = [bank[4 + i][:].rearrange("p (m v) -> p m v", v=P) for i in range(CPT)]
                    st = states[:, h % 2]
                    dve.tensor_copy(st[:, 1, :], kv[0][:, 0, :]).then_inc(state_ready, 1)
                    for c in range(1, NCH - 1):
                        dve.wait_ge(state_ready, h * (NCH - 1) + c)
                        dve.scalar_tensor_tensor(out=st[:, c + 1, :], in0=st[:, c, :], scalar=decay[:, h, c:c + 1],
                                                 in1=kv[c % CPT][:, c // CPT, :],
                                                 op0=ALU.mult, op1=ALU.add).then_inc(state_ready, 1)
                    if h + 1 < BH:
                        masked(h + 1)
                    ss = o_ss[:, h % 2, :]
                    dve.wait_ge(o_sq, (h + 1) * NT)
                    dve.tensor_scalar(ss, ss, 1.0 / P, EPS, ALU.mult, ALU.add).then_inc(o_mean, 1)
                    dve.wait_ge(o_rms, h + 1)
                    step(dve.reciprocal(ss, ss))
                    dve.tensor_tensor(o_norm_h[:, h % 2, :, :], bank[2 + h % 2][:].rearrange("p (m v) -> p m v", v=P),
                                      ss.unsqueeze(2).broadcast_to([P, NT, P]), ALU.mult).then_inc(o_scaled, 1)
                    if h:
                        gated(h - 1)
                gated(BH - 1)

            dve.memset(ones[:], 1.0).then_inc(ones_set, 1)
            dve.wait_ge(const_loaded, 32)
            split_lo(0, sizes[0])
            for k in range(KD):
                dve.wait_ge(x_loaded[k], 16)
                norm_tile(0, k)
            split_lo(1, sizes[1])
            for k in range(KD):
                norm_square(0, k)
            for kind, f, half, s0 in phases:
                if kind == "in":
                    t0 = (HALVES * f + half) * KF
                    split_ahead(s0, 2)
                    if half == 0:
                        norm_root(NORMS[f])
                    hidden(t0, s0, 0, h_hi[:, 0, :], h_lo[:, 0, :])
                    with dve.Fori(0, KF // 2 - 1) as i:
                        for t in (1, 2):
                            for part in range(2):
                                split_lo(s0 + 2 * t + part + LEAD, SLAB_IN, i)
                            hidden(t0 + t, s0 + 2 * t, t % 2, h_hi[:, bass.ds(i * 2 + t, 1), :].squeeze(1),
                                   h_lo[:, bass.ds(i * 2 + t, 1), :].squeeze(1), i * 2, i * RING)
                    for t in (KF - 2, KF - 1):
                        split_ahead(s0 + 2 * t, 2)
                        hidden(t0 + t, s0 + 2 * t, t % 2, h_hi[:, t, :], h_lo[:, t, :])
                elif kind == "out":
                    for d in range(KD):
                        split_ahead(s0 + d, 1)
                        if (f, half) == S5_SMALL:
                            s5_part(d)
                        if (f, half) == S5_KERNELS and d % 2 == 1:
                            k_skip(d // 2)
                        dve.wait_ge(slab_used, used(s0 + d))
                        add = dve.scalar_tensor_tensor(out=x[:, d, :], in0=out_ps[d % 2][:], scalar=0.5,
                                                       in1=x[:, d, :], op0=ALU.mult, op1=ALU.add)
                        if half == HALVES - 1:
                            add.then_inc(x_ready, 1)
                            norm_tile(NORMS[f] + 1, d)
                        else:
                            add.then_inc(x_half, 1)
                    if half == HALVES - 1 and NORMS[f] + 1 in (NORM_S5, NORM_FIN):
                        norm_root(NORMS[f] + 1)
                elif kind == "mixer1":
                    mixer1(s0)
                elif kind == "mixer0":
                    dve.wait_ge(small_loaded, 32)
                    step(dve.tensor_tensor(lb_c[:], lb_in[:], lb_in[:], ALU.subtract))
                    dve.tensor_scalar(sink_neg[:], sink[:], -1.0, None, ALU.mult).then_inc(lb_exp, 1)
                    dve.wait_ge(act_step, 1)
                    step(dve.reciprocal(lb_c[:], lb[:]))
                    step(dve.tensor_tensor(lb_in[:], lb[:], lb_c[:], ALU.mult))
                    step(dve.tensor_tensor(lb[:], lb_in[:], lb_in[:], ALU.subtract))
                    step(dve.tensor_scalar(lb_c[:], lb[:], -1.0, 1.0, ALU.mult, ALU.add))
                    mixer0(s0)
                elif kind == "mixer0_out":
                    for d in range(KD):
                        split_ahead(s0 + d, 1)
                        dve.wait_ge(slab_used, used(s0 + d))
                        dve.tensor_tensor(x[:, d, :], out_ps[d % 2][:], x[:, d, :], ALU.add).then_inc(x_ready, 1)
                        norm_tile(NORM_MIX + 1, d)
            for k in range(KD):
                dve.scalar_tensor_tensor(out=x[:, k, :], in0=x[:, k, :], scalar=g_all[:, NORM_FIN, k:k + 1],
                                         in1=rinv[:], op0=ALU.mult, op1=ALU.mult).then_inc(fin_ready, 1)

        @block.tensor
        def _(pe):
            def product(out, s, k, hi, lo, start, stop):
                wh = w_hi[:, slot(s), k * P:(k + 1) * P]
                wl = w_lo[:, slot(s), k * P:(k + 1) * P]
                pe.matmul(out, wh, hi, start=start, stop=False)
                pe.matmul(out, wh, lo, start=False, stop=False)
                return pe.matmul(out, wl, hi, start=False, stop=stop)

            def norm(n):
                pe.wait_ge(ssq_ready, (n + 1) * KD)
                if n:
                    pe.wait_ge(mean_ready, n)
                pe.matmul(norm_ps[:], ones[:], ssq[:], start=True, stop=True).then_inc(norm_sum, 1)

            def natural(s, count, tiles, out):
                for m in tiles:
                    for k in range(KD):
                        xh = xg_hi[:, k, m * P:(m + 1) * P]
                        xl = xg_lo[:, k, m * P:(m + 1) * P]
                        wh = w_hi[:, slot(s):slot(s) + count, k * P:(k + 1) * P]
                        wl = w_lo[:, slot(s):slot(s) + count, k * P:(k + 1) * P]
                        pe.matmul(out(m), xh, wh, start=k == 0, stop=False)
                        pe.matmul(out(m), xh, wl, start=False, stop=False)
                        mm = pe.matmul(out(m), xl, wh, start=False, stop=k == KD - 1)
                return mm

            def attention(u):
                if u < len(UNITS) and u % 2 == 0:
                    n, tp, _ = UNITS[u]
                    k0 = 0 if n else P
                    if u == 0:
                        pe.wait_ge(proj_scaled, AT + 1)
                    else:
                        pe.wait_ge(s_taken, u)
                    for j in range(2):
                        for g in range(2):
                            rows = slice(g * AD, (g + 1) * AD)
                            mm = pe.matmul(bank[g][:, j * 2 * P + k0:(j + 1) * 2 * P],
                                           a_q[rows, 2 * tp + j, n * P:(n + 1) * P],
                                           a_k[rows, (n - 1) * P + k0:(n + 1) * P], start=True, stop=True)
                            if j:
                                mm.then_inc(s_ready, 1)
                if 1 <= u <= len(UNITS):
                    v = u - 1
                    n, tp, g = UNITS[v]
                    pe.wait_ge(p_ready, 2 * (v + 1))
                    if v >= 2:
                        pe.wait_ge(pt_taken, taken(v - 2))
                    for j in range(2):
                        for kt in range(0 if n else 1, 2):
                            mm = pe.transpose(bank[2 + v % 2][:, (2 * j + kt) * P:(2 * j + kt + 1) * P],
                                              prob[:, v % 2, j, kt * P:(kt + 1) * P], ident[:])
                    mm.then_inc(pt_ready, 1)
                if u >= 3 and u % 2 == 1:
                    v = u - 3
                    n, tp, _ = UNITS[v]
                    pe.wait_ge(pt_taken, taken(v + 1))
                    if v == 0:
                        pe.wait_ge(nat_taken, NT)
                    if v % 4 == 0 and n >= 2:
                        pe.wait_ge(att_lo, n - 1)
                    kts = range(0 if n else 1, 2)
                    for kt in kts:
                        for g in range(2):
                            mm = pe.matmul(bank[4 + n % 2][g * AD:(g + 1) * AD, 2 * tp * P:2 * (tp + 1) * P]
                                           .rearrange("p (j q) -> p j q", j=2),
                                           a_v[:, n - 1 + kt, g * AD:(g + 1) * AD], prob_t[:, g, :, kt, :],
                                           start=kt == kts[0], stop=kt == 1)
                            if kt == 1:
                                mm.then_inc(pv_done, 1)

            def mixer0(s0):
                def project(s, out):
                    pe.wait_ge(slab_lo, split(s))
                    for k in range(KD):
                        if s == s0:
                            pe.wait_ge(xg_lo_ready, xg_count(NORM_MIX, k))
                        mm = product(out, s, k, xg_hi[:, k, :], xg_lo[:, k, :], k == 0, k == KD - 1)
                    mm.then_inc(slab_used, 1)

                for t in range(AT):
                    project(s0 + t, bank[t][:])
                    if t == 0:
                        norm(NORM_MIX)
                    if t == 2:
                        pe.wait_ge(rinv_ready, NORM_MIX + 1)
                        for m in range(NT):
                            mm = pe.matmul(bank[7][:, m:m + 1], rinv[0:1, m * P:(m + 1) * P], ones[0:1, 0:1],
                                           start=True, stop=True)
                        mm.then_inc(col_ready, 1)
                pe.wait_ge(proj_scaled, 1)
                project(s0 + AT, bank[0][:])
                pe.wait_ge(slab_lo, split(s0 + AT + 1))
                natural(s0 + AT + 1, 1, range(NT), lambda m: bank[4][:, m * P:(m + 1) * P]).then_inc(slab_used, 1)
                s = s0 + AT + 2
                for n in range(STEPS):
                    if n < 3 * BH:
                        if n == 0:
                            pe.wait_ge(mean_ready, NORM_MIX + 1)
                        elif n == 1:
                            pe.wait_ge(col_taken, 1)
                        else:
                            pe.wait_ge(proj_scaled, AT + 1 + n - 1)
                        project(s + n, bank[6 + n % 2][:])
                    else:
                        i = n - 3 * BH
                        pair, half = i // 2, i % 2
                        if pair == 0:
                            pe.wait_ge(proj_scaled, AT + 1 + 3 * BH)
                        else:
                            pe.wait_ge(nat_taken, NT + 2 * (half + 1))
                        first = s + 3 * BH + 2 * pair
                        assert slot(first) % 2 == 0
                        pe.wait_ge(slab_lo, split(first + 1))

                        def out(m):
                            return bank[6 + half][:, (m % 2) * 2 * P:(m % 2 + 1) * 2 * P].rearrange("p (a c) -> p a c", a=2)
                        mm = natural(first, 2, range(2 * half, 2 * half + 2), out)
                        mm.then_inc(v_ready, 1)
                        if half:
                            pe.wait_ge(v_ready, i + 1)
                            pe.sem_inc(slab_used, 2)
                    attention(n)
                assert STEPS == len(UNITS)

                def head_scores(h):
                    pe.wait_ge(b_ready, h + 1)
                    if h == 0:
                        pe.wait_ge(s_taken, len(UNITS) - 1)
                    else:
                        pe.wait_ge(sc_masked, h)
                    for m in range(NT):
                        t = slice(m * P, (m + 1) * P)
                        mm = pe.matmul(bank[0][:, t], exps(h)[1][:, h % 2, t], b_q[:, h, t], start=True, stop=True)
                    mm.then_inc(sc_ready, 1)

                def head_keys(h):
                    if h:
                        pe.wait_ge(kt_taken, h)
                    else:
                        pe.wait_ge(s_taken, len(UNITS))
                    for m in range(NT):
                        t = slice(m * P, (m + 1) * P)
                        mm = pe.transpose(bank[1][:, t], b_k[:, h, t], ident[:])
                    mm.then_inc(kt_ready, 1)

                def head_values(h):
                    v = b_v[:, :, h * P:(h + 1) * P]
                    pe.wait_ge(kt_taken, h + 1)
                    if h:
                        pe.wait_ge(state_ready, h * (NCH - 1))
                    else:
                        pe.wait_ge(nat_taken, 3 * NT)
                        pe.wait_ge(att_lo, NT)
                    for m in range(NT):
                        for i in range(CPT):
                            rows = slice(i * CH, (i + 1) * CH)
                            mm = pe.matmul(bank[4 + i][:, m * P:(m + 1) * P], k_end[rows, h % 2, m, :], v[rows, m, :],
                                           start=True, stop=True)
                    mm.then_inc(kv_ready, 1)

                def head_output(h):
                    v = b_v[:, :, h * P:(h + 1) * P]
                    ob = bank[2 + h % 2]
                    pe.wait_ge(sc_masked, h + 1)
                    if h >= 2:
                        pe.wait_ge(rec_ready, h - 1)
                    else:
                        pe.wait_ge(pt_taken, taken(len(UNITS) - 1))
                    for m in range(NT):
                        pe.matmul(ob[:, m * P:(m + 1) * P], scores[:, h % 2, m, :], v[:, m, :], start=m == 0,
                                  stop=False, skip_group_check=True)
                    for c in range(1, NCH):
                        m, i = c // CPT, c % CPT
                        pe.wait_ge(state_ready, h * (NCH - 1) + c)
                        mm = pe.matmul(ob[i * CH:(i + 1) * CH, m * P:(m + 1) * P], b_q[:, h, c * CH:(c + 1) * CH],
                                       states[:, h % 2, c, :], start=False, stop=c == NCH - 1, skip_group_check=True)
                    mm.then_inc(inter_done, 1)

                def head_turned(h):
                    pe.wait_ge(o_scaled, h + 1)
                    for m in range(NT):
                        mm = pe.transpose(bank[2 + h % 2][:, m * P:(m + 1) * P], o_norm_h[:, h % 2, m, :], ident[:])
                    mm.then_inc(ot_ready, 1)

                head_scores(0)
                attention(STEPS)
                head_keys(0)
                attention(STEPS + 1)
                head_scores(1)
                head_values(0)
                head_keys(1)
                head_output(0)
                for h in range(1, BH):
                    head_values(h)
                    if h + 1 < BH:
                        head_scores(h + 1)
                        head_keys(h + 1)
                    head_turned(h - 1)
                    head_output(h)
                head_turned(BH - 1)

            def w_turn():
                pe.wait_ge(s5_w_ready, 1)
                for part, name in enumerate(("w_r", "w_i")):
                    w = tiny[name][:].rearrange("p j a -> p (j a)")
                    for half in range(L * PAIRS // P):
                        mm = pe.transpose(bank[7][:, (2 * part + half) * P:(2 * part + half + 1) * P],
                                          w[:, half * P:(half + 1) * P], ident[:])
                mm.then_inc(s5_w_turned, 1)

            def kernels(q):
                if q == 0:
                    pe.wait_ge(bb_loaded, 16)
                else:
                    pe.wait_ge(k_ready, q)
                pe.wait_ge(cq_loaded[q % 2], 32 * (q // 2 + 1))
                per = PAIRS // KD
                for t in range(KD // QUARTERS):
                    for i in range(per):
                        for part in range(2):
                            mm = pe.matmul(bank[7][i * 2 * GC:(i + 1) * 2 * GC, t * P:(t + 1) * P],
                                           s5_bb[:, q * PQ + t * per + i, part, :], s5_cq[:, q % 2, part, t * per + i, :],
                                           start=part == 0, stop=part == 1)
                mm.then_inc(k_summed, 1)

            def mixer1(s0):
                pe.wait_ge(mean_ready, NORM_S5 + 1)
                m3 = rms[0:1, :].rearrange("p (c j) -> p j c", j=L)
                pe.wait_ge(pool_const, POOL_ALL)
                for j in range(L):
                    mm = pe.matmul(bank[7][:, 0:NC], r_sel[:, (L - 1 - j) * GC:(2 * L - 1 - j) * GC], m3[:, j, :],
                                   start=j == 0, stop=j == L - 1)
                mm.then_inc(row_ready, 1)
                pe.wait_ge(bm_loaded[0], 16)
                pe.wait_ge(bm_loaded[1], 16)
                for b in range(PAIRS // PPB):
                    pe.wait_ge(u_ready[b], 1)
                    for part in range(2):
                        for a in range(PPB):
                            for g in range(2):
                                pair = b * PPB + a
                                mm = pe.matmul(bank[4 * part + b][g * NS:(g + 1) * NS, a * NC:(a + 1) * NC],
                                               s5_bm[:, 2 * pair + g, part, :], s5_u[:, group(pair, g), :],
                                               start=True, stop=True)
                    mm.then_inc(st_ready, 1)
                pe.wait_ge(t_loaded, 16 * L)

                def within(q):
                    pe.wait_ge(st_taken, q + 1)
                    for i in range(2):
                        k = 2 * q + i
                        for a in range(PER):
                            for g in range(2):
                                pair = k * PER + a
                                pe.matmul(y_bank(k)[g * NC:(g + 1) * NC, a * P:(a + 1) * P],
                                          s5_u[:, group(pair, g), :], s5_t[:, 2 * pair + g, :],
                                          start=a == 0, stop=False, skip_group_check=True)

                def from_states(q):
                    pe.wait_ge(c_loaded[q], 16 * 2)
                    pe.wait_ge(scanned, 2 * (q + 1))
                    for turn in range(2):
                        for a in range(PER):
                            for part in range(2):
                                for i in range(2):
                                    k, g = 2 * q + i, i ^ turn
                                    pair = k * PER + a
                                    rows = slice(g * NS, (g + 1) * NS)
                                    last = a == PER - 1 and part == 1
                                    mm = pe.matmul(y_bank(k)[g * NC:(g + 1) * NC, a * P:(a + 1) * P],
                                                   s5_x[rows, part, pair, :], s5_c[rows, pair, part, :],
                                                   start=False, stop=last, skip_group_check=True)
                                    if last and turn:
                                        mm.then_inc(y_ready, 1)

                def y_turned(q):
                    pe.wait_ge(y_taken_a, q + 1)
                    pe.wait_ge(y_taken_d, q + 1)
                    for turn in range(2):
                        for j in range(L):
                            for i in range(2):
                                k, g = 2 * q + i, i ^ turn
                                rows = slice(g * NC, (g + 1) * NC)
                                out = y_bank(k)[g * NS:(g + 1) * NS, j * NC:(j + 1) * NC]
                                if g == 0:
                                    mm = pe.transpose(out, s5_y[rows, k, j, :], ident[rows, rows])
                                else:
                                    mm = pe.matmul(out, s5_y[rows, k, j, :], ident[rows, rows], start=True, stop=True)
                                if turn and j == L - 1:
                                    mm.then_inc(yt_ready, 1)

                within(0)
                within(1)
                from_states(0)
                for q in range(2, QUARTERS):
                    within(q)
                    from_states(q - 1)
                    y_turned(q - 2)
                from_states(QUARTERS - 1)
                y_turned(QUARTERS - 2)
                y_turned(QUARTERS - 1)
                for d in range(KD):
                    if d >= 2:
                        pe.wait_ge(glu_mul, d - 1)
                    for part, out in enumerate((gate_ps[d % 2], up_ps[d % 2])):
                        s = s0 + 2 * d + part
                        pe.wait_ge(slab_lo, split(s))
                        for k in range(KD):
                            if d == 0 and part == 0:
                                pe.wait_ge(y_lo_ready, k + 1)
                            mm = product(out[:], s, k, y_hi[:, k, :], y_lo[:, k, :], k == 0, k == KD - 1)
                        mm.then_inc(slab_used, 1)

            pe.wait_ge(ones_set, 1)
            for kind, f, half, s0 in phases:
                t0 = (HALVES * f + half) * KF
                if kind == "in":
                    def tile(t, n, i=0, turn=0):
                        pe.wait_ge(banks_free, t0 + t + 1 + i)
                        for part, out in enumerate((gate_ps[t % 2], up_ps[t % 2])):
                            s = s0 + 2 * t + part
                            pe.wait_ge(slab_lo, split(s) + turn)
                            for k in range(KD):
                                if n is not None and part == 0:
                                    pe.wait_ge(xg_lo_ready, xg_count(n, k))
                                mm = product(out[:], s, k, xg_hi[:, k, :], xg_lo[:, k, :], k == 0, k == KD - 1)
                            mm.then_inc(slab_used, 1)
                            if n is not None and part == (n == 0):
                                norm(n)

                    tile(0, NORMS[f] if half == 0 else None)
                    with pe.Fori(0, KF // 2) as i:
                        tile(1, None, i * 2, i * RING)
                        tile(2, None, i * 2, i * RING)
                elif kind == "out":
                    for d in range(KD):
                        s = s0 + d
                        if d >= 2:
                            if half == HALVES - 1:
                                pe.wait_ge(x_ready, NORMS[f] * KD + d - 1)
                            else:
                                pe.wait_ge(x_half, f * KD + d - 1)
                        pe.wait_ge(slab_lo, split(s))
                        for k in range(KF):
                            if d == 0:
                                pe.wait_ge(hid_lo, t0 + k + 1)
                            mm = product(out_ps[d % 2][:], s, k, h_hi[:, k, :], h_lo[:, k, :], k == 0, k == KF - 1)
                        mm.then_inc(slab_used, 1)
                        if (f, half) == S5_SMALL and d == KD - 2:
                            w_turn()
                        if (f, half) == S5_KERNELS and d % 2 == 0:
                            kernels(d // 2)
                    if half == HALVES - 1 and NORMS[f] + 1 in (NORM_S5, NORM_FIN):
                        norm(NORMS[f] + 1)
                elif kind == "mixer1":
                    mixer1(s0)
                elif kind == "mixer0":
                    pe.wait_ge(pool_const, POOL_CONSTS)
                    mixer0(s0)
                elif kind == "mixer0_out":
                    for d in range(KD):
                        s = s0 + d
                        if d >= 2:
                            pe.wait_ge(x_ready, NORM_MIX * KD + d - 1)
                        pe.wait_ge(slab_lo, split(s))
                        for k in range(KD):
                            if d == 0:
                                if k == 0:
                                    pe.wait_ge(att_lo, NT)
                                    pe.wait_ge(state_ready, BH * (NCH - 1))
                                if k >= AT:
                                    pe.wait_ge(mix_lo, k - AT + 1)
                            hi, lo = (att_h[:, k, :], att_l[:, k, :]) if k < AT else (rec_h[:, k - AT, :], rec_l[:, k - AT, :])
                            mm = product(out_ps[d % 2][:], s, k, hi, lo, k == 0, k == KD - 1)
                        mm.then_inc(slab_used, 1)

        @block.gpsimd
        def _(pool):
            pool.sem_inc(slab_used, RING)
            pool.sem_inc(slab_lo, RING)
            pool.sem_inc(banks_free, 2)
            done = [0]

            def step(ins):
                done[0] += 1
                ins.then_inc(pool_const, 1)
                pool.wait_ge(pool_const, done[0])

            step(pool.memset(ident[:], 0.0))
            step(pool.affine_select(out=ident[:], in_=ident[:], compare_op=ALU.not_equal, fill=1.0, base=0,
                                    pattern=[[-1, P]], channel_multiplier=1))
            step(pool.memset(causal[:], 1.0))
            c3 = causal[:].rearrange("p (c j) -> p c j", j=CH)
            step(pool.affine_select(out=c3, in_=c3, compare_op=ALU.is_ge, fill=0.0, base=0,
                                    pattern=[[CH, CPT], [1, CH]], channel_multiplier=-1))
            step(pool.affine_select(out=c3, in_=c3, compare_op=ALU.is_ge, fill=0.0, base=0,
                                    pattern=[[-CH, CPT], [0, CH]], channel_multiplier=1))
            step(pool.iota(dist[:].bitcast(I32), pattern=[[-1, 2 * P]], base=P, channel_multiplier=1))
            step(pool.tensor_copy(dist[:], dist[:].bitcast(I32)))
            step(pool.affine_select(out=dist[:], in_=dist[:], compare_op=ALU.is_ge, fill=MASKED, base=P,
                                    pattern=[[-1, 2 * P]], channel_multiplier=1))
            step(pool.affine_select(out=dist[:], in_=dist[:], compare_op=ALU.is_ge, fill=MASKED, base=-1,
                                    pattern=[[1, 2 * P]], channel_multiplier=-1))
            assert done[0] == POOL_CONSTS
            step(pool.memset(r_sel[:], 0.0))
            step(pool.memset(r_sel[:, (L - 1) * GC:L * GC], 1.0))
            assert done[0] == POOL_ALL

            pool.wait_ge(v_ready, STEPS - 3 * BH)
            pool.memset(scores[:], 0.0).then_inc(zeroed, 1)
            for h in (2, 3):
                pool.wait_ge(b_ready, h)
                pool.wait_ge(exp_ready, 2 * h + 2)
                e3 = late_e[:, 0, :].rearrange("p (c j) -> p c j", j=CH)
                pool.tensor_copy(decay[:, h, :], e3[:, :, CH - 1]).then_inc(decay_ready, 1)
                pool.tensor_tensor(b_q[:, h, :], b_q[:, h, :], late_e[:, 0, :], ALU.mult).then_inc(qdec_ready, 1)
                pool.tensor_tensor(late_kinv[:, h % 2, :], b_k[:, h, :], late_e[:, 1, :], ALU.mult)\
                    .then_inc(decay_ready, 1)
                pool.wait_ge(decay_ready, 2 * (h - 1))
                c3 = b_cum[:, h, :].rearrange("p (c j) -> p c j", j=CH)
                pool.tensor_tensor(c3, c3[:, :, CH - 1:CH].broadcast_to([P, NCH, CH]), c3, ALU.subtract)\
                    .then_inc(rest_ready, 1)
                pool.wait_ge(rest_exp, h + 1)
                pool.tensor_tensor(b_k[:, h, :], b_k[:, h, :], b_cum[:, h, :], ALU.mult).then_inc(b_ready, 1)
            pool.wait_ge(slab_used, used(next(s0 for k, _, _, s0 in phases if k == "mixer0_out") + KD - 1))
            pool.iota(k_count[:].bitcast(I32), pattern=[[1, L + 1]], base=0, channel_multiplier=0)\
                .then_inc(s5_count, 1)
            pool.wait_ge(s5_count, 1)
            pool.tensor_copy(k_count[:], k_count[:].bitcast(I32)).then_inc(s5_count, 1)
            pool.dma_start(tiny["lam_r"][:], s5_a_re).then_inc(s5_loaded, 16)
            pool.dma_start(tiny["lam_i"][:], s5_a_im).then_inc(s5_loaded, 16)
            for g in range(2):
                pool.dma_start(tiny["log_dt"][g * NS:(g + 1) * NS, :], s5_log_step[g].partition_broadcast(NS))\
                    .then_inc(s5_loaded, 16)

            made = [0]
            loads = [0]
            stores = [0]

            def link(ins):
                made[0] += 1
                ins.then_inc(pool_step, 1)
                pool.wait_ge(pool_step, made[0])

            def fetch(out, src):
                loads[0] += 1
                pool.dma_start(out, src).then_inc(mk_loaded, 16)

            def fetched():
                pool.wait_ge(mk_loaded, 16 * loads[0])

            def store(out, src):
                stores[0] += 1
                pool.dma_start(out, src).then_inc(mk_stored, 16)

            def kept():
                pool.wait_ge(mk_stored, 16 * stores[0])

            tt = pool.tensor_tensor
            pool.wait_ge(s5_w_rows, 1)
            store(dram_w.rearrange("w (h j) (a g) s -> (j a) (w h) (g s)", h=2, g=2), w_rows[:])
            kept()
            for q in range(4):
                gs = slice(q * GQ, (q + 1) * GQ)
                kept()
                for j in range(L):
                    fetch(mk_w[j * GC:(j + 1) * GC, :, :], dram_w[:, L - 1 - j, gs, :].rearrange("w g s -> w (g s)")
                          .partition_broadcast(GC))
                for src, name in ((s5_bt_re, "br"), (s5_bt_im, "bi")):
                    fetch(mk[name][:], src[:, q * GQ * NS:(q + 1) * GQ * NS].unsqueeze(0)
                          .broadcast_to([L, GC, GQ * NS]))
                fetched()
                wr, wi = mk_w[:, 0, :], mk_w[:, 1, :]
                br, bi, t1, t2 = (mk[n][:] for n in ("br", "bi", "t1", "t2"))
                link(tt(t1, wr, br, ALU.mult))
                link(tt(t2, wi, bi, ALU.mult))
                link(tt(t1, t1, t2, ALU.subtract))
                link(tt(t2, wr, bi, ALU.mult))
                link(tt(wr, wi, br, ALU.mult))
                link(tt(t2, t2, wr, ALU.add))
                store(dram_bm[:, gs, 0, :], mk["t1"][:].rearrange("p (g s) -> p g s", s=NS))
                store(dram_bm[:, gs, 1, :], mk["t2"][:].rearrange("p (g s) -> p g s", s=NS))
            kept()
            fetch(mk["cr"][:], s5_c_re)
            fetch(mk["ci"][:], s5_c_im)
            fetched()
            link(pool.tensor_scalar(mk["ncr"][:], mk["cr"][:], -1.0, None, ALU.mult))
            for q in range(4):
                ps = slice(q * PQ, (q + 1) * PQ)

                def over_k(a):
                    return a[:, ps, :].unsqueeze(2).broadcast_to([P, PQ, L + 1, GC])

                def over_c(a):
                    return a[:, :, ps].rearrange("p k a -> p a k").unsqueeze(3).broadcast_to([P, PQ, L + 1, GC])

                def v(a):
                    return a.rearrange("p a (k c) -> p a k c", c=GC)

                cr, ci, ncr = over_k(mk["cr"][:]), over_k(mk["ci"][:]), over_k(mk["ncr"][:])
                pr, pi = over_c(pow_r[:]), over_c(pow_i[:])
                t1, t2 = v(mk["u1"][:]), v(mk["u2"][:])
                for n in range(PQ):
                    link(tt(t1[:, n], cr[:, n], pr[:, n], ALU.mult))
                    link(tt(t2[:, n], ci[:, n], pi[:, n], ALU.mult))
                kept()
                link(tt(mk_c[:, 0], mk["u1"][:], mk["u2"][:], ALU.subtract))
                for n in range(PQ):
                    link(tt(t1[:, n], ncr[:, n], pi[:, n], ALU.mult))
                    link(tt(t2[:, n], ci[:, n], pr[:, n], ALU.mult))
                link(tt(mk_c[:, 1], mk["u1"][:], mk["u2"][:], ALU.subtract))
                for part in range(2):
                    store(dram_c[:, part, ps, :], mk_c[:, part])
            kept()
            fetch(mk["sr"][:], s5_b_re)
            fetch(mk["si"][:], s5_b_im)
            link(pool.memset(mk_bb[:], 0.0))
            fetched()
            sr, si, t1, t2 = (mk[n][:] for n in ("sr", "si", "s1", "s2"))
            cr = coef[:, 0, :].unsqueeze(2).broadcast_to([P, PAIRS, GC])
            ci = coef[:, 1, :].unsqueeze(2).broadcast_to([P, PAIRS, GC])
            for part, (a, b, op) in enumerate(((sr, si, ALU.subtract), (si, sr, ALU.add))):
                link(tt(t1, cr, a, ALU.mult))
                link(tt(t2, ci, b, ALU.mult))
                for g in range(2):
                    rows = slice(g * NS, (g + 1) * NS)
                    link(tt(mk_bb[rows, :, part, g * GC:(g + 1) * GC], t1[rows], t2[rows], op))
            store(dram_bb, mk_bb[:].rearrange("p a b c -> p (a b c)"))
            link(pool.memset(mk_zero[:], 0.0))
            store(dram_k.rearrange("(t p) c -> p t c", p=P)[:, :, 0:(L - 1) * GC], mk_zero[:])
            kept()
            assert stores[0] == MK_STORES

            pool.dma_start(s5_bb[:].rearrange("p a b c -> p (a b c)"), dram_bb).then_inc(bb_loaded, 16)
            dk = dram_k.rearrange("(t p) c -> p t c", p=P)
            n = KD // QUARTERS

            def load_c(q):
                for part in range(2):
                    pool.dma_start(s5_cq[:, q % 2, part, :, :],
                                   dram_c[:, part, q * PQ:(q + 1) * PQ, 0:L * GC]).then_inc(cq_loaded[q % 2], 16)

            load_c(0)
            load_c(1)
            for q in range(QUARTERS):
                pool.wait_ge(k_diag, n * (q + 1))
                pool.dma_start(dk[:, q * n:(q + 1) * n, (L - 1) * GC:], s5_k[:, q % 2, :, :]).then_inc(k_stored, 16)
                pool.wait_ge(k_stored, 16 * (q + 1))
                if q + 2 < QUARTERS:
                    load_c(q + 2)

            link(pool.iota(c_count[:].bitcast(I32), pattern=[[1, NC]], base=0, channel_multiplier=0))
            link(pool.tensor_copy(c_count[:], c_count[:].bitcast(I32)))
            link(pool.tensor_scalar(theta_hi[:], theta[:], ROUND_10, -ROUND_10, ALU.add, ALU.add))
            link(tt(theta_lo[:], theta[:], theta_hi[:], ALU.subtract))
            cc = c_count[:].unsqueeze(1).broadcast_to([P, PAIRS, NC])

            def over_chunks(a):
                return a[:].unsqueeze(2).broadcast_to([P, PAIRS, NC])

            link(tt(turn_s[:], cc, over_chunks(theta_hi), ALU.mult))
            link(tt(turn_c[:], cc, over_chunks(theta), ALU.mult))
            link(pool.tensor_scalar(turn_c[:], turn_c[:], 1.0 / TWO_PI, ROUND, ALU.mult, ALU.add))
            link(pool.tensor_scalar(turn_c[:], turn_c[:], -ROUND, None, ALU.add))
            link(pool.tensor_scalar(turn_t[:], turn_c[:], -TWO_PI_PARTS[0], None, ALU.mult))
            link(tt(turn_s[:], turn_s[:], turn_t[:], ALU.add))
            link(tt(turn_t[:], cc, over_chunks(theta_lo), ALU.mult))
            link(tt(turn_s[:], turn_s[:], turn_t[:], ALU.add))
            for part in TWO_PI_PARTS[1:]:
                link(pool.tensor_scalar(turn_t[:], turn_c[:], -part, None, ALU.mult))
                link(tt(turn_s[:], turn_s[:], turn_t[:], ALU.add))
            link(pool.tensor_scalar(turn_c[:], turn_s[:], TWO_PI / 4, None, ALU.add))
            link(pool.tensor_scalar(turn_t[:], turn_c[:], TWO_PI / 2, -TWO_PI, ALU.is_gt, ALU.mult))
            link(tt(turn_c[:], turn_c[:], turn_t[:], ALU.add))
            link(pool.tensor_scalar(turn_c[:], turn_c[:], PI_BELOW, -PI_BELOW, ALU.min, ALU.max))
            pool.tensor_scalar(turn_s[:], turn_s[:], PI_BELOW, -PI_BELOW, ALU.min, ALU.max).then_inc(turns_ready, 1)
            for part, turn in enumerate((turn_s, turn_c)):
                pool.wait_ge(sines_ready, part + 1)
                store(dram_sines[:, part, :], turn[:].rearrange("p a c -> p (a c)"))
            kept()
            early = GQ
            pool.dma_start(s5_bm[:, early:, :, :], dram_bm[:, early:, :, :]).then_inc(bm_loaded[0], 16)
            pool.wait_ge(hid_lo, 3 * HALVES * KF)
            pool.dma_start(s5_bm[:, 0:early, :, :], dram_bm[:, 0:early, :, :]).then_inc(bm_loaded[1], 16)
            first = next(s0 for k, _, _, s0 in phases if k == "mixer1")
            pool.wait_ge(slab_lo, split(first - 1))
            pool.dma_start(sines[:].rearrange("p w a c -> p w (a c)"), dram_sines).then_inc(sines_loaded, 16)
            pool.wait_ge(rinv_ready, NORM_S5 + 1)
            for q in (2, 3):
                scale_u(pool, q)
            b, v = (turned[:, i].rearrange("p w (n c) -> p w n c", c=NC) for i in range(2))
            last = slice(0, NC - 1)
            pool.wait_ge(x_zeroed, 1)
            for q in range(QUARTERS):
                ps = slice(q * PQ, (q + 1) * PQ)
                pool.wait_ge(rotated, 2 * (q + 1))
                tt(s5_x[:, 0, ps, 1:], b[:, 0, :, last], v[:, 1, :, last], ALU.subtract).then_inc(scanned, 1)
                tt(s5_x[:, 1, ps, 1:], v[:, 0, :, last], b[:, 1, :, last], ALU.add).then_inc(scanned, 1)


def layouts(inputs):
    a = {k: np.asarray(v) for k, v in inputs.items()}
    d = a["x"].shape[2]
    groups, states, gc = a["s5_b_re"].shape[1:]
    pairs, kd = groups // 2, d // P

    def features(v):
        return v.reshape(-1, P).T

    per = pairs // kd

    def by_state(v):
        return v[0].reshape(kd, 2, per, states).transpose(1, 3, 0, 2).reshape(2 * states, pairs)

    def b_by_state(v):
        return v[0].reshape(kd, 2, per, states, gc).transpose(1, 3, 0, 2, 4).reshape(2 * states, pairs, gc)

    def b_by_channel(v):
        return v[0].reshape(kd, 2, per, states, gc).transpose(4, 0, 2, 1, 3).reshape(gc, groups * states)

    def c_by_state(v):
        return v[0].reshape(kd, 2, per, gc, states).transpose(1, 4, 0, 2, 3).reshape(2 * states, pairs, gc)

    return [
        ("x_t", a["x"][0].T), ("norm_g", a["norm_g"].reshape(-1, kd, P).transpose(2, 0, 1)),
        ("ffn_w_in", a["ffn_w_in"]), ("ffn_w_out", a["ffn_w_out"]),
        ("mix_w_in", a["mix_w_in"][0]), ("attn_sinks", a["attn_sinks"]), ("hgrn_lb", features(a["hgrn_lb"])),
        ("mix_w_out", a["mix_w_out"][0]),
        ("s5_a_re", by_state(a["s5_a_re"])), ("s5_a_im", by_state(a["s5_a_im"])),
        ("s5_log_step", a["s5_log_step"].reshape(kd, 2, per).transpose(1, 0, 2).reshape(2, pairs)),
        ("s5_b_re", b_by_state(a["s5_b_re"])), ("s5_b_im", b_by_state(a["s5_b_im"])),
        ("s5_bt_re", b_by_channel(a["s5_b_re"])), ("s5_bt_im", b_by_channel(a["s5_b_im"])),
        ("s5_c_re", c_by_state(a["s5_c_re"])), ("s5_c_im", c_by_state(a["s5_c_im"])),
        ("s5_d", a["s5_d"].reshape(kd, 2, per, gc).transpose(2, 1, 3, 0).reshape(P, kd)), ("s5_w_glu", a["s5_w_glu"][0]), ("final_g", features(a["final_g"])),
    ]


def kernel(**inputs):
    import concourse.bacc as bacc
    from concourse.bass_utils import run_bass_kernel_spmd

    nc = bacc.Bacc("TRN2", target_bir_lowering=False, num_devices=1)
    arrays, args = {}, []
    for name, v in layouts(inputs):
        v = np.ascontiguousarray(v)
        arrays[name] = v
        args.append(nc.dram_tensor(name, v.shape, mybir.dt.from_np(v.dtype), kind="ExternalInput").ap())
    tokens, d = np.asarray(inputs["x"]).shape[1:]
    args.append(nc.dram_tensor("out_t", (d, tokens), F32, kind="ExternalOutput").ap())
    trunk(nc, *args)
    r = run_bass_kernel_spmd(nc, [arrays], core_ids=[0])
    return np.ascontiguousarray(r.results[0]["out_t"].T)[None]
```
